# Optimizing a Trainium2 kernel written in Bass

```python
import jax, jax.numpy as jnp
from jax import lax
import numpy as np

D_MODEL = 1024
BATCH = 1
SEQ = 512
DEPTH = 1

RMS_EPS = 1e-6
HG_HEADS = 4
HG_DK = 128
HG_DV = 128
HG_WIDTH = 512
HG_CHUNK = 64
RW_HEADS = 8
RW_HEAD = 64
RW_WIDTH = 512
RW_DECAY_LORA = 64
RW_AAA_LORA = 64
RW_GATE_LORA = 128
RW_GN_EPS = 64e-5
RW_COLS = 1792
IN_WIDTHS = (512, 512, 512, 512, 1792, 1024, 1024)
IN_COLS = 5888
PK_HEADS = 8
PK_DIM = 128
PK_HALF = 64
N_KEYS = 128
N_EXPERTS = 16384
PK_TOPK = 16
PEER_BLOCK = 128
PLE_DIM = 256

kernel_name = "hgrn2_rwkv7_peer_hybrid_block"

def rms_norm(x, w):
    xf = x.astype(jnp.float32)
    y = xf * lax.rsqrt(jnp.mean(xf * xf, axis=-1, keepdims=True) + RMS_EPS)
    return (y * w.astype(jnp.float32)).astype(x.dtype)

def split_cols(cols, widths):
    out, start = [], 0
    for wd in widths:
        out.append(cols[..., start:start + wd])
        start += wd
    return out

def hgrn2_mixer(q, f_logit, i_val, g_out, lb, norm_w):
    B, S, _ = q.shape
    nc = S // HG_CHUNK
    f32 = jnp.float32
    q = jax.nn.silu(q.astype(f32)) * (HG_DK ** -0.5)
    f = lb + (1.0 - lb) * jax.nn.sigmoid(f_logit.astype(f32))
    log_f = jnp.log(f)
    k = 1.0 - f
    v = i_val.astype(f32)

    def to_chunks(t, d):
        return t.reshape(B, nc, HG_CHUNK, HG_HEADS, d).transpose(1, 0, 3, 2, 4)

    qc = to_chunks(q, HG_DK)
    kc = to_chunks(k, HG_DK)
    gc = to_chunks(log_f, HG_DK)
    vc = to_chunks(v, HG_DV)
    causal = jnp.tril(jnp.ones((HG_CHUNK, HG_CHUNK), dtype=bool))[:, :, None]

    def step(state, inp):
        q_c, k_c, v_c, g_c = inp
        b = jnp.cumsum(g_c, axis=2)
        o_inter = jnp.einsum('bhtk,bhkv->bhtv', q_c * jnp.exp(b), state)
        diff = b[:, :, :, None, :] - b[:, :, None, :, :]
        dec = jnp.where(causal, jnp.exp(jnp.where(causal, diff, 0.0)), 0.0)
        att = jnp.einsum('bhtk,bhsk,bhtsk->bhts', q_c, k_c, dec)
        o_intra = jnp.einsum('bhts,bhsv->bhtv', att, v_c)
        b_last = b[:, :, -1:, :]
        new_state = jnp.exp(b_last[:, :, 0, :])[..., None] * state + jnp.einsum('bhsk,bhsv->bhkv', k_c * jnp.exp(b_last - b), v_c)
        return new_state, o_inter + o_intra

    s0 = jnp.zeros((B, HG_HEADS, HG_DK, HG_DV), f32)
    _, o = lax.scan(step, s0, (qc, kc, vc, gc))
    o = o.transpose(1, 0, 3, 2, 4).reshape(B, S, HG_HEADS, HG_DV)
    o = o * lax.rsqrt(jnp.mean(o * o, axis=-1, keepdims=True) + RMS_EPS)
    o = o.reshape(B, S, HG_WIDTH) * norm_w.astype(f32) * jax.nn.silu(g_out.astype(f32))
    return o.astype(g_out.dtype)

def rwkv7_mixer(rw, mu, w0, w2, a0, a2, g2, k_k, k_a, r_k, ln_w, ln_b):
    B, S, _ = rw.shape
    f32 = jnp.float32
    prev = jnp.pad(rw, ((0, 0), (1, 0), (0, 0)))[:, :S]
    rw = rw + (prev - rw) * mu
    r, k, v, wd, ad, gd = split_cols(rw, (RW_WIDTH, RW_WIDTH, RW_WIDTH, RW_DECAY_LORA, RW_AAA_LORA, RW_GATE_LORA))
    w_log = -jax.nn.softplus(-(w0 + jnp.tanh(wd) @ w2).astype(f32)) - 0.5
    decay = jnp.exp(-jnp.exp(w_log))
    a = jax.nn.sigmoid((a0 + ad @ a2).astype(f32))
    g = (jax.nn.sigmoid(gd) @ g2).astype(f32)

    def heads(t):
        return t.astype(f32).reshape(B, S, RW_HEADS, RW_HEAD)

    r = heads(r)
    k = heads(k)
    v = heads(v)
    decay = heads(decay)
    a = heads(a)
    kk = k * k_k.astype(f32).reshape(RW_HEADS, RW_HEAD)
    kk = kk / jnp.maximum(jnp.sqrt(jnp.sum(kk * kk, axis=-1, keepdims=True)), 1e-12)
    k = k * (1.0 + (a - 1.0) * k_a.astype(f32).reshape(RW_HEADS, RW_HEAD))

    def step(state, inp):
        r_t, w_t, k_t, v_t, kk_t, a_t = inp
        sa = jnp.einsum('bhvk,bhk->bhv', state, kk_t)
        state = state * w_t[:, :, None, :] - sa[..., None] * (kk_t * a_t)[:, :, None, :] + v_t[..., None] * k_t[:, :, None, :]
        return state, jnp.einsum('bhvk,bhk->bhv', state, r_t)

    xs = (jnp.moveaxis(r, 1, 0), jnp.moveaxis(decay, 1, 0), jnp.moveaxis(k, 1, 0), jnp.moveaxis(v, 1, 0), jnp.moveaxis(kk, 1, 0), jnp.moveaxis(a, 1, 0))
    s0 = jnp.zeros((B, RW_HEADS, RW_HEAD, RW_HEAD), f32)
    _, y = lax.scan(step, s0, xs)
    y = jnp.moveaxis(y, 0, 1)
    mean = jnp.mean(y, axis=-1, keepdims=True)
    var = jnp.mean(jnp.square(y - mean), axis=-1, keepdims=True)
    y = ((y - mean) * lax.rsqrt(var + RW_GN_EPS)).reshape(B, S, RW_WIDTH) * ln_w.astype(f32) + ln_b.astype(f32)
    bonus = jnp.sum(r * k * r_k.astype(f32).reshape(RW_HEADS, RW_HEAD), axis=-1, keepdims=True) * v
    y = (y + bonus.reshape(B, S, RW_WIDTH)) * g
    return y.astype(rw.dtype)

def peer_ffn(h, wq, sub_keys, u_emb, v_emb):
    B, S, D = h.shape
    f32 = jnp.float32
    h_blocks = h.reshape(B * S // PEER_BLOCK, PEER_BLOCK, D)

    def block(hb):
        tb = hb.shape[0]
        q = (hb @ wq).reshape(tb, PK_HEADS, 2, PK_HALF)
        sc = jnp.einsum('thcd,cnd->thcn', q, sub_keys).astype(f32)
        s_top, i_top = lax.top_k(sc, PK_TOPK)
        cand = s_top[:, :, 0, :, None] + s_top[:, :, 1, None, :]
        c_s, c_i = lax.top_k(cand.reshape(tb, PK_HEADS, PK_TOPK * PK_TOPK), PK_TOPK)
        idx1 = jnp.take_along_axis(i_top[:, :, 0], c_i // PK_TOPK, axis=-1)
        idx2 = jnp.take_along_axis(i_top[:, :, 1], c_i % PK_TOPK, axis=-1)
        idx = idx1 * N_KEYS + idx2
        gate = jax.nn.softmax(c_s, axis=-1)
        u = jnp.take(u_emb, idx, axis=0)
        act = jax.nn.gelu(jnp.einsum('td,thkd->thk', hb, u).astype(f32), approximate=False)
        v_sel = jnp.take(v_emb, idx, axis=0)
        return jnp.einsum('thk,thkd->td', (gate * act).astype(hb.dtype), v_sel)

    return lax.map(block, h_blocks).reshape(B, S, D)

def setup_inputs(seed: int = 0) -> dict:
    key = jax.random.key(seed)
    ks = jax.random.split(key, 32)
    f32 = jnp.float32

    def nrm(k, shape, scale):
        return jax.random.normal(k, shape, f32) * scale

    def gain(k, shape):
        return 1.0 + 0.02 * jax.random.normal(k, shape, f32)

    return {
        "x": nrm(ks[0], (BATCH, SEQ, D_MODEL), 1.0),
        "p": nrm(ks[1], (DEPTH, BATCH, SEQ, PLE_DIM), 1.0),
        "norm_mix_w": gain(ks[2], (DEPTH, D_MODEL)),
        "w_in": nrm(ks[3], (DEPTH, D_MODEL, IN_COLS), D_MODEL ** -0.5),
        "hg_lb": nrm(ks[4], (DEPTH + 1, HG_WIDTH), 0.1),
        "hg_norm_w": gain(ks[5], (DEPTH, HG_WIDTH)),
        "rw_mu": jax.random.uniform(ks[6], (DEPTH, RW_COLS), f32),
        "rw_w0": jax.random.uniform(ks[7], (DEPTH, RW_WIDTH), f32, minval=-5.5, maxval=-0.5),
        "rw_w2": nrm(ks[8], (DEPTH, RW_DECAY_LORA, RW_WIDTH), 0.1),
        "rw_a0": nrm(ks[9], (DEPTH, RW_WIDTH), 0.1),
        "rw_a2": nrm(ks[10], (DEPTH, RW_AAA_LORA, RW_WIDTH), 0.1),
        "rw_g2": nrm(ks[11], (DEPTH, RW_GATE_LORA, RW_WIDTH), RW_GATE_LORA ** -0.5),
        "rw_k_k": 0.85 + nrm(ks[12], (DEPTH, RW_WIDTH), 0.02),
        "rw_k_a": gain(ks[13], (DEPTH, RW_WIDTH)),
        "rw_r_k": nrm(ks[14], (DEPTH, RW_WIDTH), 0.1),
        "rw_ln_w": gain(ks[15], (DEPTH, RW_WIDTH)),
        "rw_ln_b": nrm(ks[16], (DEPTH, RW_WIDTH), 0.02),
        "w_branch_hg": nrm(ks[17], (DEPTH, HG_WIDTH, D_MODEL), HG_WIDTH ** -0.5),
        "w_branch_rw": nrm(ks[18], (DEPTH, RW_WIDTH, D_MODEL), RW_WIDTH ** -0.5),
        "w_out": nrm(ks[19], (DEPTH, D_MODEL, D_MODEL), D_MODEL ** -0.5),
        "norm_ffn_w": gain(ks[20], (DEPTH, D_MODEL)),
        "peer_wq": nrm(ks[21], (DEPTH, D_MODEL, PK_HEADS * PK_DIM), D_MODEL ** -0.5),
        "peer_keys": nrm(ks[22], (DEPTH, 2, N_KEYS, PK_HALF), PK_HALF ** -0.5),
        "peer_u": nrm(ks[23], (DEPTH, N_EXPERTS, D_MODEL), D_MODEL ** -0.5),
        "peer_v": nrm(ks[24], (DEPTH, N_EXPERTS, D_MODEL), PK_HEADS ** -0.5),
        "norm_ple_w": gain(ks[25], (DEPTH, D_MODEL)),
        "ple_proj": nrm(ks[26], (DEPTH, PLE_DIM, D_MODEL), PLE_DIM ** -0.5),
        "ple_gate": nrm(ks[27], (DEPTH, D_MODEL, D_MODEL), D_MODEL ** -0.5),
        "final_norm_w": gain(ks[28], (D_MODEL,)),
    }

def reference(x, p, norm_mix_w, w_in, hg_lb, hg_norm_w, rw_mu, rw_w0, rw_w2, rw_a0, rw_a2, rw_g2, rw_k_k, rw_k_a, rw_r_k, rw_ln_w, rw_ln_b, w_branch_hg, w_branch_rw, w_out, norm_ffn_w, peer_wq, peer_keys, peer_u, peer_v, norm_ple_w, ple_proj, ple_gate, final_norm_w):
    lower_bounds = jnp.cumsum(jax.nn.softmax(hg_lb.astype(jnp.float32), axis=0), axis=0)
    for i in range(DEPTH):
        h = rms_norm(x, norm_mix_w[i])
        cols = h @ w_in[i]
        hq, hf, hi, hgo, rw_cols, gate_hg, gate_rw = split_cols(cols, IN_WIDTHS)
        y_hg = hgrn2_mixer(hq, hf, hi, hgo, lower_bounds[i], hg_norm_w[i])
        y_rw = rwkv7_mixer(rw_cols, rw_mu[i], rw_w0[i], rw_w2[i], rw_a0[i], rw_a2[i], rw_g2[i], rw_k_k[i], rw_k_a[i], rw_r_k[i], rw_ln_w[i], rw_ln_b[i])
        merged = jax.nn.sigmoid(gate_hg) * (y_hg @ w_branch_hg[i]) + jax.nn.sigmoid(gate_rw) * (y_rw @ w_branch_rw[i])
        x = x + merged @ w_out[i]
        x = x + peer_ffn(rms_norm(x, norm_ffn_w[i]), peer_wq[i], peer_keys[i], peer_u[i], peer_v[i])
        ple_g = jax.nn.sigmoid(rms_norm(x, norm_ple_w[i]) @ ple_gate[i])
        x = x + ple_g * (p[i] @ ple_proj[i])
    return rms_norm(x, final_norm_w)


_drawn_inputs = setup_inputs


def setup_inputs(seed=0):
    import zlib

    import numpy as np

    out = dict(_drawn_inputs(seed))
    spreads = {}
    factors = {'hg_lb': 5.641,
     'hg_norm_w': 43.839,
     'rw_w2': 2.951,
     'rw_a0': 2.946,
     'rw_k_k': 126.347,
     'rw_k_a': 4.35,
     'rw_ln_w': 50.81,
     'rw_ln_b': 54.07,
     'norm_ple_w': 200.0,
     'final_norm_w': 20.478,
     'norm_ffn_w': 16.422}
    for name, (base, spread) in spreads.items():
        noise = np.random.default_rng([zlib.crc32(name.encode()), seed]).standard_normal(out[name].shape)
        drawn = base * np.exp(spread * noise) if base else spread * noise
        out[name] = __import__('jax').numpy.asarray(drawn.astype(out[name].dtype))
    for name, factor in factors.items():
        out[name] = (out[name] * factor).astype(out[name].dtype)
    return out
```

```python
from contextlib import ExitStack

import concourse.bass as bass
from concourse import mybir

F32 = mybir.dt.float32
I32 = mybir.dt.int32
U32 = mybir.dt.uint32
ALU = mybir.AluOpType
ACT = mybir.ActivationFunctionType
AX = mybir.AxisListType

P = 128
SEQ = 512
D = 1024
KD = D // P
NB = SEQ // P
EPS = 1e-6
GN_EPS = 64e-5
HG_HEADS = 4
RW_HEADS = 8
PAIRS = RW_HEADS // 2
RH = 64
LEVELS = [64, 32, 16, 8, 4, 2, 1]
STRIP = 256
RING = 3
PK_HEADS = 8
N_KEYS = 128
TOPK = 16
PLE = 256
CAND = [TOPK // (i + 1) for i in range(TOPK)]
N_CAND = sum(CAND)
EXP_HALF = 0.6065306597126334
LOWEST = -3.0e38
N_CONSTANTS = 9 + 6 * len(LEVELS)
SLOT = 512

COLS = {}
_at = 0
for _name, _n in [("norm_mix", 8), ("mu", 14), ("w0", 4), ("a0", 4), ("k_k", 4), ("k_a", 4), ("r_k", 4),
                  ("ln_w", 4), ("ln_b", 4), ("lb0", 4), ("lb1", 4), ("hg_norm", 4), ("norm_ple", 8)]:
    COLS[_name] = (_at, _n)
    _at += _n
N_COLS = _at

RW_STRIPS = [14, 10, 11, 8, 9, 12, 13]
FEATURE_STRIPS = RW_STRIPS + [0, 1, 2, 3, 6, 7]
TOKEN_STRIPS = [4, 5]
GATE_STRIPS = list(range(15, 23))


class Link:

    def __init__(self, eng, sem):
        self.eng, self.sem, self.n = eng, sem, 0

    def __call__(self, ins):
        ins.then_inc(self.sem, 1)
        self.n += 1
        self.eng.wait_ge(self.sem, self.n)

    def restart(self):
        self.eng.sem_clear(self.sem)
        self.n = 0


class Core:

    def __init__(self, nc, ctx):
        self.nc, self.ctx = nc, ctx
        self.const = ctx.enter_context(nc.sbuf_tensor("const", [P, 3072], F32))
        self.arena = ctx.enter_context(nc.sbuf_tensor("arena", [P, 97 * SLOT], F32))
        self.bank = [ctx.enter_context(nc.psum_tensor(f"bank{i}", [P, 512], F32)) for i in range(8)]
        at = 0

        def const(n):
            nonlocal at
            at += n
            return self.const[:, at - n:at]

        self.ident = const(P)
        self.ones_pair = const(P)
        self.ones_full = const(P)
        self.mask_t = const(len(LEVELS) * P).rearrange("p (l t) -> p l t", t=P)
        self.mask_n = const(len(LEVELS) * P).rearrange("p (l t) -> p l t", t=P)
        self.causal = const(2 * P).rearrange("p (a t) -> p a t", a=2)
        self.masks = self.const[:, 0:at]
        self.cols = const(N_COLS)
        self.lb = const(4)
        self.one_minus_lb = const(4)
        self.one_minus_ka = const(4)
        self.iota_cand = const(N_CAND)
        self.stats = const(64)
        self.zero_col = const(1)

    def sem(self, name):
        return self.ctx.enter_context(self.nc.semaphore(name))

    def col(self, name, i):
        at, _ = COLS[name]
        return self.cols[:, at + i:at + i + 1]

    def slots(self, at, n, inner=SLOT):
        return self.arena[:, at * SLOT:(at + n) * SLOT].rearrange("p (a b) -> p a b", b=inner)


def mixer_inputs(core):
    return {
        "h_t": core.slots(0, 8), "r": core.slots(8, 4), "k": core.slots(12, 4), "v": core.slots(16, 4),
        "ld": core.slots(20, 4), "hq": core.slots(24, 4), "hgo": core.slots(28, 4), "sgd": core.slots(32, 1)[:, 0, :],
        "kk": core.slots(33, 4), "nb": core.slots(37, 4), "cum": core.slots(41, 4), "hk": core.slots(45, 4),
        "hcum": core.slots(49, 4), "vh": core.slots(53, 4),
    }


def make_constants(core, gp, made):
    n = 0

    def did(ins):
        nonlocal n
        n += 1
        ins.then_inc(made, 1)
        gp.wait_ge(made, n)

    did(gp.memset(core.masks, 0.0))
    did(gp.affine_select(out=core.ident, in_=core.ident, pattern=[[-1, P]], compare_op=ALU.not_equal, fill=1.0,
                         base=0, channel_multiplier=1))
    did(gp.memset(core.ones_pair[0:RH, 0:RH], 1.0))
    did(gp.memset(core.ones_pair[RH:P, RH:P], 1.0))
    did(gp.memset(core.ones_full, 1.0))
    did(gp.memset(core.causal, 1.0))
    did(gp.affine_select(out=core.causal[:, 0, :], in_=core.causal[:, 0, :], pattern=[[1, P]], compare_op=ALU.is_gt,
                         fill=0.0, base=0, channel_multiplier=-1))
    did(gp.affine_select(out=core.causal[:, 1, :], in_=core.causal[:, 1, :], pattern=[[1, P]], compare_op=ALU.is_ge,
                         fill=0.0, base=0, channel_multiplier=-1))
    for level, n_ in enumerate(LEVELS):
        blocks = P // (2 * n_)
        for mask, half, lo in ((core.mask_t, 1, 0), (core.mask_n, 0, n_)):
            view = mask[:, level, :].rearrange("p (b two n) -> p b two n", two=2, n=n_)[:, :, half, :]
            did(gp.memset(view, 1.0))
            did(gp.affine_select(out=view, in_=view, pattern=[[-2 * n_, blocks], [0, n_]], compare_op=ALU.is_ge,
                                 fill=0.0, base=-lo, channel_multiplier=1))
            did(gp.affine_select(out=view, in_=view, pattern=[[2 * n_, blocks], [0, n_]], compare_op=ALU.is_ge,
                                 fill=0.0, base=lo + n_ - 1, channel_multiplier=-1))
    did(gp.iota(core.iota_cand, pattern=[[1, N_CAND]], base=0, channel_multiplier=0,
                allow_small_or_imprecise_dtypes=True))
    assert n == N_CONSTANTS


def project(core, x, w_in_strips, params, w2, a2, g2):
    nc = core.nc
    m = mixer_inputs(core)
    bank = core.bank
    ring = [core.slots(57 + 4 * i, 4, STRIP) for i in range(RING)]
    xs = core.slots(8, 8, D)
    x_in = core.slots(16, 8, D)
    raw = [core.arena[:, (69 * SLOT + i * 520):(69 * SLOT + i * 520 + 513)] for i in range(2)]
    diff = core.slots(72, 2)
    low = core.slots(74, 1)[:, 0, :]
    gd = core.slots(75, 1)[:, 0, :]
    w2a2 = core.slots(76, 1)[:, 0, :]
    chunk_ones = core.slots(78, 1)[:, 0, :]
    sig = core.slots(79, 2)
    sq = core.slots(81, 4)
    ln_f = core.slots(85, 4)
    ka = core.slots(89, 2)
    junk = core.slots(91, 2, D)[:, 0, :]
    ssq, mean, root, rstd = (core.stats[:, 4 * i:4 * i + 4] for i in range(4))
    lb_t = core.stats[:, 16:32].rearrange("p (a b) -> p a b", b=4)

    loaded_x = core.sem("x_loaded")
    loaded_p = core.sem("params_loaded")
    strip_loaded = [core.sem(f"strip_loaded{i}") for i in range(RING)]
    constants = core.sem("constants_made")
    squares = core.sem("squares_summed")
    rooted = core.sem("mean_squares_rooted")
    ms_ready = core.sem("mean_squares_ready")
    scaled = core.sem("x_scaled")
    turned = core.sem("x_turned")
    h_ready = core.sem("h_ready")
    cols_ready = core.sem("columns_ready")
    cols_taken = core.sem("columns_taken")
    mixed = core.sem("shifts_mixed")
    low_ready = core.sem("low_rank_ready")
    lora_done = core.sem("lora_done")
    lora_taken = core.sem("lora_taken")
    sig_used = core.sem("lora_sigmoid_used")
    kk_raw = core.sem("kk_raw_ready")
    kk_sq = core.sem("kk_squared")
    norm_done = core.sem("kk_norm_summed")
    norm_rooted = core.sem("kk_norm_rooted")
    hg_taken = core.sem("hgrn_tiles_taken")
    hg_used = core.sem("hgrn_tiles_used")
    f_ready = core.sem("f_ready")
    ln_ready = core.sem("log_f_ready")
    lb_diff = core.sem("lb_differences")
    lb_exp = core.sem("lb_exponentials")
    v_link = core.sem("project_vector_link")
    a_link = core.sem("project_scalar_link")

    n_rw = 2 * len(RW_STRIPS)
    n_feature = 2 * len(FEATURE_STRIPS)
    rw_tiles = [(low, 12), (gd, 13)]
    for name, first in (("k", 4), ("r", 0), ("v", 8)):
        rw_tiles += [(m[name][:, j, :], first + j) for j in range(4)]

    with nc.Block() as block:
        @block.sync
        def _(sp):
            for b in range(NB):
                sp.dma_start(x_in[:, b, :], x[b * P:(b + 1) * P, :]).then_inc(loaded_x, 16)
            for n, strip in enumerate(FEATURE_STRIPS + TOKEN_STRIPS):
                if n >= RING:
                    sp.wait_ge(cols_ready, 2 * (n - RING) + 2)
                sp.dma_start(ring[n % RING], w_in_strips[strip]).then_inc(strip_loaded[n % RING], 16)

        @block.gpsimd
        def _(gp):
            gp.dma_start(core.cols, params).then_inc(loaded_p, 16)
            gp.dma_start(w2a2[0:RH, :], w2).then_inc(loaded_p, 16)
            gp.dma_start(w2a2[RH:P, :], a2).then_inc(loaded_p, 16)
            make_constants(core, gp, constants)

        @block.tensor
        def _(pe):
            pe.wait_ge(constants, N_CONSTANTS)
            for dk in range(KD):
                for b in range(NB):
                    pe.wait_ge(scaled, b + 1)
                    if dk >= 2 and b == 0:
                        pe.wait_ge(h_ready, dk - 1)
                    ins = pe.transpose(bank[6 + dk % 2][:, b * P:(b + 1) * P], xs[:, b, dk * P:(dk + 1) * P], core.ident)
                ins.then_inc(turned, 1)
            pe.wait_ge(h_ready, KD)

            def strips(i, count):
                for s in range(count):
                    pe.wait_ge(strip_loaded[s], 16 * (i + 1))
                    for half in range(2):
                        tile = 2 * s + half
                        if not (isinstance(i, int) and i == 0):
                            pe.wait_ge(cols_taken, 6 * i + tile - 5)
                        for k in range(KD):
                            ins = pe.matmul(bank[tile][:], ring[s][:, k, half * P:(half + 1) * P], m["h_t"][:, k, :],
                                            start=(k == 0), stop=(k == KD - 1))
                        ins.then_inc(cols_ready, 1)

            strips(0, RING)
            pe.wait_ge(low_ready, 1)
            pe.wait_ge(mixed, 1)
            for j in range(PAIRS):
                for half in range(2):
                    if j:
                        pe.wait_ge(lora_taken, 2 * (j - 1) + half + 1)
                    rows = slice(RH * half, RH * (half + 1))
                    pe.matmul(bank[6 + half][:], w2a2[rows, j * P:(j + 1) * P], low[rows, :], start=True,
                              stop=True).then_inc(lora_done, 1)
            with pe.Fori(1, len(FEATURE_STRIPS) // RING) as i:
                strips(i, RING)
            pe.wait_ge(lora_taken, 2 * PAIRS)
            for j in range(PAIRS):
                pe.wait_ge(kk_sq, j + 1)
                if j >= 2:
                    pe.wait_ge(norm_rooted, j - 1)
                pe.matmul(bank[6 + j % 2][:], core.ones_pair, sq[:, j, :], start=True, stop=True).then_inc(norm_done, 1)
            strips(len(FEATURE_STRIPS) // RING, 1)
            t = n_feature
            for n in range(len(FEATURE_STRIPS), len(FEATURE_STRIPS) + len(TOKEN_STRIPS)):
                pe.wait_ge(strip_loaded[n % RING], 16 * (n // RING + 1))
                for b in range(NB):
                    pe.wait_ge(cols_taken, t - 5)
                    for k in range(KD):
                        ins = pe.matmul(bank[t % 6][:, 0:STRIP], m["h_t"][:, k, b * P:(b + 1) * P], ring[n % RING][:, k, :],
                                        start=(k == 0), stop=(k == KD - 1))
                    ins.then_inc(cols_ready, 1)
                    t += 1

        @block.scalar
        def _(act):
            for b in range(NB):
                act.wait_ge(loaded_x, 16 * NB)
                act.activation(junk, x_in[:, b, :], ACT.Square, accum_out=ssq[:, b:b + 1]).then_inc(squares, 1)
                act.wait_ge(squares, b + 1)
            act.wait_ge(ms_ready, 1)
            act.activation(root, mean, ACT.Sqrt).then_inc(rooted, 1)
            act.wait_ge(lb_diff, 1)
            act.activation(lb_t[:, 2, :], lb_t[:, 0, :], ACT.Exp)
            act.activation(lb_t[:, 3, :], lb_t[:, 1, :], ACT.Exp).then_inc(lb_exp, 1)
            act.wait_ge(loaded_p, 48)
            for dk in range(KD):
                act.wait_ge(turned, dk + 1)
                act.activation(m["h_t"][:, dk, :], bank[6 + dk % 2][:], ACT.Copy,
                               scale=core.col("norm_mix", dk)).then_inc(h_ready, 1)

            def take_rw(t):
                act.wait_ge(cols_ready, t + 1)
                if t >= 2:
                    act.wait_ge(mixed, t - 1)
                act.activation(raw[t % 2][:, 1:SEQ + 1], bank[t % 6][:], ACT.Copy).then_inc(cols_taken, 1)

            def square_kk(j):
                act.wait_ge(kk_raw, j + 1)
                act.activation(sq[:, j, :], m["kk"][:, j, :], ACT.Square).then_inc(kk_sq, 1)

            take_rw(0)
            take_rw(1)
            act.wait_ge(mixed, 1)
            act.activation(low[0:RH, :], low[0:RH, :], ACT.Tanh).then_inc(low_ready, 1)
            act.wait_ge(mixed, 2)
            act.activation(m["sgd"], gd, ACT.Sigmoid)
            for t in range(2, 6):
                take_rw(t)
            for j in range(PAIRS):
                act.wait_ge(lora_done, 2 * j + 1)
                if j >= 2:
                    act.wait_ge(sig_used, j - 1)
                act.activation(sig[:, j % 2, :], bank[6][:], ACT.Sigmoid, bias=core.col("w0", j)).then_inc(lora_taken, 1)
                act.wait_ge(lora_done, 2 * j + 2)
                act.activation(m["nb"][:, j, :], bank[7][:], ACT.Sigmoid, bias=core.col("a0", j)).then_inc(lora_taken, 1)
            for t in range(6, n_rw):
                take_rw(t)
                if t < 6 + PAIRS:
                    square_kk(t - 6)
            for j in range(12):
                t = n_rw + j
                if j == 10:
                    for i in range(PAIRS):
                        act.wait_ge(norm_done, i + 1)
                        act.activation(sq[:, i, :], bank[6 + i % 2][:], ACT.Sqrt).then_inc(norm_rooted, 1)
                act.wait_ge(cols_ready, t + 1)
                if j >= 2:
                    act.wait_ge(hg_used, j - 1)
                else:
                    act.wait_ge(sig_used, PAIRS)
                ins = act.activation(sig[:, j % 2, :], bank[t % 6][:], ACT.Sigmoid)
                if not 4 <= j < 8:
                    dest = m["hq"][:, j, :] if j < 4 else m["hgo"][:, j - 8, :]
                    ins = act.activation(dest, bank[t % 6][:], ACT.Copy)
                ins.then_inc(cols_taken, 1)
            for t in range(n_feature, n_feature + 2 * NB):
                act.wait_ge(cols_ready, t + 1)
                s, b = divmod(t - n_feature, NB)
                act.activation(m["vh"][:, b, s * STRIP:(s + 1) * STRIP], bank[t % 6][:, 0:STRIP],
                               ACT.Copy).then_inc(cols_taken, 1)
            act.wait_ge(f_ready, 4)
            act.activation(ln_f, m["hcum"], ACT.Ln).then_inc(ln_ready, 1)

        @block.vector
        def _(v):
            link = Link(v, v_link)
            for i in range(2):
                v.memset(raw[i][:, 0:1], 0.0)
            link(v.memset(chunk_ones, 1.0))
            link(v.memset(chunk_ones.rearrange("p (c t) -> p c t", t=P)[:, :, 0:1], 0.0))
            v.wait_ge(squares, NB)
            v.tensor_scalar(mean, ssq, 1.0 / D, EPS, ALU.mult, ALU.add).then_inc(ms_ready, 1)
            v.wait_ge(rooted, 1)
            link(v.reciprocal(rstd, root))
            for b in range(NB):
                v.tensor_scalar(xs[:, b, :], x_in[:, b, :], rstd[:, b:b + 1], None, ALU.mult).then_inc(scaled, 1)
            v.wait_ge(constants, N_CONSTANTS)
            v.wait_ge(loaded_p, 48)
            lb0 = core.cols[:, COLS["lb0"][0]:COLS["lb0"][0] + 4]
            lb1 = core.cols[:, COLS["lb1"][0]:COLS["lb1"][0] + 4]
            top = core.stats[:, 32:36]
            link(v.tensor_tensor(top, lb0, lb1, ALU.max))
            v.tensor_tensor(lb_t[:, 0, :], lb0, top, ALU.subtract)
            v.tensor_tensor(lb_t[:, 1, :], lb1, top, ALU.subtract).then_inc(lb_diff, 1)
            v.wait_ge(lb_exp, 1)
            link(v.tensor_tensor(top, lb_t[:, 2, :], lb_t[:, 3, :], ALU.add))
            link(v.reciprocal(lb_t[:, 0, :], top))
            link(v.tensor_tensor(core.lb, lb_t[:, 2, :], lb_t[:, 0, :], ALU.mult))
            v.tensor_scalar(core.one_minus_lb, core.lb, -1.0, 1.0, ALU.mult, ALU.add)
            at, n = COLS["k_a"]
            link(v.tensor_scalar(core.one_minus_ka, core.cols[:, at:at + n], -1.0, 1.0, ALU.mult, ALU.add))

            def mix_shift(t):
                dest, c = rw_tiles[t]
                v.wait_ge(cols_taken, t + 1)
                link(v.tensor_tensor(diff[:, 0, :], raw[t % 2][:, 0:SEQ], raw[t % 2][:, 1:SEQ + 1], ALU.subtract))
                v.scalar_tensor_tensor(out=dest, in0=diff[:, 0, :], scalar=core.col("mu", c),
                                       in1=raw[t % 2][:, 1:SEQ + 1], op0=ALU.mult, op1=ALU.add).then_inc(mixed, 1)
                v.wait_ge(mixed, t + 1)

            def raw_kk(j):
                v.tensor_scalar(m["kk"][:, j, :], m["k"][:, j, :], core.col("k_k", j), None,
                                ALU.mult).then_inc(kk_raw, 1)

            for t in range(6):
                mix_shift(t)
                if t >= 2:
                    raw_kk(t - 2)
            for j in range(PAIRS):
                v.wait_ge(lora_taken, 2 * j + 1)
                v.tensor_scalar(m["ld"][:, j, :], sig[:, j % 2, :], -EXP_HALF, None, ALU.mult).then_inc(sig_used, 1)
                v.wait_ge(sig_used, j + 1)
                v.tensor_tensor_scan(m["cum"][:, j, :], chunk_ones, m["ld"][:, j, :], 0.0, ALU.mult, ALU.add)
            for t in range(6, n_rw):
                mix_shift(t)
            for j in range(12):
                v.wait_ge(cols_taken, n_rw + j + 1)
                if j < 4:
                    q = m["hq"][:, j, :]
                    v.scalar_tensor_tensor(out=q, in0=q, scalar=float(P) ** -0.5, in1=sig[:, j % 2, :], op0=ALU.mult,
                                           op1=ALU.mult).then_inc(hg_used, 1)
                elif j < 8:
                    h = j - 4
                    v.tensor_scalar(m["hcum"][:, h, :], sig[:, j % 2, :], core.one_minus_lb[:, h:h + 1],
                                    core.lb[:, h:h + 1], ALU.mult, ALU.add).then_inc(hg_used, 1)
                    v.wait_ge(hg_used, j + 1)
                    v.tensor_scalar(m["hk"][:, h, :], m["hcum"][:, h, :], -1.0, 1.0, ALU.mult,
                                    ALU.add).then_inc(f_ready, 1)
                else:
                    g = m["hgo"][:, j - 8, :]
                    v.scalar_tensor_tensor(out=g, in0=g, scalar=core.col("hg_norm", j - 8), in1=sig[:, j % 2, :],
                                           op0=ALU.mult, op1=ALU.mult).then_inc(hg_used, 1)
            for j in range(PAIRS):
                a, k, kk = m["nb"][:, j, :], m["k"][:, j, :], m["kk"][:, j, :]
                v.wait_ge(lora_taken, 2 * j + 2)
                link(v.tensor_scalar(ka[:, 0, :], a, core.col("k_a", j), core.one_minus_ka[:, j:j + 1], ALU.mult, ALU.add))
                v.tensor_tensor(k, k, ka[:, 0, :], ALU.mult)
                v.wait_ge(norm_rooted, j + 1)
                link(v.tensor_scalar(sq[:, j, :], sq[:, j, :], 1e-12, None, ALU.max))
                link(v.reciprocal(ka[:, 1, :], sq[:, j, :]))
                link(v.tensor_tensor(kk, kk, ka[:, 1, :], ALU.mult))
                link(v.scalar_tensor_tensor(out=a, in0=kk, scalar=-1.0, in1=a, op0=ALU.mult, op1=ALU.mult))
            v.wait_ge(ln_ready, 1)
            for h in range(HG_HEADS):
                ins = v.tensor_tensor_scan(m["hcum"][:, h, :], chunk_ones, ln_f[:, h, :], 0.0, ALU.mult, ALU.add)
            link(ins)


def mix(core):
    nc = core.nc
    m = mixer_inputs(core)
    bank = core.bank

    def tile(at, n=1, inner=P):
        return core.slots(at, n, inner)

    scores = core.slots(57, 8, P).rearrange("p (h a) t -> p h a t", a=4)
    x_t, x_n = tile(65, 2), tile(67, 2)
    y_sb = core.slots(69, 2).rearrange("p b (h t) -> p b h t", t=P)
    level_e = core.slots(71, 2).rearrange("p b (h t) -> p b h t", t=P)
    level_g = core.slots(73, 2).rearrange("p b (h t) -> p b h t", t=P)
    att_t, q_e, k_e, k_tok_h, state_h, v_h = (tile(s) for s in (75, 76, 77, 78, 79, 80))
    e1, e2, e3 = tile(81), tile(82), tile(83)
    kr = core.slots(84, 2, P).rearrange("p (j a) t -> p j a t", a=2)
    k_s, b_s, k_tok, b_tok, v_tok, v_stage = (tile(s) for s in (86, 87, 88, 89, 90, 91))
    state = core.slots(92, 1, RH)[:, 0:PAIRS, :]
    state_0 = core.slots(92, 1, RH)[:, PAIRS:2 * PAIRS, :]
    rhs = core.slots(93, 1, RH)
    u = core.slots(94, 1, RH)
    e_inter, k_stage = tile(95), tile(96)
    exp_mid = core.stats[:, 0:4]

    per = dict(staged=2, rw_diff=1, rw_exp=1, rw_scaled=1, tok_ready=4, tok_taken=4, scores_ready=PAIRS,
               scores_taken=PAIRS, xt_first=2, x_first=2, x_first_taken=2, hg_diff=len(LEVELS), hg_exp=len(LEVELS),
               hg_scaled=len(LEVELS), hg_scores=len(LEVELS) + 1, hg_att=len(LEVELS) + 1, inter_diff=1, inter_exp=1,
               inter_scaled=1, rhs_ready=1, rhs_taken=1, u_ready=1, u_taken=1, out_ready=1, hg_out=2, state_ready=1)
    s = {n: core.sem("mix_" + n) for n in per}
    wait_carrier = core.sem("mix_wait_carrier")
    vector_link = core.sem("mix_vector_link")

    def after(name, c, k):
        return c * per[name] + k

    inv_y = [core.sem(f"mix_inverse_y{i}") for i in range(2)]
    inv_y_taken = [core.sem(f"mix_inverse_y_taken{i}") for i in range(2)]
    inv_z = [core.sem(f"mix_inverse_z{i}") for i in range(2)]
    inv_done = [core.sem(f"mix_inverse_updated{i}") for i in range(2)]
    first_state = core.sem("mix_first_state")
    pe_end = core.sem("mix_tensor_chunk_end")
    act_end = core.sem("mix_scalar_chunk_end")
    dve_end = core.sem("mix_vector_chunk_end")

    n_inv = len(LEVELS) - 1
    inv_level = [len(LEVELS) - 2 - i for i in range(n_inv)]
    head_bank = {"y": (2, 5), "z": (3, 6), "zt": (4, 7)}

    def waited(v):
        v.sem_inc(wait_carrier, 1)

    def halves(ap, level):
        return ap.rearrange("p h (b two n) -> p h b two n", two=2, n=LEVELS[level])

    def heads_of(bank_ap):
        return bank_ap[:].rearrange("p (h t) -> p h t", t=P)

    with nc.Block() as block:
        @block.gpsimd
        def _(gp):
            gp.memset(core.slots(57, 8), 0.0)
            gp.memset(core.slots(92, 1), 0.0)
            gp.memset(state_h, 0.0).then_inc(first_state, 1)

        @block.scalar
        def _(act):
            act.wait_ge(first_state, 1)
            with act.Fori(0, NB) as c:
                act.wait_ge(pe_end, c)
                act.wait_ge(dve_end, c)
                act.wait_ge(act_end, c)
                now = bass.ds(c * P, P)
                act.activation(v_stage, m["v"][:, :, now], ACT.Copy).then_inc(s["staged"], 1)
                act.activation(v_h, m["vh"][:, bass.ds(c, 1), :], ACT.Copy)
                act.activation(k_stage, m["hk"][:, :, now], ACT.Copy).then_inc(s["staged"], 1)

                def level_exp(i):
                    act.wait_ge(s["hg_diff"], after("hg_diff", c, i))
                    act.activation(level_e[:, i % 2], level_e[:, i % 2], ACT.Exp).then_inc(s["hg_exp"], 1)

                act.wait_ge(s["rw_diff"], after("rw_diff", c, 1))
                act.activation(e3, e1, ACT.Exp, scale=-1.0)
                act.activation(e2, e2, ACT.Exp)
                act.activation(exp_mid, m["cum"][:, :, bass.ds(c * P + P // 2 - 1, 1)], ACT.Exp)
                act.activation(e1, e1, ACT.Exp).then_inc(s["rw_exp"], 1)
                act.wait_ge(s["tok_ready"], after("tok_ready", c, 1))
                act.activation(v_tok, heads_of(bank[6]), ACT.Copy).then_inc(s["tok_taken"], 1)
                level_exp(1)
                act.activation(e_inter, m["hcum"][:, :, now], ACT.Exp)
                act.wait_ge(s["inter_diff"], after("inter_diff", c, 1))
                act.activation(k_e, k_e, ACT.Exp).then_inc(s["inter_exp"], 1)
                act.wait_ge(s["tok_ready"], after("tok_ready", c, 2))
                act.activation(k_tok, heads_of(bank[7]), ACT.Copy).then_inc(s["tok_taken"], 1)
                act.wait_ge(s["tok_ready"], after("tok_ready", c, 3))
                act.activation(b_tok, heads_of(bank[6]), ACT.Copy).then_inc(s["tok_taken"], 1)
                level_exp(2)
                act.wait_ge(s["tok_ready"], after("tok_ready", c, 4))
                act.activation(k_tok_h, heads_of(bank[7]), ACT.Copy).then_inc(s["tok_taken"], 1)
                for b in range(2):
                    act.wait_ge(s["x_first"], after("x_first", c, b + 1))
                    act.activation(x_n[:, 4 * b:4 * b + 4, :], heads_of(bank[head_bank["z"][b]]),
                                   ACT.Copy).then_inc(s["x_first_taken"], 1)
                for i in range(n_inv):
                    for b in range(2):
                        act.wait_ge(inv_y[b], c * n_inv + i + 1)
                        act.activation(y_sb[:, b], heads_of(bank[head_bank["y"][b]]),
                                       ACT.Copy).then_inc(inv_y_taken[b], 1)
                    if i + 3 <= len(LEVELS):
                        level_exp(i + 3)
                act.wait_ge(s["rhs_ready"], after("rhs_ready", c, 1))
                for e in range(2):
                    ins = act.activation(rhs[:, 4 * e:4 * e + 4, :],
                                         bank[(2, 5)[e]][:, 0:PAIRS * RH].rearrange("p (j v) -> p j v", v=RH), ACT.Copy)
                ins.then_inc(s["rhs_taken"], 1)
                act.wait_ge(s["u_ready"], after("u_ready", c, 1))
                act.activation(u, bank[3][:].rearrange("p (h v) -> p h v", v=RH), ACT.Copy).then_inc(s["u_taken"], 1)
                act.wait_ge(s["hg_out"], after("hg_out", c, 1))
                act.activation(m["hq"][:, :, now], heads_of(bank[0]), ACT.Copy)
                act.wait_ge(s["out_ready"], after("out_ready", c, 1))
                act.activation(m["ld"][:, :, now], heads_of(bank[4]), ACT.Copy).then_inc(act_end, 1)

        @block.vector
        def _(v):
            link = Link(v, vector_link)
            v.wait_ge(first_state, 1)
            with v.Fori(0, NB) as c:
                v.wait_ge(pe_end, c)
                v.wait_ge(act_end, c)
                v.wait_ge(dve_end, c)
                now = bass.ds(c * P, P)
                hcum = m["hcum"][:, :, now]
                full = [P, PAIRS, P]

                def level_diff(i):
                    b, out = halves(hcum, i - 1), halves(level_e[:, i % 2], i - 1)
                    n = LEVELS[i - 1]
                    edge = b[:, :, :, 0, n - 1:n].to_broadcast([P, HG_HEADS, P // (2 * n), n])
                    v.tensor_tensor(out[:, :, :, 0, :], edge, b[:, :, :, 0, :], ALU.subtract)
                    v.tensor_tensor(out[:, :, :, 1, :], b[:, :, :, 1, :], edge, ALU.subtract).then_inc(s["hg_diff"], 1)

                def level_scale(i):
                    v.wait_ge(s["hg_exp"], after("hg_exp", c, i))
                    e, g = halves(level_e[:, i % 2], i - 1), halves(level_g[:, i % 2], i - 1)
                    k, q = halves(m["hk"][:, :, now], i - 1), halves(m["hq"][:, :, now], i - 1)
                    v.tensor_tensor(g[:, :, :, 0, :], e[:, :, :, 0, :], k[:, :, :, 0, :], ALU.mult)
                    v.tensor_tensor(g[:, :, :, 1, :], e[:, :, :, 1, :], q[:, :, :, 1, :],
                                    ALU.mult).then_inc(s["hg_scaled"], 1)

                def level_keep(i):
                    v.wait_ge(s["hg_att"], after("hg_att", c, i))
                    v.wait_ge(s["hg_scores"], after("hg_scores", c, i + 1))
                    waited(v)
                    mask = core.mask_t[:, i - 1:i, :].bitcast(I32).to_broadcast([P, HG_HEADS, P])
                    v.copy_predicated(att_t, mask, heads_of(bank[i % 2])).then_inc(s["hg_att"], 1)

                mid = m["cum"][:, :, bass.ds(c * P + P // 2 - 1, 1)].to_broadcast(full)
                link(v.tensor_tensor(e1, m["cum"][:, :, now], mid, ALU.subtract))
                v.tensor_tensor(e2, e1, m["ld"][:, :, now], ALU.subtract).then_inc(s["rw_diff"], 1)
                level_diff(1)
                last = m["hcum"][:, :, bass.ds(c * P + P - 1, 1)].to_broadcast(full)
                v.tensor_tensor(k_e, last, hcum, ALU.subtract).then_inc(s["inter_diff"], 1)
                level_diff(2)
                v.wait_ge(s["rw_exp"], after("rw_exp", c, 1))
                v.tensor_tensor(state_0, state, exp_mid.unsqueeze(2).to_broadcast([P, PAIRS, RH]), ALU.mult)
                v.tensor_tensor(kr[:, :, 0, :], m["kk"][:, :, now], e2, ALU.mult)
                v.tensor_tensor(kr[:, :, 1, :], m["r"][:, :, now], e1, ALU.mult)
                v.tensor_tensor(k_s, m["k"][:, :, now], e3, ALU.mult)
                v.tensor_tensor(b_s, m["nb"][:, :, now], e3, ALU.mult).then_inc(s["rw_scaled"], 1)
                level_scale(1)
                v.wait_ge(s["inter_exp"], after("inter_exp", c, 1))
                v.tensor_tensor(q_e, m["hq"][:, :, now], e_inter, ALU.mult)
                v.tensor_tensor(k_e, k_e, m["hk"][:, :, now], ALU.mult).then_inc(s["inter_scaled"], 1)
                for j in range(PAIRS):
                    v.wait_ge(s["scores_ready"], after("scores_ready", c, j + 1))
                    waited(v)
                    mask = core.causal.rearrange("p a t -> p (a t)").bitcast(I32).unsqueeze(1).to_broadcast([P, 2, 2 * P])
                    for e in range(2):
                        ins = v.copy_predicated(scores[:, 2 * j + e].rearrange("p (b a) t -> p b (a t)", b=2), mask,
                                                bank[2 + 2 * (j % 2) + e][:].rearrange("p (b a) -> p b a", b=2))
                    ins.then_inc(s["scores_taken"], 1)
                    if j == 0:
                        v.wait_ge(s["hg_scores"], after("hg_scores", c, 1))
                        v.tensor_tensor(att_t, heads_of(bank[0]), core.ident.unsqueeze(1).to_broadcast([P, HG_HEADS, P]),
                                        ALU.mult).then_inc(s["hg_att"], 1)
                    if j % 2 == 1:
                        heads = slice(2 * (j - 1), 2 * (j + 1))
                        v.wait_ge(s["scores_taken"], after("scores_taken", c, j + 1))
                        mask1 = core.mask_t[:, len(LEVELS) - 1:len(LEVELS), :].to_broadcast([P, 4, P])
                        link(v.tensor_tensor(x_t[:, heads, :], scores[:, heads, 0, :], mask1, ALU.mult))
                        v.tensor_tensor(x_t[:, heads, :], x_t[:, heads, :],
                                        core.ident.unsqueeze(1).to_broadcast([P, 4, P]), ALU.add).then_inc(s["xt_first"], 1)
                for i in range(n_inv):
                    if i + 2 <= len(LEVELS):
                        level_scale(i + 2)
                    if i + 3 <= len(LEVELS):
                        level_diff(i + 3)
                    level_keep(i + 1)
                    lv = inv_level[i]
                    for b in range(2):
                        heads = slice(4 * b, 4 * b + 4)
                        v.wait_ge(inv_z[b], c * n_inv + i + 1)
                        waited(v)
                        if i < n_inv - 1:
                            v.copy_predicated(x_n[:, heads, :], core.mask_n[:, lv:lv + 1, :].bitcast(I32).to_broadcast([P, 4, P]),
                                              heads_of(bank[head_bank["z"][b]]))
                        v.copy_predicated(x_t[:, heads, :], core.mask_t[:, lv:lv + 1, :].bitcast(I32).to_broadcast([P, 4, P]),
                                          heads_of(bank[head_bank["zt"][b]])).then_inc(inv_done[b], 1)
                level_keep(len(LEVELS))
                v.wait_ge(s["hg_out"], after("hg_out", c, 2))
                for h in range(HG_HEADS):
                    v.scalar_tensor_tensor(out=state_h[:, h, :], in0=state_h[:, h, :], scalar=e_inter[:, h, P - 1:P],
                                           in1=heads_of(bank[1])[:, h, :], op0=ALU.mult, op1=ALU.add)
                v.wait_ge(s["state_ready"], after("state_ready", c, 1))
                link(v.tensor_tensor(state, state_0, bank[6][:, 0:PAIRS * RH].rearrange("p (j v) -> p j v", v=RH), ALU.add))
                v.tensor_tensor(state, state, e1[:, :, P - 1:P].to_broadcast([P, PAIRS, RH]), ALU.mult).then_inc(dve_end, 1)
                link.restart()

        @block.tensor
        def _(pe):
            pe.wait_ge(first_state, 1)
            with pe.Fori(0, NB) as c:
                pe.wait_ge(act_end, c)
                pe.wait_ge(dve_end, c)
                pe.wait_ge(pe_end, c)
                now = bass.ds(c * P, P)

                def turn(src, to):
                    for j in range(4):
                        ins = pe.transpose(bank[to][:, j * P:(j + 1) * P], src[:, j, :], core.ident)
                    ins.then_inc(s["tok_ready"], 1)

                def level_scores(i):
                    pe.wait_ge(s["hg_scaled"], after("hg_scaled", c, i))
                    if i >= 2:
                        pe.wait_ge(s["hg_att"], i - 1)
                    for h in range(HG_HEADS):
                        g = level_g[:, i % 2, h, :]
                        ins = pe.matmul(bank[i % 2][:, h * P:(h + 1) * P], g, g, start=True, stop=True)
                    ins.then_inc(s["hg_scores"], 1)

                pe.wait_ge(s["staged"], after("staged", c, 1))
                turn(v_stage, 6)
                pe.wait_ge(s["staged"], after("staged", c, 2))
                for h in range(HG_HEADS):
                    ins = pe.matmul(bank[0][:, h * P:(h + 1) * P], k_stage[:, h, :], m["hq"][:, h, now], start=True, stop=True)
                ins.then_inc(s["hg_scores"], 1)
                pe.wait_ge(s["rw_scaled"], after("rw_scaled", c, 1))
                turn(k_s, 7)
                pe.wait_ge(s["tok_taken"], after("tok_taken", c, 1))
                turn(b_s, 6)
                for j in range(PAIRS):
                    if j >= 2:
                        pe.wait_ge(s["scores_taken"], after("scores_taken", c, j - 1))
                    for e in range(2):
                        rows = slice(RH * e, RH * (e + 1))
                        to = bank[2 + 2 * (j % 2) + e]
                        both = kr[rows, j].rearrange("p a t -> p (a t)")
                        pe.matmul(to[:, 0:2 * P], b_s[rows, j, :], both, start=True, stop=True)
                        ins = pe.matmul(to[:, 2 * P:4 * P], k_s[rows, j, :], both, start=True, stop=True)
                    ins.then_inc(s["scores_ready"], 1)
                pe.wait_ge(s["inter_scaled"], after("inter_scaled", c, 1))
                pe.wait_ge(s["tok_taken"], after("tok_taken", c, 2))
                turn(k_e, 7)
                for b in range(2):
                    pe.wait_ge(s["xt_first"], after("xt_first", c, b + 1))
                    pe.wait_ge(s["scores_taken"], after("scores_taken", c, 3 + b))
                    pe.wait_ge(s["tok_taken"], after("tok_taken", c, 3))
                    for j in range(4):
                        ins = pe.transpose(bank[head_bank["z"][b]][:, j * P:(j + 1) * P], x_t[:, 4 * b + j, :], core.ident)
                    ins.then_inc(s["x_first"], 1)
                pe.wait_ge(s["scores_taken"], after("scores_taken", c, PAIRS))
                pe.wait_ge(s["tok_taken"], after("tok_taken", c, 4))
                for i in range(n_inv):
                    for b in range(2):
                        if i == 0:
                            pe.wait_ge(s["x_first_taken"], after("x_first_taken", c, b + 1))
                        else:
                            pe.wait_ge(inv_done[b], c * n_inv + i)
                        for j in range(4):
                            h = 4 * b + j
                            ins = pe.matmul(bank[head_bank["y"][b]][:, j * P:(j + 1) * P], scores[:, h, 0, :], x_n[:, h, :],
                                            start=True, stop=True)
                        ins.then_inc(inv_y[b], 1)
                    level_scores(i + 1)
                    for b in range(2):
                        pe.wait_ge(inv_y_taken[b], c * n_inv + i + 1)
                        for j in range(4):
                            h = 4 * b + j
                            if i < n_inv - 1:
                                pe.matmul(bank[head_bank["z"][b]][:, j * P:(j + 1) * P], x_t[:, h, :], y_sb[:, b, j, :],
                                          start=True, stop=True)
                            ins = pe.matmul(bank[head_bank["zt"][b]][:, j * P:(j + 1) * P], y_sb[:, b, j, :], x_t[:, h, :],
                                            start=True, stop=True)
                        ins.then_inc(inv_z[b], 1)
                level_scores(len(LEVELS))
                for e in range(2):
                    rows = slice(RH * e, RH * (e + 1))
                    for j in range(PAIRS):
                        h = 2 * j + e
                        to = bank[(2, 5)[e]][:, j * RH:(j + 1) * RH]
                        pe.matmul(to, kr[rows, j, 0, :], state_0[rows, j, :], start=True, stop=False)
                        ins = pe.matmul(to, scores[:, h, 2, :], v_tok.rearrange("p j v -> p (j v)")[:, h * RH:(h + 1) * RH],
                                        start=False, stop=True)
                ins.then_inc(s["rhs_ready"], 1)
                pe.wait_ge(s["hg_att"], after("hg_att", c, len(LEVELS) + 1))
                for h in range(HG_HEADS):
                    to = bank[0][:, h * P:(h + 1) * P]
                    pe.matmul(to, v_h[:, h, :], att_t[:, h, :], start=True, stop=False)
                    ins = pe.matmul(to, state_h[:, h, :], q_e[:, h, :], start=False, stop=True)
                ins.then_inc(s["hg_out"], 1)
                for h in range(HG_HEADS):
                    ins = pe.matmul(bank[1][:, h * P:(h + 1) * P], k_tok_h[:, h, :], v_h[:, h, :], start=True, stop=True)
                ins.then_inc(s["hg_out"], 1)
                pe.wait_ge(s["rhs_taken"], after("rhs_taken", c, 1))
                pe.wait_ge(inv_done[0], c * n_inv + n_inv)
                pe.wait_ge(inv_done[1], c * n_inv + n_inv)
                for h in range(RW_HEADS):
                    ins = pe.matmul(bank[3][:, h * RH:(h + 1) * RH], x_t[:, h, :], rhs[:, PAIRS * (h % 2) + h // 2, :],
                                    start=True, stop=True)
                ins.then_inc(s["u_ready"], 1)
                pe.wait_ge(s["u_taken"], after("u_taken", c, 1))
                v_heads = v_tok.rearrange("p j v -> p (j v)")
                for e in range(2):
                    rows = slice(RH * e, RH * (e + 1))
                    for j in range(PAIRS):
                        h = 2 * j + e
                        to = bank[4][rows, j * P:(j + 1) * P]
                        pe.matmul(to, v_heads[:, h * RH:(h + 1) * RH], scores[:, h, 3, :], start=True, stop=False)
                        pe.matmul(to, u[:, h, :], scores[:, h, 1, :], start=False, stop=False)
                        ins = pe.matmul(to, state_0[rows, j, :], kr[rows, j, 1, :], start=False, stop=True)
                ins.then_inc(s["out_ready"], 1)
                for e in range(2):
                    rows = slice(RH * e, RH * (e + 1))
                    for j in range(PAIRS):
                        h = 2 * j + e
                        to = bank[6][rows, j * RH:(j + 1) * RH]
                        pe.matmul(to, k_tok[:, j, rows], v_heads[:, h * RH:(h + 1) * RH], start=True, stop=False)
                        ins = pe.matmul(to, b_tok[:, j, rows], u[:, h, :], start=False, stop=True)
                ins.then_inc(s["state_ready"], 1)
                pe.nop().then_inc(pe_end, 1)


def finish(core, x, w_in_strips, g2, w_branch_hg, w_branch_rw, w_out, norm_ffn, wq):
    nc = core.nc
    m = mixer_inputs(core)
    bank = core.bank
    gates_all = core.slots(33, 16)
    gates = (gates_all[:, 0:8, :], gates_all[:, 8:16, :])
    ring = [core.slots(57 + 4 * i, 4, STRIP) for i in range(2)]
    yc, y_sq, y_root, y_inv, rk, out, o_sq, o_root, g2_all, g2_now = (core.slots(s, 1)[:, 0, :] for s in range(65, 75))
    g2_now = g2_now[:, 0:P]
    w_hg, w_rw = core.slots(75, 8, D), core.slots(83, 8, D)
    norm_row = core.slots(91, 2, D)[:, 0, :]
    product = core.slots(93, 2)
    merged = core.slots(8, 8)
    w_out_sb = core.slots(57, 16, D)
    x2 = core.slots(49, 8, D)
    wq_sb = core.slots(75, 16, D)
    h_tok, h_t, q_t = core.slots(33, 8, D), core.slots(0, 8), core.slots(41, 8)
    junk = core.slots(73, 2, D)[:, 0, :]
    ssq, mean, root, rstd = (core.stats[:, 4 * i:4 * i + 4] for i in range(4))

    strip_loaded = [core.sem(f"gate_strip_loaded{i}") for i in range(2)]
    g2_loaded = core.sem("g2_loaded")
    weights = core.sem("branch_weights_loaded")
    w_out_loaded = core.sem("w_out_loaded")
    x_loaded = core.sem("x_reloaded")
    wq_loaded = core.sem("wq_loaded")
    y_mean = core.sem("y_mean_summed")
    centred = core.sem("y_centred")
    y_squared = core.sem("y_squared")
    y_var = core.sem("y_variance_summed")
    rooting = core.sem("variances_ready")
    rooted = core.sem("variances_rooted")
    o_squared = core.sem("o_squared")
    o_sum = core.sem("o_squares_summed")
    rk_ready = core.sem("rk_ready")
    rk_sum = core.sem("rk_summed")
    g2_staged = core.sem("g2_staged")
    g_ready = core.sem("g_ready")
    y_done = core.sem("y_done")
    gates_ready = core.sem("gates_ready")
    gates_taken = core.sem("gates_taken")
    branch_ready = core.sem("branch_ready")
    branch_used = core.sem("branch_used")
    merged_ready = core.sem("merged_ready")
    out_ready = core.sem("w_out_summed")
    x2_ready = core.sem("x2_ready")
    squares = core.sem("x2_squares_summed")
    ms_ready = core.sem("x2_mean_squares_ready")
    x2_rooted = core.sem("x2_rooted")
    h_ready = core.sem("ffn_input_ready")
    turned = core.sem("ffn_input_turned")
    turned_taken = core.sem("ffn_input_turned_taken")
    q_ready = core.sem("queries_ready")
    v_link = core.sem("finish_vector_link")

    with nc.Block() as block:
        @block.sync
        def _(sp):
            sp.dma_start(g2_all, g2).then_inc(g2_loaded, 16)
            for n, strip in enumerate(GATE_STRIPS):
                if n >= 2:
                    sp.wait_ge(gates_ready, 2 * (n - 2) + 2)
                sp.dma_start(ring[n % 2], w_in_strips[strip]).then_inc(strip_loaded[n % 2], 16)
                if n == 1:
                    sp.dma_start(w_hg, w_branch_hg.rearrange("(k p) n -> p k n", p=P)).then_inc(weights, 16)
                    sp.dma_start(w_rw, w_branch_rw.rearrange("(k p) n -> p k n", p=P)).then_inc(weights, 16)
                    sp.dma_start(norm_row, norm_ffn.partition_broadcast(P)).then_inc(weights, 16)
            sp.wait_ge(y_done, PAIRS)
            sp.wait_ge(gates_ready, 16)
            sp.dma_start(x2, x.rearrange("(b p) d -> p b d", p=P)).then_inc(x_loaded, 16)
            sp.dma_start(w_out_sb, w_out.rearrange("(k p) n -> p k n", p=P)).then_inc(w_out_loaded, 16)
            sp.wait_ge(branch_ready, 16)
            sp.dma_start(wq_sb, wq.rearrange("(k p) n -> p k n", p=P)).then_inc(wq_loaded, 16)

        @block.tensor
        def _(pe):
            pe.wait_ge(g2_loaded, 16)
            with pe.Fori(0, PAIRS) as j:
                one = bass.ds(j, 1)

                def strip(half):
                    pe.wait_ge(strip_loaded[half], 16 * (j + 1))
                    for t in range(2):
                        b = 2 * half + t
                        pe.wait_ge(gates_taken, 4 * j + b - 3 + 4)
                        for k in range(KD):
                            ins = pe.matmul(bank[b][:], ring[half][:, k, t * P:(t + 1) * P], m["h_t"][:, k, :],
                                            start=(k == 0), stop=(k == KD - 1))
                        ins.then_inc(gates_ready, 1)

                pe.wait_ge(y_done, j)
                pe.matmul(bank[4][:], core.ones_pair, m["ld"][:, one, :], start=True, stop=True).then_inc(y_mean, 1)
                pe.wait_ge(rk_ready, j + 1)
                pe.matmul(bank[5][:], core.ones_pair, rk, start=True, stop=True).then_inc(rk_sum, 1)
                pe.wait_ge(g2_staged, j + 1)
                pe.matmul(bank[6][:], g2_now, m["sgd"], start=True, stop=True).then_inc(g_ready, 1)
                pe.wait_ge(o_squared, j + 1)
                pe.matmul(bank[7][:], core.ones_full, o_sq, start=True, stop=True).then_inc(o_sum, 1)
                strip(0)
                pe.wait_ge(y_squared, j + 1)
                pe.matmul(bank[4][:], core.ones_pair, y_sq, start=True, stop=True).then_inc(y_var, 1)
                strip(1)
            pe.wait_ge(weights, 48)
            pe.wait_ge(y_done, PAIRS)
            pe.wait_ge(gates_taken, 4 * PAIRS + 4)
            for t in range(KD):
                if t >= 2:
                    pe.wait_ge(branch_used, 2 * (t - 1))
                for which, w, y in ((0, w_hg, m["hq"]), (1, w_rw, m["ld"])):
                    for k in range(4):
                        ins = pe.matmul(bank[2 * (t % 2) + which][:], w[:, k, t * P:(t + 1) * P], y[:, k, :],
                                        start=(k == 0), stop=(k == 3))
                    ins.then_inc(branch_ready, 1)
            pe.wait_ge(merged_ready, KD)
            pe.wait_ge(w_out_loaded, 16)
            for b in range(NB):
                for half in range(2):
                    if b >= 2:
                        pe.wait_ge(x2_ready, 2 * (b - 2) + half + 1)
                    for k in range(KD):
                        ins = pe.matmul(bank[2 * (b % 2) + half][:], merged[:, k, b * P:(b + 1) * P],
                                        w_out_sb[:, k, half * 512:(half + 1) * 512], start=(k == 0), stop=(k == KD - 1))
                    ins.then_inc(out_ready, 1)
            for b in range(NB):
                pe.wait_ge(h_ready, b + 1)
                for half in range(2):
                    if b:
                        pe.wait_ge(turned_taken, 2 * (b - 1) + half + 1)
                    for k in range(4):
                        dk = 4 * half + k
                        ins = pe.transpose(bank[4 + half][:, k * P:(k + 1) * P], h_tok[:, b, dk * P:(dk + 1) * P], core.ident)
                    ins.then_inc(turned, 1)
            pe.wait_ge(turned_taken, 2 * NB)
            pe.wait_ge(wq_loaded, 16)
            pe.wait_ge(x2_ready, 2 * NB)
            for h in range(PK_HEADS):
                if h >= 2:
                    pe.wait_ge(turned_taken, 2 * NB + h - 1)
                for k in range(KD):
                    ins = pe.matmul(bank[h % 2][:], wq_sb[:, k, h * P:(h + 1) * P], h_t[:, k, :], start=(k == 0),
                                    stop=(k == KD - 1))
                ins.then_inc(q_ready, 1)

        @block.scalar
        def _(act):
            act.wait_ge(g2_loaded, 16)
            act.nop().then_inc(gates_taken, 4)
            with act.Fori(0, PAIRS) as j:
                one = bass.ds(j, 1)
                act.wait_ge(g_ready, j)
                act.activation(g2_now, g2_all[:, bass.ds(j * P, P)], ACT.Copy).then_inc(g2_staged, 1)
                act.wait_ge(o_sum, j)
                act.activation(o_sq, m["hq"][:, one, :], ACT.Square).then_inc(o_squared, 1)
                act.wait_ge(centred, j + 1)
                act.wait_ge(y_var, j)
                act.activation(y_sq, yc, ACT.Square).then_inc(y_squared, 1)

                def gate(b):
                    act.wait_ge(gates_ready, 4 * j + b + 1)
                    act.activation(gates_all[:, bass.ds(4 * j + b, 1), :], bank[b][:], ACT.Sigmoid).then_inc(gates_taken, 1)

                for b in range(4):
                    gate(b)
                act.wait_ge(rooting, 2 * j + 2)
                act.activation(y_root, y_root, ACT.Sqrt)
                act.activation(o_root, o_root, ACT.Sqrt).then_inc(rooted, 1)
            for b in range(NB):
                act.wait_ge(x2_ready, 2 * b + 2)
                if b:
                    act.wait_ge(squares, b)
                act.activation(junk, x2[:, b, :], ACT.Square, accum_out=ssq[:, b:b + 1]).then_inc(squares, 1)
                act.wait_ge(ms_ready, b + 1)
                act.activation(root[:, b:b + 1], mean[:, b:b + 1], ACT.Sqrt).then_inc(x2_rooted, 1)
            for b in range(NB):
                for half in range(2):
                    act.wait_ge(turned, 2 * b + half + 1)
                    act.activation(h_t[:, 4 * half:4 * half + 4, b * P:(b + 1) * P],
                                   bank[4 + half][:].rearrange("p (k t) -> p k t", t=P), ACT.Copy).then_inc(turned_taken, 1)
            for h in range(PK_HEADS):
                act.wait_ge(q_ready, h + 1)
                act.activation(q_t[:, h, :], bank[h % 2][:], ACT.Copy).then_inc(turned_taken, 1)

        @block.vector
        def _(v):
            link = Link(v, v_link)
            with v.Fori(0, PAIRS) as j:
                one = bass.ds(j, 1)

                def col(name):
                    return core.cols[:, bass.ds(j + COLS[name][0], 1)]

                y, o = m["ld"][:, one, :], m["hq"][:, one, :]
                link(v.scalar_tensor_tensor(out=rk, in0=m["r"][:, one, :], scalar=col("r_k"), in1=m["k"][:, one, :],
                                            op0=ALU.mult, op1=ALU.mult))
                v.sem_inc(rk_ready, 1)
                v.wait_ge(y_mean, j + 1)
                v.scalar_tensor_tensor(out=yc, in0=bank[4][:], scalar=-1.0 / RH, in1=y, op0=ALU.mult,
                                       op1=ALU.add).then_inc(centred, 1)
                v.wait_ge(o_sum, j + 1)
                v.tensor_scalar(o_root, bank[7][:], 1.0 / P, EPS, ALU.mult, ALU.add).then_inc(rooting, 1)
                v.wait_ge(rk_sum, j + 1)
                link(v.tensor_tensor(rk, bank[5][:], m["v"][:, one, :], ALU.mult))
                v.wait_ge(y_var, j + 1)
                v.tensor_scalar(y_root, bank[4][:], 1.0 / RH, GN_EPS, ALU.mult, ALU.add).then_inc(rooting, 1)
                v.wait_ge(rooted, j + 1)
                link(v.reciprocal(y_inv, y_root))
                link(v.tensor_tensor(yc, yc, y_inv, ALU.mult))
                link(v.tensor_scalar(out, yc, col("ln_w"), col("ln_b"), ALU.mult, ALU.add))
                link(v.tensor_tensor(out, out, rk, ALU.add))
                v.wait_ge(g_ready, j + 1)
                link(v.tensor_tensor(y, out, bank[6][:], ALU.mult))
                link(v.reciprocal(y_inv, o_root))
                link(v.tensor_tensor(o, o, y_inv, ALU.mult))
                link(v.tensor_tensor(o, o, m["hgo"][:, one, :], ALU.mult))
                v.sem_inc(y_done, 1)
                link.restart()
            v.wait_ge(gates_taken, 4 * PAIRS + 4)
            for t in range(KD):
                v.wait_ge(branch_ready, 2 * t + 1)
                v.tensor_tensor(product[:, 0, :], bank[2 * (t % 2)][:], gates[0][:, t, :], ALU.mult).then_inc(branch_used, 1)
                v.wait_ge(branch_ready, 2 * t + 2)
                v.tensor_tensor(product[:, 1, :], bank[2 * (t % 2) + 1][:], gates[1][:, t, :], ALU.mult).then_inc(branch_used, 1)
                v.wait_ge(branch_used, 2 * t + 2)
                v.tensor_tensor(merged[:, t, :], product[:, 0, :], product[:, 1, :], ALU.add).then_inc(merged_ready, 1)
                v.wait_ge(merged_ready, t + 1)
            v.wait_ge(x_loaded, 16)
            v.wait_ge(weights, 48)

            def residual(b):
                for half in range(2):
                    v.wait_ge(out_ready, 2 * b + half + 1)
                    part = x2[:, b, half * 512:(half + 1) * 512]
                    v.tensor_tensor(part, part, bank[2 * (b % 2) + half][:], ALU.add).then_inc(x2_ready, 1)

            def normed(b):
                v.wait_ge(squares, b + 1)
                v.tensor_scalar(mean[:, b:b + 1], ssq[:, b:b + 1], 1.0 / D, EPS, ALU.mult, ALU.add).then_inc(ms_ready, 1)
                v.wait_ge(x2_rooted, b + 1)
                link(v.reciprocal(rstd[:, b:b + 1], root[:, b:b + 1]))
                v.scalar_tensor_tensor(out=h_tok[:, b, :], in0=x2[:, b, :], scalar=rstd[:, b:b + 1], in1=norm_row,
                                       op0=ALU.mult, op1=ALU.mult).then_inc(h_ready, 1)

            residual(0)
            for b in range(1, NB):
                residual(b)
                normed(b - 1)
            normed(NB - 1)


def experts(core, keys_t, u_emb, v_emb, ple_gate, ple_proj, p_in, final_norm):
    nc = core.nc
    bank = core.bank
    turns = NB * PK_HEADS // 2
    per_block = PK_HEADS // 2
    picks = 2 * TOPK
    depth = 8
    diags = 4
    uses = picks // depth
    x2, h_tok, q_t = core.slots(49, 8, D), core.slots(33, 8, D), core.slots(41, 8)
    u_ring, v_ring = core.slots(0, 16, D), core.slots(57, 16, D)
    keys = core.slots(24, 1, 2 * N_KEYS)[:, 0, :]
    sc = core.slots(25, 1, N_KEYS)
    rest = core.slots(26, 1, N_KEYS)
    q_now = core.slots(30, 1, P)[:, 0:2, :]
    diag = core.slots(31, 1, P)
    onehot = core.arena[:, 91 * SLOT:91 * SLOT + picks * N_CAND]
    at = 27 * SLOT

    def small(*shape, dt=F32):
        nonlocal at
        n = 1
        for d in shape:
            n *= d
        ap = core.arena[:, at:at + n]
        at += n
        if dt != F32:
            ap = ap.bitcast(dt)
        return ap if len(shape) == 1 else ap.rearrange("p (a b) -> p a b", b=shape[1])

    top, top_i, top_f = small(4, TOPK), small(4, TOPK, dt=U32), small(4, TOPK)
    cand, cand_id, cand_rest = small(2, N_CAND), small(2, N_CAND), small(2, N_CAND)
    best, best_i, best_f = small(2, TOPK), small(2, TOPK, dt=U32), small(2, TOPK)
    ids_f, shifted, weight = small(picks), small(2, TOPK), small(2, TOPK)
    total, inverse = small(2), small(2)
    gate_next, gate_now = small(2, TOPK), small(2, TOPK)
    ids = small(2, picks, dt=U32)
    dots, gelu, coef = small(2, TOPK), small(2, TOPK), small(2, TOPK)
    assert at <= 30 * SLOT

    keys_zero = core.sem("keys_zeroed")
    keys_loaded = core.sem("keys_loaded")
    ple_loaded = core.sem("ple_weights_loaded")
    u_loaded = [core.sem(f"u_row_loaded{i}") for i in range(depth)]
    v_loaded = [core.sem(f"v_row_loaded{i}") for i in range(depth)]
    u_used = core.sem("u_row_used")
    v_used = core.sem("v_row_used")
    q_staged = core.sem("query_staged")
    sc_ready = core.sem("key_scores_ready")
    sc_taken = core.sem("key_scores_taken")
    ids_ready = core.sem("ids_ready")
    shift_ready = core.sem("best_scores_shifted")
    exp_ready = core.sem("best_scores_exp")
    gelu_ready = core.sem("gelu_ready")
    coef_ready = core.sem("coefficients_ready")
    diag_ready = core.sem("diagonal_ready")
    acc_taken = core.sem("sum_taken")
    v_link = core.sem("experts_vector_link")
    carrier = core.sem("experts_gpsimd_wait_carrier")
    carrier_v = core.sem("experts_vector_wait_carrier")

    with nc.Block() as block:
        @block.sync
        def _(sp):
            sp.wait_ge(keys_zero, 1)
            for c in range(2):
                sp.dma_start(keys[RH * c:RH * (c + 1), c * N_KEYS:(c + 1) * N_KEYS], keys_t[c]).then_inc(keys_loaded, 16)
            sp.dma_start(core.slots(75, 16, D), ple_gate.rearrange("(k p) n -> p k n", p=P)).then_inc(ple_loaded, 16)
            sp.dma_start(core.slots(16, 4, D), ple_proj.rearrange("(k p) n -> p k n", p=P)).then_inc(ple_loaded, 16)
            sp.dma_start(core.slots(20, 2, PLE), p_in.rearrange("(b p) d -> p b d", p=P)).then_inc(ple_loaded, 16)
            sp.dma_start(core.slots(22, 2, D)[:, 0, :], final_norm.partition_broadcast(P)).then_inc(ple_loaded, 16)
            sp.wait_ge(ple_loaded, 64)

        @block.gpsimd
        def _(gp):
            gp.memset(keys, 0.0).then_inc(keys_zero, 1)

            def gather(n, parity, half):
                for table, ring, loaded, used in ((u_emb, u_ring, u_loaded, u_used), (v_emb, v_ring, v_loaded, v_used)):
                    for k in range(half * TOPK, (half + 1) * TOPK):
                        gp.wait_ge(used, picks * n + k + 1)
                        gp.sem_inc(carrier, 1)
                        gp.indirect_dma_start(ring[:, k % depth, :], None, table,
                                              bass.IndirectOffsetOnAxis(ap=ids[:, parity, k:k + 1], axis=0),
                                              ).then_inc(loaded[k % depth], 16)

            with gp.Fori(0, turns, 2) as n:
                for parity in range(2):
                    gp.wait_ge(ids_ready, n + parity + 1)
                    gp.sem_inc(carrier, 1)
                    gather(n + parity, parity, 0)
                    gather(n + parity, parity, 1)

        @block.tensor
        def _(pe):
            pe.nop().then_inc(v_used, depth)
            pe.wait_ge(keys_loaded, 32)

            def key_scores(n):
                pe.wait_ge(q_staged, n + 1)
                pe.wait_ge(sc_taken, n)
                for h in range(2):
                    ins = pe.matmul(bank[2][:, h * 2 * N_KEYS:(h + 1) * 2 * N_KEYS], q_now[:, h, :], keys, start=True,
                                    stop=True)
                ins.then_inc(sc_ready, 1)

            def turn(n, more):
                if more:
                    key_scores(n + 1)
                pe.wait_ge(acc_taken, n)
                for k in range(picks):
                    pe.wait_ge(v_loaded[k % depth], 16 * (uses * n + k // depth + 1))
                    pe.wait_ge(diag_ready, picks * n + k + 1)
                    for half in range(2):
                        ins = pe.matmul(bank[half][:], diag[:, k % diags, :], v_ring[:, k % depth, half * 512:(half + 1) * 512],
                                        start=(k == 0), stop=(k == picks - 1))
                    ins.then_inc(v_used, 1)

            key_scores(0)
            with pe.Fori(0, turns - 1) as n:
                turn(n, True)
            turn(turns - 1, False)

        @block.scalar
        def _(act):
            def stage_query(n):
                act.wait_ge(sc_ready, n)
                block_, pair = n // per_block, n % per_block
                act.activation(q_now, q_t[:, bass.ds(2 * pair, 2), bass.ds(block_ * P, P)], ACT.Copy).then_inc(q_staged, 1)

            def head(n, half):
                act.wait_ge(u_used, depth + picks * n + TOPK * (half + 1))
                act.activation(gelu[:, half, :], dots[:, half, :], ACT.Gelu).then_inc(gelu_ready, 1)
                act.wait_ge(coef_ready, 2 * n + half + 1)
                for k in range(TOPK * half, TOPK * (half + 1)):
                    act.wait_ge(v_used, depth + picks * n + k - diags + 1)
                    act.activation(diag[:, k % diags, :], core.ident, ACT.Copy,
                                   scale=coef[:, half, k % TOPK:k % TOPK + 1]).then_inc(diag_ready, 1)

            def softmax_exp(n):
                act.wait_ge(shift_ready, n + 1)
                act.activation(weight, shifted, ACT.Exp).then_inc(exp_ready, 1)

            stage_query(0)
            softmax_exp(0)
            with act.Fori(0, turns - 1) as n:
                stage_query(n + 1)
                head(n, 0)
                softmax_exp(n + 1)
                head(n, 1)
            for half in range(2):
                head(turns - 1, half)

        @block.vector
        def _(v):
            link = Link(v, v_link)
            v.nop().then_inc(u_used, depth)

            def select(n):
                v.wait_ge(sc_ready, n + 1)
                v.tensor_copy(sc, bank[2][:].rearrange("p (a b) -> p a b", b=N_KEYS)).then_inc(sc_taken, 1)
                v.wait_ge(sc_taken, n + 1)
                v.sem_inc(carrier_v, 1)
                for a in range(4):
                    ins = v.max(top[:, a, 0:8], sc[:, a, :])
                link(ins)
                for a in range(4):
                    v.max_index(top_i[:, a, 0:8], top[:, a, 0:8], sc[:, a, :])
                    ins = v.match_replace(rest[:, a, :], top[:, a, 0:8], sc[:, a, :], LOWEST)
                link(ins)
                for a in range(4):
                    ins = v.max(top[:, a, 8:16], rest[:, a, :])
                link(ins)
                for a in range(4):
                    ins = v.max_index(top_i[:, a, 8:16], top[:, a, 8:16], rest[:, a, :])
                link(ins)
                link(v.tensor_copy(top_f, top_i))
                scores_ = top.rearrange("p (h c) k -> p h c k", c=2)
                index_ = top_f.rearrange("p (h c) k -> p h c k", c=2)
                to = 0
                for i in range(8):
                    w = CAND[i]
                    v.tensor_tensor(cand[:, :, to:to + w], scores_[:, :, 0, i:i + 1].to_broadcast([P, 2, w]),
                                    scores_[:, :, 1, 0:w], ALU.add)
                    v.scalar_tensor_tensor(out=cand_id[:, :, to:to + w], in0=index_[:, :, 0, i:i + 1].to_broadcast([P, 2, w]),
                                           scalar=float(N_KEYS), in1=index_[:, :, 1, 0:w], op0=ALU.mult, op1=ALU.add)
                    to += w
                v.tensor_tensor(cand[:, :, to:], scores_[:, :, 0, 8:16], scores_[:, :, 1, 0:1].to_broadcast([P, 2, 8]), ALU.add)
                link(v.scalar_tensor_tensor(out=cand_id[:, :, to:], in0=index_[:, :, 0, 8:16], scalar=float(N_KEYS),
                                            in1=index_[:, :, 1, 0:1].to_broadcast([P, 2, 8]), op0=ALU.mult, op1=ALU.add))
                for h in range(2):
                    ins = v.max(best[:, h, 0:8], cand[:, h, :])
                link(ins)
                for h in range(2):
                    v.max_index(best_i[:, h, 0:8], best[:, h, 0:8], cand[:, h, :])
                    ins = v.match_replace(cand_rest[:, h, :], best[:, h, 0:8], cand[:, h, :], LOWEST)
                link(ins)
                for h in range(2):
                    ins = v.max(best[:, h, 8:16], cand_rest[:, h, :])
                link(ins)
                for h in range(2):
                    ins = v.max_index(best_i[:, h, 8:16], best[:, h, 8:16], cand_rest[:, h, :])
                link(ins)
                v.tensor_tensor(shifted, best, best[:, :, 0:1].to_broadcast([P, 2, TOPK]), ALU.subtract).then_inc(shift_ready, 1)
                link(v.tensor_copy(best_f, best_i))
                hot = onehot.rearrange("p (k c) -> p k c", c=N_CAND)
                link(v.tensor_tensor(hot, best_f.rearrange("p h k -> p (h k)").unsqueeze(2).to_broadcast([P, picks, N_CAND]),
                                     core.iota_cand.unsqueeze(1).to_broadcast([P, picks, N_CAND]), ALU.is_equal))
                hot4 = onehot.rearrange("p (h k c) -> p h k c", h=2, c=N_CAND)
                link(v.tensor_tensor(hot4, hot4, cand_id.unsqueeze(2).to_broadcast([P, 2, TOPK, N_CAND]), ALU.mult))
                link(v.tensor_reduce(ids_f, hot, AX.X, ALU.add))
                v.tensor_copy(ids[:, bass.ds(n % 2, 1), :], ids_f).then_inc(ids_ready, 1)

            def softmax_rest(n):
                v.wait_ge(exp_ready, n + 1)
                link(v.tensor_reduce(total, weight, AX.X, ALU.add))
                link(v.reciprocal(inverse, total))
                link(v.tensor_tensor(gate_next, weight, inverse.unsqueeze(2).to_broadcast([P, 2, TOPK]), ALU.mult))

            def dot_products(n, half):
                h = h_tok[:, bass.ds(n // per_block, 1), :]
                for k in range(half * TOPK, (half + 1) * TOPK):
                    v.wait_ge(u_loaded[k % depth], 16 * (uses * n + k // depth + 1))
                    row = u_ring[:, k % depth, :]
                    v.scalar_tensor_tensor(out=row, in0=row, scalar=1.0, in1=h, op0=ALU.mult, op1=ALU.mult,
                                           accum_out=dots[:, half, k % TOPK:k % TOPK + 1]).then_inc(u_used, 1)

            def coefficients(n, half):
                v.wait_ge(gelu_ready, 2 * n + half + 1)
                v.tensor_tensor(coef[:, half, :], gelu[:, half, :], gate_now[:, half, :], ALU.mult).then_inc(coef_ready, 1)

            def turn(n, more):
                v.wait_ge(coef_ready, 2 * n)
                link(v.tensor_copy(gate_now, gate_next))
                dot_products(n, 0)
                coefficients(n, 0)
                if more:
                    select(n + 1)
                dot_products(n, 1)
                coefficients(n, 1)
                if more:
                    softmax_rest(n + 1)
                for half in range(2):
                    v.wait_ge(v_used, depth + picks * (n + 1))
                    part = x2[:, bass.ds(n // per_block, 1), half * 512:(half + 1) * 512]
                    ins = v.tensor_tensor(part, part, bank[half][:], ALU.add)
                ins.then_inc(acc_taken, 1)
                v.wait_ge(acc_taken, n + 1)
                v.sem_inc(carrier_v, 1)
                link.restart()

            select(0)
            softmax_rest(0)
            link.restart()
            with v.Fori(0, turns - 1) as n:
                turn(n, True)
            turn(turns - 1, False)


def ple(core, out):
    nc = core.nc
    bank = core.bank
    x2 = core.slots(49, 8, D)
    gate_w, proj_w, p_sb = core.slots(75, 16, D), core.slots(16, 4, D), core.slots(20, 2, PLE)
    final_row = core.slots(22, 2, D)[:, 0, :]
    xs = core.slots(0, 8, D)
    h_t = core.slots(8, 8)
    p_t = core.slots(24, 2)
    gate = core.slots(33, 4, D)
    y = core.slots(41, 4, D)
    junk = core.slots(57, 2, D)[:, 0, :]
    ssq, mean, root, rstd = (core.stats[:, 8 * i:8 * i + 8] for i in range(4))
    squares = core.sem("ple_squares")
    ms_ready = core.sem("ple_mean_squares")
    rooted = core.sem("ple_rooted")
    scaled = core.sem("ple_scaled")
    turned = core.sem("ple_turned")
    taken = core.sem("ple_turned_taken")
    p_turned = core.sem("ple_p_turned")
    p_taken = core.sem("ple_p_taken")
    gate_ready = core.sem("ple_gate_summed")
    proj_ready = core.sem("ple_proj_summed")
    gated = core.sem("ple_gated")
    x3_ready = core.sem("ple_x_ready")
    done = core.sem("ple_output_ready")
    stored = [core.sem(f"ple_stored{i}") for i in range(2)]
    v_link = core.sem("ple_vector_link")

    with nc.Block() as block:
        @block.sync
        def _(sp):
            for b in range(NB):
                sp.wait_ge(done, b + 1)
                sp.dma_start(out[b * P:(b + 1) * P, :], y[:, b % 2, :]).then_inc(stored[b % 2], 16)
            for i in range(2):
                sp.wait_ge(stored[i], 16 * NB // 2)

        @block.tensor
        def _(pe):
            for b in range(NB):
                for k in range(2):
                    ins = pe.transpose(bank[7][:, k * P:(k + 1) * P], p_sb[:, b, k * P:(k + 1) * P], core.ident)
                ins.then_inc(p_turned, 1)
                pe.wait_ge(p_taken, b + 1)

            def turn_block(b):
                pe.wait_ge(scaled, b + 1)
                for half in range(2):
                    if b:
                        pe.wait_ge(taken, 2 * (b - 1) + half + 1)
                    for k in range(4):
                        dk = 4 * half + k
                        ins = pe.transpose(bank[4 + half][:, k * P:(k + 1) * P], xs[:, b, dk * P:(dk + 1) * P], core.ident)
                    ins.then_inc(turned, 1)

            turn_block(0)
            for b in range(NB):
                if b + 1 < NB:
                    turn_block(b + 1)
                now = slice(b * P, (b + 1) * P)
                pe.wait_ge(taken, 2 * b + 2)
                for half in range(2):
                    cols = slice(half * 512, (half + 1) * 512)
                    if b:
                        pe.wait_ge(gated, 2 * (b - 1) + half + 1)
                    for k in range(KD):
                        ins = pe.matmul(bank[half][:], h_t[:, k, now], gate_w[:, k, cols], start=(k == 0), stop=(k == KD - 1))
                    ins.then_inc(gate_ready, 1)
                for half in range(2):
                    cols = slice(half * 512, (half + 1) * 512)
                    if b:
                        pe.wait_ge(x3_ready, 2 * (b - 1) + half + 1)
                    for k in range(2):
                        ins = pe.matmul(bank[2 + half][:], p_t[:, k, now], proj_w[:, k, cols], start=(k == 0), stop=(k == 1))
                    ins.then_inc(proj_ready, 1)

        @block.scalar
        def _(act):
            for b in range(NB):
                act.wait_ge(p_turned, b + 1)
                act.activation(p_t[:, :, b * P:(b + 1) * P], bank[7][:, 0:2 * P].rearrange("p (k t) -> p k t", t=P),
                               ACT.Copy).then_inc(p_taken, 1)

            def square(i, src):
                if i:
                    act.wait_ge(squares, i)
                act.activation(junk, src, ACT.Square, accum_out=ssq[:, i:i + 1]).then_inc(squares, 1)

            def sqrt(i):
                act.wait_ge(ms_ready, i + 1)
                act.activation(root[:, i:i + 1], mean[:, i:i + 1], ACT.Sqrt).then_inc(rooted, 1)

            for b in range(NB):
                square(b, x2[:, b, :])
            act.wait_ge(ms_ready, NB)
            act.activation(root[:, 0:NB], mean[:, 0:NB], ACT.Sqrt).then_inc(rooted, NB)
            for b in range(NB):
                for half in range(2):
                    act.wait_ge(turned, 2 * b + half + 1)
                    for k in range(4):
                        dk = 4 * half + k
                        ins = act.activation(h_t[:, dk, b * P:(b + 1) * P], bank[4 + half][:, k * P:(k + 1) * P], ACT.Copy,
                                             scale=core.col("norm_ple", dk))
                    ins.then_inc(taken, 1)
                for half in range(2):
                    act.wait_ge(gate_ready, 2 * b + half + 1)
                    if b >= 2:
                        act.wait_ge(x3_ready, 2 * (b - 2) + half + 1)
                    act.activation(gate[:, b % 2, half * 512:(half + 1) * 512], bank[half][:], ACT.Sigmoid).then_inc(gated, 1)
                act.wait_ge(x3_ready, 2 * b + 2)
                square(NB + b, x2[:, b, :])
                sqrt(NB + b)

        @block.vector
        def _(v):
            link = Link(v, v_link)
            v.wait_ge(squares, NB)
            v.tensor_scalar(mean[:, 0:NB], ssq[:, 0:NB], 1.0 / D, EPS, ALU.mult, ALU.add).then_inc(ms_ready, NB)
            v.wait_ge(rooted, NB)
            link(v.reciprocal(rstd[:, 0:NB], root[:, 0:NB]))
            for b in range(NB):
                v.tensor_scalar(xs[:, b, :], x2[:, b, :], rstd[:, b:b + 1], None, ALU.mult).then_inc(scaled, 1)
            for b in range(NB):
                for half in range(2):
                    cols = slice(half * 512, (half + 1) * 512)
                    v.wait_ge(gated, 2 * b + half + 1)
                    v.wait_ge(proj_ready, 2 * b + half + 1)
                    link(v.tensor_tensor(gate[:, b % 2, cols], gate[:, b % 2, cols], bank[2 + half][:], ALU.mult))
                    v.tensor_tensor(x2[:, b, cols], x2[:, b, cols], gate[:, b % 2, cols], ALU.add).then_inc(x3_ready, 1)
                i = NB + b
                v.wait_ge(squares, i + 1)
                v.tensor_scalar(mean[:, i:i + 1], ssq[:, i:i + 1], 1.0 / D, EPS, ALU.mult, ALU.add).then_inc(ms_ready, 1)
                v.wait_ge(rooted, i + 1)
                link(v.reciprocal(rstd[:, i:i + 1], root[:, i:i + 1]))
                if b >= 2:
                    v.wait_ge(stored[b % 2], 16 * (b // 2))
                v.scalar_tensor_tensor(out=y[:, b % 2, :], in0=x2[:, b, :], scalar=rstd[:, i:i + 1], in1=final_row,
                                       op0=ALU.mult, op1=ALU.mult).then_inc(done, 1)


def hybrid_block(nc, x, strips, params, w2, a2, g2, w_branch_hg, w_branch_rw, w_out, norm_ffn, wq, keys_t, u_emb, v_emb,
                 ple_gate, ple_proj, p_in, final_norm, out):
    with ExitStack() as ctx:
        core = Core(nc, ctx)
        project(core, x, strips, params, w2, a2, g2)
        mix(core)
        finish(core, x, strips, g2, w_branch_hg, w_branch_rw, w_out, norm_ffn, wq)
        experts(core, keys_t, u_emb, v_emb, ple_gate, ple_proj, p_in, final_norm)
        ple(core, out)


def kernel(**inputs):
    import numpy as np
    import concourse.bacc as bacc
    from concourse.bass_utils import run_bass_kernel_spmd

    a = {name: np.asarray(value) for name, value in inputs.items()}
    vectors = [a["norm_mix_w"], a["rw_mu"], a["rw_w0"], a["rw_a0"], a["rw_k_k"], a["rw_k_a"], a["rw_r_k"], a["rw_ln_w"],
               a["rw_ln_b"], a["hg_lb"][0], a["hg_lb"][1], a["hg_norm_w"], a["norm_ple_w"]]
    arrays = {
        "x": a["x"][0],
        "w_in_strips": a["w_in"][0].reshape(KD, P, -1, STRIP).transpose(2, 1, 0, 3),
        "params": np.concatenate([vector.reshape(-1, P).T for vector in vectors], axis=1),
        "w2": a["rw_w2"][0], "a2": a["rw_a2"][0], "g2": a["rw_g2"][0],
        "w_branch_hg": a["w_branch_hg"][0], "w_branch_rw": a["w_branch_rw"][0], "w_out": a["w_out"][0],
        "norm_ffn": a["norm_ffn_w"][0], "wq": a["peer_wq"][0], "keys_t": a["peer_keys"][0].transpose(0, 2, 1),
        "u_emb": a["peer_u"][0], "v_emb": a["peer_v"][0], "ple_gate": a["ple_gate"][0], "ple_proj": a["ple_proj"][0],
        "p_in": a["p"][0, 0], "final_norm": a["final_norm_w"],
    }
    arrays = {name: np.ascontiguousarray(value) for name, value in arrays.items()}
    nc = bacc.Bacc("TRN2", target_bir_lowering=False, num_devices=1)
    args = [nc.dram_tensor(name, value.shape, mybir.dt.from_np(value.dtype), kind="ExternalInput").ap()
            for name, value in arrays.items()]
    out = nc.dram_tensor("out", (SEQ, D), F32, kind="ExternalOutput").ap()
    hybrid_block(nc, *args, out)
    result = run_bass_kernel_spmd(nc, [arrays], core_ids=[0])
    return result.results[0]["out"].reshape(1, SEQ, D)
```

```python
from contextlib import ExitStack

import concourse.bass as bass
from concourse import mybir

F32 = mybir.dt.float32
I32 = mybir.dt.int32
U32 = mybir.dt.uint32
ALU = mybir.AluOpType
ACT = mybir.ActivationFunctionType
AX = mybir.AxisListType

P = 128
SEQ = 512
D = 1024
KD = D // P
NB = SEQ // P
EPS = 1e-6
GN_EPS = 64e-5
HG_HEADS = 4
RW_HEADS = 8
PAIRS = RW_HEADS // 2
RH = 64
LEVELS = [64, 32, 16, 8, 4, 2, 1]
STRIP = 256
RING = 3
PK_HEADS = 8
N_KEYS = 128
TOPK = 16
PLE = 256
CAND = [TOPK // (i + 1) for i in range(TOPK)]
N_CAND = sum(CAND)
EXP_HALF = 0.6065306597126334
LOWEST = -3.0e38
N_CONSTANTS = 9 + 6 * len(LEVELS)
SLOT = 512
X2_AT = [3, 0, 1, 2]

COLS = {}
_at = 0
for _name, _n in [("norm_mix", 8), ("mu", 14), ("w0", 4), ("a0", 4), ("k_k", 4), ("k_a", 4), ("r_k", 4),
                  ("ln_w", 4), ("ln_b", 4), ("lb0", 4), ("lb1", 4), ("hg_norm", 4), ("norm_ple", 8)]:
    COLS[_name] = (_at, _n)
    _at += _n
N_COLS = _at

RW_STRIPS = [14, 10, 11, 8, 9, 12, 13]
FEATURE_STRIPS = RW_STRIPS + [0, 1, 2, 3, 6, 7]
TOKEN_STRIPS = [4, 5]
GATE_STRIPS = list(range(15, 23))


class Link:

    def __init__(self, eng, sem):
        self.eng, self.sem, self.n = eng, sem, 0

    def __call__(self, ins):
        ins.then_inc(self.sem, 1)
        self.n += 1
        self.eng.wait_ge(self.sem, self.n)

    def restart(self):
        self.eng.sem_clear(self.sem)
        self.n = 0


class Core:

    def __init__(self, nc, ctx):
        self.nc, self.phase_sems = nc, []
        self.const = ctx.enter_context(nc.sbuf_tensor("const", [P, 3072], F32))
        self.arena = ctx.enter_context(nc.sbuf_tensor("arena", [P, 97 * SLOT], F32))
        self.bank = [ctx.enter_context(nc.psum_tensor(f"bank{i}", [P, 512], F32)) for i in range(8)]
        at = 0

        def const(n):
            nonlocal at
            at += n
            return self.const[:, at - n:at]

        self.ident = const(P)
        self.ones_pair = const(P)
        self.ones_full = const(P)
        self.mask_t = const(len(LEVELS) * P).rearrange("p (l t) -> p l t", t=P)
        self.mask_n = const(len(LEVELS) * P).rearrange("p (l t) -> p l t", t=P)
        self.causal = const(2 * P).rearrange("p (a t) -> p a t", a=2)
        self.masks = self.const[:, 0:at]
        self.cols = const(N_COLS)
        self.lb = const(4)
        self.one_minus_lb = const(4)
        self.one_minus_ka = const(4)
        self.iota_cand = const(N_CAND)
        self.stats = const(64)
        self.zero_col = const(1)

    def sem(self, name):
        self.phase_sems.append(self.nc.alloc_semaphore(name=name))
        return self.phase_sems[-1]

    def end_phase(self):
        self.nc.clear_and_free_semaphores(self.phase_sems)
        self.phase_sems = []
        self.nc.all_engine_barrier()

    def col(self, name, i):
        at, _ = COLS[name]
        return self.cols[:, at + i:at + i + 1]

    def slots(self, at, n, inner=SLOT):
        return self.arena[:, at * SLOT:(at + n) * SLOT].rearrange("p (a b) -> p a b", b=inner)


def mixer_inputs(core):
    return {
        "h_t": core.slots(0, 8), "r": core.slots(8, 4), "k": core.slots(12, 4), "v": core.slots(16, 4),
        "ld": core.slots(20, 4), "hq": core.slots(24, 4), "hgo": core.slots(28, 4), "sgd": core.slots(32, 1)[:, 0, :],
        "kk": core.slots(33, 4), "nb": core.slots(37, 4), "cum": core.slots(41, 4), "hk": core.slots(45, 4),
        "hcum": core.slots(49, 4), "vh": core.slots(53, 4),
    }


def make_constants(core, gp, made):
    n = 0

    def did(ins):
        nonlocal n
        n += 1
        ins.then_inc(made, 1)
        gp.wait_ge(made, n)

    did(gp.memset(core.masks, 0.0))
    did(gp.affine_select(out=core.ident, in_=core.ident, pattern=[[-1, P]], compare_op=ALU.not_equal, fill=1.0,
                         base=0, channel_multiplier=1))
    did(gp.memset(core.ones_pair[0:RH, 0:RH], 1.0))
    did(gp.memset(core.ones_pair[RH:P, RH:P], 1.0))
    did(gp.memset(core.ones_full, 1.0))
    did(gp.memset(core.causal, 1.0))
    did(gp.affine_select(out=core.causal[:, 0, :], in_=core.causal[:, 0, :], pattern=[[1, P]], compare_op=ALU.is_gt,
                         fill=0.0, base=0, channel_multiplier=-1))
    did(gp.affine_select(out=core.causal[:, 1, :], in_=core.causal[:, 1, :], pattern=[[1, P]], compare_op=ALU.is_ge,
                         fill=0.0, base=0, channel_multiplier=-1))
    for level, n_ in enumerate(LEVELS):
        blocks = P // (2 * n_)
        for mask, half, lo in ((core.mask_t, 1, 0), (core.mask_n, 0, n_)):
            view = mask[:, level, :].rearrange("p (b two n) -> p b two n", two=2, n=n_)[:, :, half, :]
            did(gp.memset(view, 1.0))
            did(gp.affine_select(out=view, in_=view, pattern=[[-2 * n_, blocks], [0, n_]], compare_op=ALU.is_ge,
                                 fill=0.0, base=-lo, channel_multiplier=1))
            did(gp.affine_select(out=view, in_=view, pattern=[[2 * n_, blocks], [0, n_]], compare_op=ALU.is_ge,
                                 fill=0.0, base=lo + n_ - 1, channel_multiplier=-1))
    did(gp.iota(core.iota_cand, pattern=[[1, N_CAND]], base=0, channel_multiplier=0,
                allow_small_or_imprecise_dtypes=True))
    assert n == N_CONSTANTS


def project(core, x, w_in_strips, params, w2, a2, g2):
    nc = core.nc
    m = mixer_inputs(core)
    bank = core.bank
    ring = [core.slots(57 + 4 * i, 4, STRIP) for i in range(RING)]
    xs = core.slots(8, 8, D)
    x_in = core.slots(16, 8, D)
    raw = [core.arena[:, (69 * SLOT + i * 520):(69 * SLOT + i * 520 + 513)] for i in range(2)]
    diff = core.slots(72, 2)
    low = core.slots(74, 1)[:, 0, :]
    gd = core.slots(75, 1)[:, 0, :]
    w2a2 = core.slots(76, 1)[:, 0, :]
    chunk_ones = core.slots(78, 1)[:, 0, :]
    sig = core.slots(79, 2)
    sq = core.slots(81, 4)
    ln_f = core.slots(85, 4)
    ka = core.slots(89, 2)
    junk = core.slots(91, 2, D)[:, 0, :]
    ssq, mean, root, rstd = (core.stats[:, 4 * i:4 * i + 4] for i in range(4))
    lb_t = core.stats[:, 16:32].rearrange("p (a b) -> p a b", b=4)

    loaded_x = core.sem("x_loaded")
    loaded_p = core.sem("params_loaded")
    strip_loaded = [core.sem(f"strip_loaded{i}") for i in range(RING)]
    constants = core.sem("constants_made")
    squares = core.sem("squares_summed")
    rooted = core.sem("mean_squares_rooted")
    ms_ready = core.sem("mean_squares_ready")
    scaled = core.sem("x_scaled")
    turned = core.sem("x_turned")
    h_ready = core.sem("h_ready")
    cols_ready = core.sem("columns_ready")
    cols_taken = core.sem("columns_taken")
    mixed = core.sem("shifts_mixed")
    low_ready = core.sem("low_rank_ready")
    lora_done = core.sem("lora_done")
    lora_taken = core.sem("lora_taken")
    sig_used = core.sem("lora_sigmoid_used")
    kk_raw = core.sem("kk_raw_ready")
    kk_sq = core.sem("kk_squared")
    norm_done = core.sem("kk_norm_summed")
    norm_rooted = core.sem("kk_norm_rooted")
    hg_taken = core.sem("hgrn_tiles_taken")
    hg_used = core.sem("hgrn_tiles_used")
    f_ready = core.sem("f_ready")
    ln_ready = core.sem("log_f_ready")
    lb_diff = core.sem("lb_differences")
    lb_exp = core.sem("lb_exponentials")
    v_link = core.sem("project_vector_link")
    a_link = core.sem("project_scalar_link")

    n_rw = 2 * len(RW_STRIPS)
    n_feature = 2 * len(FEATURE_STRIPS)
    rw_tiles = [(low, 12), (gd, 13)]
    for name, first in (("k", 4), ("r", 0), ("v", 8)):
        rw_tiles += [(m[name][:, j, :], first + j) for j in range(4)]

    with nc.Block() as block:
        @block.sync
        def _(sp):
            for b in range(NB):
                sp.dma_start(x_in[:, b, :], x[b * P:(b + 1) * P, :]).then_inc(loaded_x, 16)
            for n, strip in enumerate(FEATURE_STRIPS + TOKEN_STRIPS):
                if n >= RING:
                    sp.wait_ge(cols_ready, 2 * (n - RING) + 2)
                sp.dma_start(ring[n % RING], w_in_strips[strip]).then_inc(strip_loaded[n % RING], 16)

        @block.gpsimd
        def _(gp):
            gp.dma_start(core.cols, params).then_inc(loaded_p, 16)
            gp.dma_start(w2a2[0:RH, :], w2).then_inc(loaded_p, 16)
            gp.dma_start(w2a2[RH:P, :], a2).then_inc(loaded_p, 16)
            make_constants(core, gp, constants)

        @block.tensor
        def _(pe):
            pe.wait_ge(constants, N_CONSTANTS)
            for dk in range(KD):
                for b in range(NB):
                    pe.wait_ge(scaled, b + 1)
                    if dk >= 2 and b == 0:
                        pe.wait_ge(h_ready, dk - 1)
                    ins = pe.transpose(bank[6 + dk % 2][:, b * P:(b + 1) * P], xs[:, b, dk * P:(dk + 1) * P], core.ident)
                ins.then_inc(turned, 1)
            pe.wait_ge(h_ready, KD)

            def strips(i, count):
                for s in range(count):
                    pe.wait_ge(strip_loaded[s], 16 * (i + 1))
                    for half in range(2):
                        tile = 2 * s + half
                        if not (isinstance(i, int) and i == 0):
                            pe.wait_ge(cols_taken, 6 * i + tile - 5)
                        for k in range(KD):
                            ins = pe.matmul(bank[tile][:], ring[s][:, k, half * P:(half + 1) * P], m["h_t"][:, k, :],
                                            start=(k == 0), stop=(k == KD - 1))
                        ins.then_inc(cols_ready, 1)

            strips(0, RING)
            pe.wait_ge(low_ready, 1)
            pe.wait_ge(mixed, 1)
            for j in range(PAIRS):
                for half in range(2):
                    if j:
                        pe.wait_ge(lora_taken, 2 * (j - 1) + half + 1)
                    rows = slice(RH * half, RH * (half + 1))
                    pe.matmul(bank[6 + half][:], w2a2[rows, j * P:(j + 1) * P], low[rows, :], start=True,
                              stop=True).then_inc(lora_done, 1)
            with pe.Fori(1, len(FEATURE_STRIPS) // RING) as i:
                strips(i, RING)
            pe.wait_ge(lora_taken, 2 * PAIRS)
            for j in range(PAIRS):
                pe.wait_ge(kk_sq, j + 1)
                if j >= 2:
                    pe.wait_ge(norm_rooted, j - 1)
                pe.matmul(bank[6 + j % 2][:], core.ones_pair, sq[:, j, :], start=True, stop=True).then_inc(norm_done, 1)
            strips(len(FEATURE_STRIPS) // RING, 1)
            t = n_feature
            for n in range(len(FEATURE_STRIPS), len(FEATURE_STRIPS) + len(TOKEN_STRIPS)):
                pe.wait_ge(strip_loaded[n % RING], 16 * (n // RING + 1))
                for b in range(NB):
                    pe.wait_ge(cols_taken, t - 5)
                    for k in range(KD):
                        ins = pe.matmul(bank[t % 6][:, 0:STRIP], m["h_t"][:, k, b * P:(b + 1) * P], ring[n % RING][:, k, :],
                                        start=(k == 0), stop=(k == KD - 1))
                    ins.then_inc(cols_ready, 1)
                    t += 1

        @block.scalar
        def _(act):
            for b in range(NB):
                act.wait_ge(loaded_x, 16 * NB)
                act.activation(junk, x_in[:, b, :], ACT.Square, accum_out=ssq[:, b:b + 1]).then_inc(squares, 1)
                act.wait_ge(squares, b + 1)
            act.wait_ge(ms_ready, 1)
            act.activation(root, mean, ACT.Sqrt).then_inc(rooted, 1)
            act.wait_ge(lb_diff, 1)
            act.activation(lb_t[:, 2, :], lb_t[:, 0, :], ACT.Exp)
            act.activation(lb_t[:, 3, :], lb_t[:, 1, :], ACT.Exp).then_inc(lb_exp, 1)
            act.wait_ge(loaded_p, 48)
            for dk in range(KD):
                act.wait_ge(turned, dk + 1)
                act.activation(m["h_t"][:, dk, :], bank[6 + dk % 2][:], ACT.Copy,
                               scale=core.col("norm_mix", dk)).then_inc(h_ready, 1)

            def take_rw(t):
                act.wait_ge(cols_ready, t + 1)
                if t >= 2:
                    act.wait_ge(mixed, t - 1)
                act.activation(raw[t % 2][:, 1:SEQ + 1], bank[t % 6][:], ACT.Copy).then_inc(cols_taken, 1)

            def square_kk(j):
                act.wait_ge(kk_raw, j + 1)
                act.activation(sq[:, j, :], m["kk"][:, j, :], ACT.Square).then_inc(kk_sq, 1)

            take_rw(0)
            take_rw(1)
            act.wait_ge(mixed, 1)
            act.activation(low[0:RH, :], low[0:RH, :], ACT.Tanh).then_inc(low_ready, 1)
            act.wait_ge(mixed, 2)
            act.activation(m["sgd"], gd, ACT.Sigmoid)
            for t in range(2, 6):
                take_rw(t)
            for j in range(PAIRS):
                act.wait_ge(lora_done, 2 * j + 1)
                if j >= 2:
                    act.wait_ge(sig_used, j - 1)
                act.activation(sig[:, j % 2, :], bank[6][:], ACT.Sigmoid, bias=core.col("w0", j)).then_inc(lora_taken, 1)
                act.wait_ge(lora_done, 2 * j + 2)
                act.activation(m["nb"][:, j, :], bank[7][:], ACT.Sigmoid, bias=core.col("a0", j)).then_inc(lora_taken, 1)
            for t in range(6, n_rw):
                take_rw(t)
                if t < 6 + PAIRS:
                    square_kk(t - 6)
            for j in range(12):
                t = n_rw + j
                if j == 10:
                    for i in range(PAIRS):
                        act.wait_ge(norm_done, i + 1)
                        act.activation(sq[:, i, :], bank[6 + i % 2][:], ACT.Sqrt).then_inc(norm_rooted, 1)
                act.wait_ge(cols_ready, t + 1)
                if j >= 2:
                    act.wait_ge(hg_used, j - 1)
                else:
                    act.wait_ge(sig_used, PAIRS)
                ins = act.activation(sig[:, j % 2, :], bank[t % 6][:], ACT.Sigmoid)
                if not 4 <= j < 8:
                    dest = m["hq"][:, j, :] if j < 4 else m["hgo"][:, j - 8, :]
                    ins = act.activation(dest, bank[t % 6][:], ACT.Copy)
                ins.then_inc(cols_taken, 1)
            for t in range(n_feature, n_feature + 2 * NB):
                act.wait_ge(cols_ready, t + 1)
                s, b = divmod(t - n_feature, NB)
                act.activation(m["vh"][:, b, s * STRIP:(s + 1) * STRIP], bank[t % 6][:, 0:STRIP],
                               ACT.Copy).then_inc(cols_taken, 1)
            act.wait_ge(f_ready, 4)
            act.activation(ln_f, m["hcum"], ACT.Ln).then_inc(ln_ready, 1)

        @block.vector
        def _(v):
            link = Link(v, v_link)
            for i in range(2):
                v.memset(raw[i][:, 0:1], 0.0)
            link(v.memset(chunk_ones, 1.0))
            link(v.memset(chunk_ones.rearrange("p (c t) -> p c t", t=P)[:, :, 0:1], 0.0))
            v.wait_ge(squares, NB)
            v.tensor_scalar(mean, ssq, 1.0 / D, EPS, ALU.mult, ALU.add).then_inc(ms_ready, 1)
            v.wait_ge(rooted, 1)
            link(v.reciprocal(rstd, root))
            for b in range(NB):
                v.tensor_scalar(xs[:, b, :], x_in[:, b, :], rstd[:, b:b + 1], None, ALU.mult).then_inc(scaled, 1)
            v.wait_ge(constants, N_CONSTANTS)
            v.wait_ge(loaded_p, 48)
            lb0 = core.cols[:, COLS["lb0"][0]:COLS["lb0"][0] + 4]
            lb1 = core.cols[:, COLS["lb1"][0]:COLS["lb1"][0] + 4]
            top = core.stats[:, 32:36]
            link(v.tensor_tensor(top, lb0, lb1, ALU.max))
            v.tensor_tensor(lb_t[:, 0, :], lb0, top, ALU.subtract)
            v.tensor_tensor(lb_t[:, 1, :], lb1, top, ALU.subtract).then_inc(lb_diff, 1)
            v.wait_ge(lb_exp, 1)
            link(v.tensor_tensor(top, lb_t[:, 2, :], lb_t[:, 3, :], ALU.add))
            link(v.reciprocal(lb_t[:, 0, :], top))
            link(v.tensor_tensor(core.lb, lb_t[:, 2, :], lb_t[:, 0, :], ALU.mult))
            v.tensor_scalar(core.one_minus_lb, core.lb, -1.0, 1.0, ALU.mult, ALU.add)
            at, n = COLS["k_a"]
            link(v.tensor_scalar(core.one_minus_ka, core.cols[:, at:at + n], -1.0, 1.0, ALU.mult, ALU.add))

            def mix_shift(t):
                dest, c = rw_tiles[t]
                v.wait_ge(cols_taken, t + 1)
                link(v.tensor_tensor(diff[:, 0, :], raw[t % 2][:, 0:SEQ], raw[t % 2][:, 1:SEQ + 1], ALU.subtract))
                v.scalar_tensor_tensor(out=dest, in0=diff[:, 0, :], scalar=core.col("mu", c),
                                       in1=raw[t % 2][:, 1:SEQ + 1], op0=ALU.mult, op1=ALU.add).then_inc(mixed, 1)
                v.wait_ge(mixed, t + 1)

            def raw_kk(j):
                v.tensor_scalar(m["kk"][:, j, :], m["k"][:, j, :], core.col("k_k", j), None,
                                ALU.mult).then_inc(kk_raw, 1)

            for t in range(6):
                mix_shift(t)
                if t >= 2:
                    raw_kk(t - 2)
            for j in range(PAIRS):
                v.wait_ge(lora_taken, 2 * j + 1)
                v.tensor_scalar(m["ld"][:, j, :], sig[:, j % 2, :], -EXP_HALF, None, ALU.mult).then_inc(sig_used, 1)
                v.wait_ge(sig_used, j + 1)
                v.tensor_tensor_scan(m["cum"][:, j, :], chunk_ones, m["ld"][:, j, :], 0.0, ALU.mult, ALU.add)
            for t in range(6, n_rw):
                mix_shift(t)
            for j in range(12):
                v.wait_ge(cols_taken, n_rw + j + 1)
                if j < 4:
                    q = m["hq"][:, j, :]
                    v.scalar_tensor_tensor(out=q, in0=q, scalar=float(P) ** -0.5, in1=sig[:, j % 2, :], op0=ALU.mult,
                                           op1=ALU.mult).then_inc(hg_used, 1)
                elif j < 8:
                    h = j - 4
                    v.tensor_scalar(m["hcum"][:, h, :], sig[:, j % 2, :], core.one_minus_lb[:, h:h + 1],
                                    core.lb[:, h:h + 1], ALU.mult, ALU.add).then_inc(hg_used, 1)
                    v.wait_ge(hg_used, j + 1)
                    v.tensor_scalar(m["hk"][:, h, :], m["hcum"][:, h, :], -1.0, 1.0, ALU.mult,
                                    ALU.add).then_inc(f_ready, 1)
                else:
                    g = m["hgo"][:, j - 8, :]
                    v.scalar_tensor_tensor(out=g, in0=g, scalar=core.col("hg_norm", j - 8), in1=sig[:, j % 2, :],
                                           op0=ALU.mult, op1=ALU.mult).then_inc(hg_used, 1)
            for j in range(PAIRS):
                a, k, kk = m["nb"][:, j, :], m["k"][:, j, :], m["kk"][:, j, :]
                v.wait_ge(lora_taken, 2 * j + 2)
                link(v.tensor_scalar(ka[:, 0, :], a, core.col("k_a", j), core.one_minus_ka[:, j:j + 1], ALU.mult, ALU.add))
                v.tensor_tensor(k, k, ka[:, 0, :], ALU.mult)
                v.wait_ge(norm_rooted, j + 1)
                link(v.tensor_scalar(sq[:, j, :], sq[:, j, :], 1e-12, None, ALU.max))
                link(v.reciprocal(ka[:, 1, :], sq[:, j, :]))
                link(v.tensor_tensor(kk, kk, ka[:, 1, :], ALU.mult))
                link(v.scalar_tensor_tensor(out=a, in0=kk, scalar=-1.0, in1=a, op0=ALU.mult, op1=ALU.mult))
            v.wait_ge(ln_ready, 1)
            for h in range(HG_HEADS):
                ins = v.tensor_tensor_scan(m["hcum"][:, h, :], chunk_ones, ln_f[:, h, :], 0.0, ALU.mult, ALU.add)
            link(ins)


def mix(core):
    nc = core.nc
    m = mixer_inputs(core)
    bank = core.bank

    def tile(at, n=1, inner=P):
        return core.slots(at, n, inner)

    scores = core.slots(57, 8, P).rearrange("p (h a) t -> p h a t", a=4)
    x_t, x_n = tile(65, 2), tile(67, 2)
    y_sb = core.slots(69, 2).rearrange("p b (h t) -> p b h t", t=P)
    level_e = core.slots(71, 2).rearrange("p b (h t) -> p b h t", t=P)
    level_g = core.slots(73, 2).rearrange("p b (h t) -> p b h t", t=P)
    att_t, q_e, k_e, k_tok_h, state_h, v_h = (tile(s) for s in (75, 76, 77, 78, 79, 80))
    e1, e2, e3 = tile(81), tile(82), tile(83)
    kr = core.slots(84, 2, P).rearrange("p (j a) t -> p j a t", a=2)
    k_s, b_s, k_tok, b_tok, v_tok, v_stage = (tile(s) for s in (86, 87, 88, 89, 90, 91))
    state = core.slots(92, 1, RH)[:, 0:PAIRS, :]
    state_0 = core.slots(92, 1, RH)[:, PAIRS:2 * PAIRS, :]
    rhs = core.slots(93, 1, RH)
    u = core.slots(94, 1, RH)
    e_inter, k_stage = tile(95), tile(96)
    exp_mid = core.stats[:, 0:4]

    per = dict(staged=2, rw_diff=1, rw_exp=1, rw_scaled=1, tok_ready=4, tok_taken=4, scores_ready=PAIRS,
               scores_taken=PAIRS, xt_first=2, x_first=2, x_first_taken=2, hg_diff=len(LEVELS), hg_exp=len(LEVELS),
               hg_scaled=len(LEVELS), hg_scores=len(LEVELS) + 1, hg_att=len(LEVELS) + 1, inter_diff=1, inter_exp=1,
               inter_scaled=1, rhs_ready=1, rhs_taken=1, u_ready=1, u_taken=1, out_ready=1, hg_out=2, state_ready=1)
    s = {n: core.sem("mix_" + n) for n in per}
    wait_carrier = core.sem("mix_wait_carrier")
    vector_link = core.sem("mix_vector_link")

    def after(name, c, k):
        return c * per[name] + k

    inv_y = [core.sem(f"mix_inverse_y{i}") for i in range(2)]
    inv_y_taken = [core.sem(f"mix_inverse_y_taken{i}") for i in range(2)]
    inv_z = [core.sem(f"mix_inverse_z{i}") for i in range(2)]
    inv_done = [core.sem(f"mix_inverse_updated{i}") for i in range(2)]
    first_state = core.sem("mix_first_state")
    pe_end = core.sem("mix_tensor_chunk_end")
    act_end = core.sem("mix_scalar_chunk_end")
    dve_end = core.sem("mix_vector_chunk_end")

    n_inv = len(LEVELS) - 1
    inv_level = [len(LEVELS) - 2 - i for i in range(n_inv)]
    head_bank = {"y": (2, 5), "z": (3, 6), "zt": (4, 7)}

    def waited(v):
        v.sem_inc(wait_carrier, 1)

    def halves(ap, level):
        return ap.rearrange("p h (b two n) -> p h b two n", two=2, n=LEVELS[level])

    def heads_of(bank_ap):
        return bank_ap[:].rearrange("p (h t) -> p h t", t=P)

    with nc.Block() as block:
        @block.gpsimd
        def _(gp):
            gp.memset(core.slots(57, 8), 0.0)
            gp.memset(core.slots(92, 1), 0.0)
            gp.memset(state_h, 0.0).then_inc(first_state, 1)

        @block.scalar
        def _(act):
            act.wait_ge(first_state, 1)
            with act.Fori(0, NB) as c:
                act.wait_ge(pe_end, c)
                act.wait_ge(dve_end, c)
                act.wait_ge(act_end, c)
                now = bass.ds(c * P, P)
                act.activation(v_stage, m["v"][:, :, now], ACT.Copy).then_inc(s["staged"], 1)
                act.activation(v_h, m["vh"][:, bass.ds(c, 1), :], ACT.Copy)
                act.activation(k_stage, m["hk"][:, :, now], ACT.Copy).then_inc(s["staged"], 1)

                def level_exp(i):
                    act.wait_ge(s["hg_diff"], after("hg_diff", c, i))
                    act.activation(level_e[:, i % 2], level_e[:, i % 2], ACT.Exp).then_inc(s["hg_exp"], 1)

                act.wait_ge(s["rw_diff"], after("rw_diff", c, 1))
                act.activation(e3, e1, ACT.Exp, scale=-1.0)
                act.activation(e2, e2, ACT.Exp)
                act.activation(exp_mid, m["cum"][:, :, bass.ds(c * P + P // 2 - 1, 1)], ACT.Exp)
                act.activation(e1, e1, ACT.Exp).then_inc(s["rw_exp"], 1)
                act.wait_ge(s["tok_ready"], after("tok_ready", c, 1))
                act.activation(v_tok, heads_of(bank[6]), ACT.Copy).then_inc(s["tok_taken"], 1)
                level_exp(1)
                act.activation(e_inter, m["hcum"][:, :, now], ACT.Exp)
                act.wait_ge(s["inter_diff"], after("inter_diff", c, 1))
                act.activation(k_e, k_e, ACT.Exp).then_inc(s["inter_exp"], 1)
                act.wait_ge(s["tok_ready"], after("tok_ready", c, 2))
                act.activation(k_tok, heads_of(bank[7]), ACT.Copy).then_inc(s["tok_taken"], 1)
                act.wait_ge(s["tok_ready"], after("tok_ready", c, 3))
                act.activation(b_tok, heads_of(bank[6]), ACT.Copy).then_inc(s["tok_taken"], 1)
                level_exp(2)
                act.wait_ge(s["tok_ready"], after("tok_ready", c, 4))
                act.activation(k_tok_h, heads_of(bank[7]), ACT.Copy).then_inc(s["tok_taken"], 1)
                for b in range(2):
                    act.wait_ge(s["x_first"], after("x_first", c, b + 1))
                    act.activation(x_n[:, 4 * b:4 * b + 4, :], heads_of(bank[head_bank["z"][b]]),
                                   ACT.Copy).then_inc(s["x_first_taken"], 1)
                for i in range(n_inv):
                    for b in range(2):
                        act.wait_ge(inv_y[b], c * n_inv + i + 1)
                        act.activation(y_sb[:, b], heads_of(bank[head_bank["y"][b]]),
                                       ACT.Copy).then_inc(inv_y_taken[b], 1)
                    if i + 3 <= len(LEVELS):
                        level_exp(i + 3)
                act.wait_ge(s["rhs_ready"], after("rhs_ready", c, 1))
                for e in range(2):
                    ins = act.activation(rhs[:, 4 * e:4 * e + 4, :],
                                         bank[(2, 5)[e]][:, 0:PAIRS * RH].rearrange("p (j v) -> p j v", v=RH), ACT.Copy)
                ins.then_inc(s["rhs_taken"], 1)
                act.wait_ge(s["u_ready"], after("u_ready", c, 1))
                act.activation(u, bank[3][:].rearrange("p (h v) -> p h v", v=RH), ACT.Copy).then_inc(s["u_taken"], 1)
                act.wait_ge(s["hg_out"], after("hg_out", c, 1))
                act.activation(m["hq"][:, :, now], heads_of(bank[0]), ACT.Copy)
                act.wait_ge(s["out_ready"], after("out_ready", c, 1))
                act.activation(m["ld"][:, :, now], heads_of(bank[4]), ACT.Copy).then_inc(act_end, 1)

        @block.vector
        def _(v):
            link = Link(v, vector_link)
            v.wait_ge(first_state, 1)
            with v.Fori(0, NB) as c:
                v.wait_ge(pe_end, c)
                v.wait_ge(act_end, c)
                v.wait_ge(dve_end, c)
                now = bass.ds(c * P, P)
                hcum = m["hcum"][:, :, now]
                full = [P, PAIRS, P]

                def level_diff(i):
                    b, out = halves(hcum, i - 1), halves(level_e[:, i % 2], i - 1)
                    n = LEVELS[i - 1]
                    edge = b[:, :, :, 0, n - 1:n].to_broadcast([P, HG_HEADS, P // (2 * n), n])
                    v.tensor_tensor(out[:, :, :, 0, :], edge, b[:, :, :, 0, :], ALU.subtract)
                    v.tensor_tensor(out[:, :, :, 1, :], b[:, :, :, 1, :], edge, ALU.subtract).then_inc(s["hg_diff"], 1)

                def level_scale(i):
                    v.wait_ge(s["hg_exp"], after("hg_exp", c, i))
                    e, g = halves(level_e[:, i % 2], i - 1), halves(level_g[:, i % 2], i - 1)
                    k, q = halves(m["hk"][:, :, now], i - 1), halves(m["hq"][:, :, now], i - 1)
                    v.tensor_tensor(g[:, :, :, 0, :], e[:, :, :, 0, :], k[:, :, :, 0, :], ALU.mult)
                    v.tensor_tensor(g[:, :, :, 1, :], e[:, :, :, 1, :], q[:, :, :, 1, :],
                                    ALU.mult).then_inc(s["hg_scaled"], 1)

                def level_keep(i):
                    v.wait_ge(s["hg_att"], after("hg_att", c, i))
                    v.wait_ge(s["hg_scores"], after("hg_scores", c, i + 1))
                    waited(v)
                    mask = core.mask_t[:, i - 1:i, :].bitcast(I32).to_broadcast([P, HG_HEADS, P])
                    v.copy_predicated(att_t, mask, heads_of(bank[i % 2])).then_inc(s["hg_att"], 1)

                mid = m["cum"][:, :, bass.ds(c * P + P // 2 - 1, 1)].to_broadcast(full)
                link(v.tensor_tensor(e1, m["cum"][:, :, now], mid, ALU.subtract))
                v.tensor_tensor(e2, e1, m["ld"][:, :, now], ALU.subtract).then_inc(s["rw_diff"], 1)
                level_diff(1)
                last = m["hcum"][:, :, bass.ds(c * P + P - 1, 1)].to_broadcast(full)
                v.tensor_tensor(k_e, last, hcum, ALU.subtract).then_inc(s["inter_diff"], 1)
                level_diff(2)
                v.wait_ge(s["rw_exp"], after("rw_exp", c, 1))
                v.tensor_tensor(state_0, state, exp_mid.unsqueeze(2).to_broadcast([P, PAIRS, RH]), ALU.mult)
                v.tensor_tensor(kr[:, :, 0, :], m["kk"][:, :, now], e2, ALU.mult)
                v.tensor_tensor(kr[:, :, 1, :], m["r"][:, :, now], e1, ALU.mult)
                v.tensor_tensor(k_s, m["k"][:, :, now], e3, ALU.mult)
                v.tensor_tensor(b_s, m["nb"][:, :, now], e3, ALU.mult).then_inc(s["rw_scaled"], 1)
                level_scale(1)
                v.wait_ge(s["inter_exp"], after("inter_exp", c, 1))
                v.tensor_tensor(q_e, m["hq"][:, :, now], e_inter, ALU.mult)
                v.tensor_tensor(k_e, k_e, m["hk"][:, :, now], ALU.mult).then_inc(s["inter_scaled"], 1)
                for j in range(PAIRS):
                    v.wait_ge(s["scores_ready"], after("scores_ready", c, j + 1))
                    waited(v)
                    mask = core.causal.rearrange("p a t -> p (a t)").bitcast(I32).unsqueeze(1).to_broadcast([P, 2, 2 * P])
                    for e in range(2):
                        ins = v.copy_predicated(scores[:, 2 * j + e].rearrange("p (b a) t -> p b (a t)", b=2), mask,
                                                bank[2 + 2 * (j % 2) + e][:].rearrange("p (b a) -> p b a", b=2))
                    ins.then_inc(s["scores_taken"], 1)
                    if j == 0:
                        v.wait_ge(s["hg_scores"], after("hg_scores", c, 1))
                        v.tensor_tensor(att_t, heads_of(bank[0]), core.ident.unsqueeze(1).to_broadcast([P, HG_HEADS, P]),
                                        ALU.mult).then_inc(s["hg_att"], 1)
                    if j % 2 == 1:
                        heads = slice(2 * (j - 1), 2 * (j + 1))
                        v.wait_ge(s["scores_taken"], after("scores_taken", c, j + 1))
                        mask1 = core.mask_t[:, len(LEVELS) - 1:len(LEVELS), :].to_broadcast([P, 4, P])
                        link(v.tensor_tensor(x_t[:, heads, :], scores[:, heads, 0, :], mask1, ALU.mult))
                        v.tensor_tensor(x_t[:, heads, :], x_t[:, heads, :],
                                        core.ident.unsqueeze(1).to_broadcast([P, 4, P]), ALU.add).then_inc(s["xt_first"], 1)
                for i in range(n_inv):
                    if i + 2 <= len(LEVELS):
                        level_scale(i + 2)
                    if i + 3 <= len(LEVELS):
                        level_diff(i + 3)
                    level_keep(i + 1)
                    lv = inv_level[i]
                    for b in range(2):
                        heads = slice(4 * b, 4 * b + 4)
                        v.wait_ge(inv_z[b], c * n_inv + i + 1)
                        waited(v)
                        if i < n_inv - 1:
                            v.copy_predicated(x_n[:, heads, :], core.mask_n[:, lv:lv + 1, :].bitcast(I32).to_broadcast([P, 4, P]),
                                              heads_of(bank[head_bank["z"][b]]))
                        v.copy_predicated(x_t[:, heads, :], core.mask_t[:, lv:lv + 1, :].bitcast(I32).to_broadcast([P, 4, P]),
                                          heads_of(bank[head_bank["zt"][b]])).then_inc(inv_done[b], 1)
                level_keep(len(LEVELS))
                v.wait_ge(s["hg_out"], after("hg_out", c, 2))
                for h in range(HG_HEADS):
                    v.scalar_tensor_tensor(out=state_h[:, h, :], in0=state_h[:, h, :], scalar=e_inter[:, h, P - 1:P],
                                           in1=heads_of(bank[1])[:, h, :], op0=ALU.mult, op1=ALU.add)
                v.wait_ge(s["state_ready"], after("state_ready", c, 1))
                link(v.tensor_tensor(state, state_0, bank[6][:, 0:PAIRS * RH].rearrange("p (j v) -> p j v", v=RH), ALU.add))
                v.tensor_tensor(state, state, e1[:, :, P - 1:P].to_broadcast([P, PAIRS, RH]), ALU.mult).then_inc(dve_end, 1)
                link.restart()

        @block.tensor
        def _(pe):
            pe.wait_ge(first_state, 1)
            with pe.Fori(0, NB) as c:
                pe.wait_ge(act_end, c)
                pe.wait_ge(dve_end, c)
                pe.wait_ge(pe_end, c)
                now = bass.ds(c * P, P)

                def turn(src, to):
                    for j in range(4):
                        ins = pe.transpose(bank[to][:, j * P:(j + 1) * P], src[:, j, :], core.ident)
                    ins.then_inc(s["tok_ready"], 1)

                def level_scores(i):
                    pe.wait_ge(s["hg_scaled"], after("hg_scaled", c, i))
                    if i >= 2:
                        pe.wait_ge(s["hg_att"], i - 1)
                    for h in range(HG_HEADS):
                        g = level_g[:, i % 2, h, :]
                        ins = pe.matmul(bank[i % 2][:, h * P:(h + 1) * P], g, g, start=True, stop=True)
                    ins.then_inc(s["hg_scores"], 1)

                pe.wait_ge(s["staged"], after("staged", c, 1))
                turn(v_stage, 6)
                pe.wait_ge(s["staged"], after("staged", c, 2))
                for h in range(HG_HEADS):
                    ins = pe.matmul(bank[0][:, h * P:(h + 1) * P], k_stage[:, h, :], m["hq"][:, h, now], start=True, stop=True)
                ins.then_inc(s["hg_scores"], 1)
                pe.wait_ge(s["rw_scaled"], after("rw_scaled", c, 1))
                turn(k_s, 7)
                pe.wait_ge(s["tok_taken"], after("tok_taken", c, 1))
                turn(b_s, 6)
                for j in range(PAIRS):
                    if j >= 2:
                        pe.wait_ge(s["scores_taken"], after("scores_taken", c, j - 1))
                    for e in range(2):
                        rows = slice(RH * e, RH * (e + 1))
                        to = bank[2 + 2 * (j % 2) + e]
                        both = kr[rows, j].rearrange("p a t -> p (a t)")
                        pe.matmul(to[:, 0:2 * P], b_s[rows, j, :], both, start=True, stop=True)
                        ins = pe.matmul(to[:, 2 * P:4 * P], k_s[rows, j, :], both, start=True, stop=True)
                    ins.then_inc(s["scores_ready"], 1)
                pe.wait_ge(s["inter_scaled"], after("inter_scaled", c, 1))
                pe.wait_ge(s["tok_taken"], after("tok_taken", c, 2))
                turn(k_e, 7)
                for b in range(2):
                    pe.wait_ge(s["xt_first"], after("xt_first", c, b + 1))
                    pe.wait_ge(s["scores_taken"], after("scores_taken", c, 3 + b))
                    pe.wait_ge(s["tok_taken"], after("tok_taken", c, 3))
                    for j in range(4):
                        ins = pe.transpose(bank[head_bank["z"][b]][:, j * P:(j + 1) * P], x_t[:, 4 * b + j, :], core.ident)
                    ins.then_inc(s["x_first"], 1)
                pe.wait_ge(s["scores_taken"], after("scores_taken", c, PAIRS))
                pe.wait_ge(s["tok_taken"], after("tok_taken", c, 4))
                for i in range(n_inv):
                    for b in range(2):
                        if i == 0:
                            pe.wait_ge(s["x_first_taken"], after("x_first_taken", c, b + 1))
                        else:
                            pe.wait_ge(inv_done[b], c * n_inv + i)
                        for j in range(4):
                            h = 4 * b + j
                            ins = pe.matmul(bank[head_bank["y"][b]][:, j * P:(j + 1) * P], scores[:, h, 0, :], x_n[:, h, :],
                                            start=True, stop=True)
                        ins.then_inc(inv_y[b], 1)
                    level_scores(i + 1)
                    for b in range(2):
                        pe.wait_ge(inv_y_taken[b], c * n_inv + i + 1)
                        for j in range(4):
                            h = 4 * b + j
                            if i < n_inv - 1:
                                pe.matmul(bank[head_bank["z"][b]][:, j * P:(j + 1) * P], x_t[:, h, :], y_sb[:, b, j, :],
                                          start=True, stop=True)
                            ins = pe.matmul(bank[head_bank["zt"][b]][:, j * P:(j + 1) * P], y_sb[:, b, j, :], x_t[:, h, :],
                                            start=True, stop=True)
                        ins.then_inc(inv_z[b], 1)
                level_scores(len(LEVELS))
                for e in range(2):
                    rows = slice(RH * e, RH * (e + 1))
                    for j in range(PAIRS):
                        h = 2 * j + e
                        to = bank[(2, 5)[e]][:, j * RH:(j + 1) * RH]
                        pe.matmul(to, kr[rows, j, 0, :], state_0[rows, j, :], start=True, stop=False)
                        ins = pe.matmul(to, scores[:, h, 2, :], v_tok.rearrange("p j v -> p (j v)")[:, h * RH:(h + 1) * RH],
                                        start=False, stop=True)
                ins.then_inc(s["rhs_ready"], 1)
                pe.wait_ge(s["hg_att"], after("hg_att", c, len(LEVELS) + 1))
                for h in range(HG_HEADS):
                    to = bank[0][:, h * P:(h + 1) * P]
                    pe.matmul(to, v_h[:, h, :], att_t[:, h, :], start=True, stop=False)
                    ins = pe.matmul(to, state_h[:, h, :], q_e[:, h, :], start=False, stop=True)
                ins.then_inc(s["hg_out"], 1)
                for h in range(HG_HEADS):
                    ins = pe.matmul(bank[1][:, h * P:(h + 1) * P], k_tok_h[:, h, :], v_h[:, h, :], start=True, stop=True)
                ins.then_inc(s["hg_out"], 1)
                pe.wait_ge(s["rhs_taken"], after("rhs_taken", c, 1))
                pe.wait_ge(inv_done[0], c * n_inv + n_inv)
                pe.wait_ge(inv_done[1], c * n_inv + n_inv)
                for h in range(RW_HEADS):
                    ins = pe.matmul(bank[3][:, h * RH:(h + 1) * RH], x_t[:, h, :], rhs[:, PAIRS * (h % 2) + h // 2, :],
                                    start=True, stop=True)
                ins.then_inc(s["u_ready"], 1)
                pe.wait_ge(s["u_taken"], after("u_taken", c, 1))
                v_heads = v_tok.rearrange("p j v -> p (j v)")
                for e in range(2):
                    rows = slice(RH * e, RH * (e + 1))
                    for j in range(PAIRS):
                        h = 2 * j + e
                        to = bank[4][rows, j * P:(j + 1) * P]
                        pe.matmul(to, v_heads[:, h * RH:(h + 1) * RH], scores[:, h, 3, :], start=True, stop=False)
                        pe.matmul(to, u[:, h, :], scores[:, h, 1, :], start=False, stop=False)
                        ins = pe.matmul(to, state_0[rows, j, :], kr[rows, j, 1, :], start=False, stop=True)
                ins.then_inc(s["out_ready"], 1)
                for e in range(2):
                    rows = slice(RH * e, RH * (e + 1))
                    for j in range(PAIRS):
                        h = 2 * j + e
                        to = bank[6][rows, j * RH:(j + 1) * RH]
                        pe.matmul(to, k_tok[:, j, rows], v_heads[:, h * RH:(h + 1) * RH], start=True, stop=False)
                        ins = pe.matmul(to, b_tok[:, j, rows], u[:, h, :], start=False, stop=True)
                ins.then_inc(s["state_ready"], 1)
                pe.nop().then_inc(pe_end, 1)


def finish(core, x, w_in_strips, g2, w_branch_hg, w_branch_rw, w_out, norm_ffn, wq):
    nc = core.nc
    m = mixer_inputs(core)
    bank = core.bank
    gates_0 = core.slots(51, 4, P)
    gates_rest = core.slots(35, 12, SEQ - P)
    ring = [core.slots(57 + 4 * i, 4, STRIP) for i in range(2)]
    yc, y_sq, y_root, y_inv, rk, out, o_sq, o_root, g2_all, g2_now = (core.slots(s, 1)[:, 0, :] for s in range(65, 75))
    g2_now = g2_now[:, 0:P]
    w_branch = [core.slots(75 + 4 * i, 4, STRIP) for i in range(4)]
    norm_row = core.slots(95, 2, D)[:, 0, :]
    merged = core.slots(55, 2, P)
    w_out_sb = core.slots(57, 16, D)
    x2 = core.slots(41, 8, D)[:, X2_AT[0], :]
    wq_sb = core.slots(0, 16, D)
    h_tok, h_t, q_t = core.slots(33, 2, D)[:, 0, :], core.slots(28, 2, P), core.slots(49, 8)[:, :, 0:P]
    junk = core.slots(73, 2, D)[:, 0, :]
    ssq, mean, root, rstd = (core.stats[:, i:i + 1] for i in range(4))

    strip_loaded = [core.sem(f"gate_strip_loaded{i}") for i in range(2)]
    g2_loaded = core.sem("g2_loaded")
    weights = core.sem("branch_weights_loaded")
    w_out_loaded = core.sem("w_out_loaded")
    x_loaded = core.sem("x_reloaded")
    wq_loaded = core.sem("wq_loaded")
    y_mean = core.sem("y_mean_summed")
    centred = core.sem("y_centred")
    y_squared = core.sem("y_squared")
    y_var = core.sem("y_variance_summed")
    rooting = core.sem("variances_ready")
    rooted = core.sem("variances_rooted")
    o_squared = core.sem("o_squared")
    o_sum = core.sem("o_squares_summed")
    rk_ready = core.sem("rk_ready")
    rk_sum = core.sem("rk_summed")
    g2_staged = core.sem("g2_staged")
    g_ready = core.sem("g_ready")
    y_done = core.sem("y_done")
    gates_ready = core.sem("gates_ready")
    gates_taken = core.sem("gates_taken")
    branch_ready = core.sem("branch_ready")
    branch_used = core.sem("branch_used")
    merged_ready = core.sem("merged_ready")
    out_ready = core.sem("w_out_summed")
    x2_ready = core.sem("x2_ready")
    squares = core.sem("x2_squares_summed")
    ms_ready = core.sem("x2_mean_squares_ready")
    x2_rooted = core.sem("x2_rooted")
    h_ready = core.sem("ffn_input_ready")
    turned = core.sem("ffn_input_turned")
    turned_taken = core.sem("ffn_input_turned_taken")
    q_ready = core.sem("queries_ready")
    v_link = core.sem("finish_vector_link")

    with nc.Block() as block:
        @block.sync
        def _(sp):
            sp.dma_start(g2_all, g2).then_inc(g2_loaded, 16)
            for n, strip in enumerate(GATE_STRIPS):
                if n >= 2:
                    sp.wait_ge(gates_ready, 2 * (n - 2) + 2)
                sp.dma_start(ring[n % 2], w_in_strips[strip]).then_inc(strip_loaded[n % 2], 16)
                if n == 1:
                    for i in range(4):
                        for which, w in ((0, w_branch_hg), (1, w_branch_rw)):
                            sp.dma_start(w_branch[i][:, 4 * which:4 * which + 4, :],
                                         w.rearrange("(k p) n -> p k n", p=P)[:, :, i * STRIP:(i + 1) * STRIP],
                                         ).then_inc(weights, 16)
                    sp.dma_start(norm_row, norm_ffn.partition_broadcast(P)).then_inc(weights, 16)
            sp.wait_ge(y_done, PAIRS)
            sp.wait_ge(gates_ready, 16)
            sp.dma_start(x2, x[0:P, :]).then_inc(x_loaded, 16)
            sp.dma_start(w_out_sb, w_out.rearrange("(k p) n -> p k n", p=P)).then_inc(w_out_loaded, 16)
            sp.dma_start(wq_sb, wq.rearrange("(k p) n -> p k n", p=P)).then_inc(wq_loaded, 16)

        @block.tensor
        def _(pe):
            pe.wait_ge(g2_loaded, 16)
            with pe.Fori(0, PAIRS) as j:
                one = bass.ds(j, 1)

                def strip(half):
                    pe.wait_ge(strip_loaded[half], 16 * (j + 1))
                    for t in range(2):
                        b = 2 * half + t
                        pe.wait_ge(gates_taken, 4 * j + b - 3 + 4)
                        for k in range(KD):
                            ins = pe.matmul(bank[b][:], ring[half][:, k, t * P:(t + 1) * P], m["h_t"][:, k, :],
                                            start=(k == 0), stop=(k == KD - 1))
                        ins.then_inc(gates_ready, 1)

                pe.wait_ge(y_done, j)
                pe.matmul(bank[4][:], core.ones_pair, m["ld"][:, one, :], start=True, stop=True).then_inc(y_mean, 1)
                pe.wait_ge(rk_ready, j + 1)
                pe.matmul(bank[5][:], core.ones_pair, rk, start=True, stop=True).then_inc(rk_sum, 1)
                pe.wait_ge(g2_staged, j + 1)
                pe.matmul(bank[6][:], g2_now, m["sgd"], start=True, stop=True).then_inc(g_ready, 1)
                pe.wait_ge(o_squared, j + 1)
                pe.matmul(bank[7][:], core.ones_full, o_sq, start=True, stop=True).then_inc(o_sum, 1)
                strip(0)
                pe.wait_ge(y_squared, j + 1)
                pe.matmul(bank[4][:], core.ones_pair, y_sq, start=True, stop=True).then_inc(y_var, 1)
                strip(1)
            pe.wait_ge(weights, 144)
            pe.wait_ge(y_done, PAIRS)
            pe.wait_ge(gates_taken, 4 * PAIRS + 4)
            for t in range(KD):
                if t >= 2:
                    pe.wait_ge(branch_used, 2 * (t - 1))
                for which, y in ((0, m["hq"]), (1, m["ld"])):
                    for k in range(4):
                        ins = pe.matmul(bank[2 * (t % 2) + which][:, 0:P],
                                        w_branch[t // 2][:, 4 * which + k, (t % 2) * P:(t % 2 + 1) * P], y[:, k, 0:P],
                                        start=(k == 0), stop=(k == 3))
                    ins.then_inc(branch_ready, 1)
            pe.wait_ge(w_out_loaded, 16)
            for half in range(2):
                for k in range(KD):
                    pe.wait_ge(merged_ready, k + 1)
                    ins = pe.matmul(bank[4 + half][:], merged[:, k, :], w_out_sb[:, k, half * 512:(half + 1) * 512],
                                    start=(k == 0), stop=(k == KD - 1))
                ins.then_inc(out_ready, 1)
            pe.wait_ge(h_ready, 1)
            for half in range(2):
                for k in range(4):
                    dk = 4 * half + k
                    ins = pe.transpose(bank[6 + half][:, k * P:(k + 1) * P], h_tok[:, dk * P:(dk + 1) * P], core.ident)
                ins.then_inc(turned, 1)
            pe.wait_ge(wq_loaded, 16)
            for h in range(PK_HEADS):
                if h == 0:
                    pe.wait_ge(branch_used, 16)
                if h >= 2:
                    pe.wait_ge(turned_taken, h + 1)
                for k in range(KD):
                    if h == 0 and k % 4 == 0:
                        pe.wait_ge(turned_taken, 1 + k // 4)
                    ins = pe.matmul(bank[h % 2][:, 0:P], wq_sb[:, k, h * P:(h + 1) * P], h_t[:, k, :], start=(k == 0),
                                    stop=(k == KD - 1))
                ins.then_inc(q_ready, 1)

        @block.scalar
        def _(act):
            act.wait_ge(g2_loaded, 16)
            act.nop().then_inc(gates_taken, 4)
            with act.Fori(0, PAIRS) as j:
                one = bass.ds(j, 1)
                act.wait_ge(g_ready, j)
                act.activation(g2_now, g2_all[:, bass.ds(j * P, P)], ACT.Copy).then_inc(g2_staged, 1)
                act.wait_ge(o_sum, j)
                act.activation(o_sq, m["hq"][:, one, :], ACT.Square).then_inc(o_squared, 1)
                act.wait_ge(centred, j + 1)
                act.wait_ge(y_var, j)
                act.activation(y_sq, yc, ACT.Square).then_inc(y_squared, 1)

                def gate(b):
                    act.wait_ge(gates_ready, 4 * j + b + 1)
                    act.activation(gates_0[:, bass.ds(4 * j + b, 1), :], bank[b][:, 0:P], ACT.Sigmoid)
                    act.activation(gates_rest[:, bass.ds(4 * j + b, 1), :], bank[b][:, P:], ACT.Sigmoid).then_inc(gates_taken, 1)

                for b in range(4):
                    gate(b)
                act.wait_ge(rooting, 2 * j + 2)
                act.activation(y_root, y_root, ACT.Sqrt)
                act.activation(o_root, o_root, ACT.Sqrt).then_inc(rooted, 1)
            act.wait_ge(x2_ready, 2)
            act.activation(junk, x2, ACT.Square, accum_out=ssq).then_inc(squares, 1)
            act.wait_ge(ms_ready, 1)
            act.activation(root, mean, ACT.Sqrt).then_inc(x2_rooted, 1)
            for half in range(2):
                act.wait_ge(turned, half + 1)
                act.activation(h_t[:, 4 * half:4 * half + 4, :], bank[6 + half][:].rearrange("p (k t) -> p k t", t=P),
                               ACT.Copy).then_inc(turned_taken, 1)
            for h in range(PK_HEADS):
                act.wait_ge(q_ready, h + 1)
                act.activation(q_t[:, h, :], bank[h % 2][:, 0:P], ACT.Copy).then_inc(turned_taken, 1)

        @block.vector
        def _(v):
            link = Link(v, v_link)
            with v.Fori(0, PAIRS) as j:
                one = bass.ds(j, 1)

                def col(name):
                    return core.cols[:, bass.ds(j + COLS[name][0], 1)]

                y, o = m["ld"][:, one, :], m["hq"][:, one, :]
                link(v.scalar_tensor_tensor(out=rk, in0=m["r"][:, one, :], scalar=col("r_k"), in1=m["k"][:, one, :],
                                            op0=ALU.mult, op1=ALU.mult))
                v.sem_inc(rk_ready, 1)
                v.wait_ge(y_mean, j + 1)
                v.scalar_tensor_tensor(out=yc, in0=bank[4][:], scalar=-1.0 / RH, in1=y, op0=ALU.mult,
                                       op1=ALU.add).then_inc(centred, 1)
                v.wait_ge(o_sum, j + 1)
                v.tensor_scalar(o_root, bank[7][:], 1.0 / P, EPS, ALU.mult, ALU.add).then_inc(rooting, 1)
                v.wait_ge(rk_sum, j + 1)
                link(v.tensor_tensor(rk, bank[5][:], m["v"][:, one, :], ALU.mult))
                v.wait_ge(y_var, j + 1)
                v.tensor_scalar(y_root, bank[4][:], 1.0 / RH, GN_EPS, ALU.mult, ALU.add).then_inc(rooting, 1)
                v.wait_ge(rooted, j + 1)
                link(v.reciprocal(y_inv, y_root))
                link(v.tensor_tensor(yc, yc, y_inv, ALU.mult))
                link(v.tensor_scalar(out, yc, col("ln_w"), col("ln_b"), ALU.mult, ALU.add))
                link(v.tensor_tensor(out, out, rk, ALU.add))
                v.wait_ge(g_ready, j + 1)
                link(v.tensor_tensor(y, out, bank[6][:], ALU.mult))
                link(v.reciprocal(y_inv, o_root))
                link(v.tensor_tensor(o, o, y_inv, ALU.mult))
                link(v.tensor_tensor(o, o, m["hgo"][:, one, :], ALU.mult))
                v.sem_inc(y_done, 1)
                link.restart()
            v.wait_ge(gates_taken, 4 * PAIRS + 4)
            for t in range(KD):
                for which in range(2):
                    gate = gates_0[:, KD * which + t, :]
                    v.wait_ge(branch_ready, 2 * t + which + 1)
                    v.tensor_tensor(gate, bank[2 * (t % 2) + which][:, 0:P], gate, ALU.mult).then_inc(branch_used, 1)
                v.wait_ge(branch_used, 2 * t + 2)
                v.tensor_tensor(merged[:, t, :], gates_0[:, t, :], gates_0[:, KD + t, :], ALU.add).then_inc(merged_ready, 1)
            v.wait_ge(x_loaded, 16)
            for half in range(2):
                v.wait_ge(out_ready, half + 1)
                part = x2[:, half * 512:(half + 1) * 512]
                v.tensor_tensor(part, part, bank[4 + half][:], ALU.add).then_inc(x2_ready, 1)
            v.wait_ge(squares, 1)
            v.tensor_scalar(mean, ssq, 1.0 / D, EPS, ALU.mult, ALU.add).then_inc(ms_ready, 1)
            v.wait_ge(x2_rooted, 1)
            link(v.reciprocal(rstd, root))
            v.wait_ge(weights, 144)
            v.scalar_tensor_tensor(out=h_tok, in0=x2, scalar=rstd, in1=norm_row, op0=ALU.mult,
                                   op1=ALU.mult).then_inc(h_ready, 1)


def experts(core, x, w_out, wq, keys_t, u_emb, v_emb, ple_gate, ple_proj, p_in, final_norm, out):
    nc = core.nc
    bank = core.bank
    m = mixer_inputs(core)
    turns = NB * PK_HEADS // 2
    per_block = PK_HEADS // 2
    picks = 2 * TOPK
    depth = 8
    diags = 4
    uses = picks // depth
    x2, h_tok, q_t = core.slots(41, 8, D), core.slots(33, 8, D), core.slots(49, 8)
    u_ring, v_ring = core.slots(0, 16, D), core.slots(57, 16, D)
    keys = core.slots(16, 1, 2 * N_KEYS)[:, 0, :]
    sc = core.slots(17, 1, N_KEYS)
    rest = core.slots(18, 1, N_KEYS)
    q_now = core.slots(19, 1, P)[:, 0:2, :]
    diag = core.slots(31, 1, P)
    onehot = core.arena[:, 91 * SLOT:91 * SLOT + picks * N_CAND]
    others = slice(P, SEQ)
    piece = [core.slots(75 + 4 * i, 4, STRIP) for i in range(4)]
    gates = core.slots(35, 12, SEQ - P)
    merged = gates[:, 0:KD, :]
    x_others = core.slots(41, 6, D)
    h_t = core.slots(20, 8)
    norm_row = core.slots(95, 2, D)[:, 0, :]
    junk = onehot[:, 0:D]
    mean, root, rstd = (core.stats[:, 4 * i:4 * i + 3] for i in range(3))
    ple_gate_sb, ple_proj_sb, p_sb = core.slots(75, 16, D), core.slots(20, 4, D), core.slots(24, 2, PLE)
    final_row = core.slots(26, 2, D)[:, 0, :]
    p_now, p_t = core.slots(32, 1, PLE)[:, 0, :], core.slots(32, 1, PLE)[:, 1, :].rearrange("p (k t) -> p k t", t=P)
    x_now = core.slots(73, 2, D)[:, 0, :]
    x_t = core.slots(95, 2, P)
    y_all = h_tok
    end_ssq, end_mean, end_root, end_rstd = (core.stats[:, 32 + i:33 + i] for i in range(4))
    ssq_3, mean_3, root_3, rstd_3 = (core.stats[:, 36 + i:37 + i] for i in range(4))
    at = 28 * SLOT

    def small(*shape, dt=F32):
        nonlocal at
        n = 1
        for d in shape:
            n *= d
        ap = core.arena[:, at:at + n]
        at += n
        if dt != F32:
            ap = ap.bitcast(dt)
        return ap if len(shape) == 1 else ap.rearrange("p (a b) -> p a b", b=shape[1])

    top, top_i, top_f = small(4, TOPK), small(4, TOPK, dt=U32), small(4, TOPK)
    cand, cand_id, cand_rest = small(2, N_CAND), small(2, N_CAND), small(2, N_CAND)
    best, best_i, best_f = small(2, TOPK), small(2, TOPK, dt=U32), small(2, TOPK)
    ids_f, shifted, weight = small(picks), small(2, TOPK), small(2, TOPK)
    total, inverse = small(2), small(2)
    gate_next, gate_now = small(2, TOPK), small(2, TOPK)
    ids = small(2, picks, dt=U32)
    dots, gelu, coef = small(2, TOPK), small(2, TOPK), small(2, TOPK)
    assert at <= 31 * SLOT

    keys_zero = core.sem("keys_zeroed")
    keys_loaded = core.sem("keys_loaded")
    ple_loaded = core.sem("ple_weights_loaded")
    u_loaded = [core.sem(f"u_row_loaded{i}") for i in range(depth)]
    v_loaded = [core.sem(f"v_row_loaded{i}") for i in range(depth)]
    u_used = core.sem("u_row_used")
    v_used = core.sem("v_row_used")
    q_staged = core.sem("query_staged")
    sc_ready = core.sem("key_scores_ready")
    sc_taken = core.sem("key_scores_taken")
    ids_ready = core.sem("ids_ready")
    shift_ready = core.sem("best_scores_shifted")
    exp_ready = core.sem("best_scores_exp")
    gelu_ready = core.sem("gelu_ready")
    coef_ready = core.sem("coefficients_ready")
    diag_ready = core.sem("diagonal_ready")
    acc_taken = core.sem("sum_taken")
    v_link = core.sem("experts_vector_link")
    carrier = core.sem("experts_gpsimd_wait_carrier")
    carrier_v = core.sem("experts_vector_wait_carrier")
    carrier_a = core.sem("experts_scalar_wait_carrier")
    branch_ready = core.sem("others_branch_ready")
    branch_used = core.sem("others_branch_used")
    merged_ready = core.sem("others_merged_ready")
    w_out_loaded = [core.sem(f"others_w_out_loaded{i}") for i in range(4)]
    wq_loaded = [core.sem(f"others_wq_loaded{i}") for i in range(4)]
    x_loaded = core.sem("others_x_loaded")
    out_ready = core.sem("others_w_out_summed")
    x2_ready = core.sem("others_x2_ready")
    squares = core.sem("others_squares_summed")
    ms_ready = core.sem("others_mean_squares_ready")
    rooted = core.sem("others_rooted")
    h_ready = core.sem("others_input_ready")
    turned = core.sem("others_input_turned")
    turned_taken = core.sem("others_input_turned_taken")
    q_ready = core.sem("others_queries_ready")
    q_taken = core.sem("others_queries_taken")
    end_free = core.sem("end_buffers_free")
    end_staged = core.sem("end_inputs_staged")
    end_squared = core.sem("end_squares_summed")
    end_ms = core.sem("end_mean_square_ready")
    end_rooted = core.sem("end_rooted")
    end_rstd_ready = core.sem("end_rstd_ready")
    end_turned = core.sem("end_inputs_turned")
    end_turned_taken = core.sem("end_inputs_turned_taken")
    end_gate = core.sem("end_gate_summed")
    end_proj = core.sem("end_proj_summed")
    end_gated = core.sem("end_gated")
    end_x = core.sem("end_x_ready")
    end_y = core.sem("end_output_ready")
    stored = core.sem("end_output_stored")

    def out_parts(q):
        return {2: range(0, 5), 3: range(5, 10), 4: range(10, 12)}.get(q, ())

    def query_heads(q):
        return {5: (0, 1), 6: (2, 3, 4), 7: (5, 6, 7)}.get(q, ())

    with nc.Block() as block:
        @block.sync
        def _(sp):
            sp.wait_ge(keys_zero, 1)
            for c in range(2):
                sp.dma_start(keys[RH * c:RH * (c + 1), c * N_KEYS:(c + 1) * N_KEYS], keys_t[c]).then_inc(keys_loaded, 16)
            for i in range(4):
                sp.wait_ge(branch_ready, 4 * (i + 1))
                sp.dma_start(piece[i], w_out.rearrange("(k p) n -> p k n", p=P)[:, :, i * STRIP:(i + 1) * STRIP],
                             ).then_inc(w_out_loaded[i], 16)
            sp.wait_ge(merged_ready, KD)
            sp.dma_start(x_others, x[P:, :].rearrange("(b p) d -> p b d", p=P)).then_inc(x_loaded, 16)
            for i in range(4):
                sp.wait_ge(out_ready, 3 * (i + 1))
                sp.dma_start(piece[i], wq.rearrange("(k p) n -> p k n", p=P)[:, :, i * STRIP:(i + 1) * STRIP],
                             ).then_inc(wq_loaded[i], 16)
            sp.wait_ge(q_ready, PK_HEADS)
            sp.dma_start(ple_gate_sb, ple_gate.rearrange("(k p) n -> p k n", p=P)).then_inc(ple_loaded, 16)
            sp.dma_start(ple_proj_sb, ple_proj.rearrange("(k p) n -> p k n", p=P)).then_inc(ple_loaded, 16)
            sp.dma_start(p_sb, p_in.rearrange("(b p) d -> p b d", p=P)).then_inc(ple_loaded, 16)
            sp.dma_start(final_row, final_norm.partition_broadcast(P)).then_inc(ple_loaded, 16)
            for b in range(NB):
                sp.wait_ge(end_y, b + 1)
                sp.dma_start(out[b * P:(b + 1) * P, :], y_all[:, b, :]).then_inc(stored, 16)
            sp.wait_ge(stored, 16 * NB)

        @block.gpsimd
        def _(gp):
            gp.memset(keys, 0.0).then_inc(keys_zero, 1)

            def gather(n, parity, half):
                for table, ring, loaded, used in ((u_emb, u_ring, u_loaded, u_used), (v_emb, v_ring, v_loaded, v_used)):
                    for k in range(half * TOPK, (half + 1) * TOPK):
                        gp.wait_ge(used, picks * n + k + 1)
                        gp.sem_inc(carrier, 1)
                        gp.indirect_dma_start(ring[:, k % depth, :], None, table,
                                              bass.IndirectOffsetOnAxis(ap=ids[:, parity, k:k + 1], axis=0),
                                              ).then_inc(loaded[k % depth], 16)

            with gp.Fori(0, turns, 2) as n:
                for parity in range(2):
                    gp.wait_ge(ids_ready, n + parity + 1)
                    gp.sem_inc(carrier, 1)
                    gather(n + parity, parity, 0)
                    gather(n + parity, parity, 1)

        @block.tensor
        def _(pe):
            pe.nop().then_inc(v_used, depth)
            pe.wait_ge(keys_loaded, 32)

            def key_scores(n):
                pe.wait_ge(q_staged, n + 1)
                pe.wait_ge(sc_taken, n)
                for h in range(2):
                    ins = pe.matmul(bank[2][:, h * 2 * N_KEYS:(h + 1) * 2 * N_KEYS], q_now[:, h, :], keys, start=True,
                                    stop=True)
                ins.then_inc(sc_ready, 1)

            def branches(t):
                if t >= 2:
                    pe.wait_ge(branch_used, 2 * (t - 1))
                for which, y in ((0, m["hq"]), (1, m["ld"])):
                    for k in range(4):
                        ins = pe.matmul(bank[3 + 2 * (t % 2) + which][:, 0:SEQ - P],
                                        piece[t // 2][:, 4 * which + k, (t % 2) * P:(t % 2 + 1) * P], y[:, k, others],
                                        start=(k == 0), stop=(k == 3))
                    ins.then_inc(branch_ready, 1)

            def output(i):
                if i == 0:
                    pe.wait_ge(merged_ready, KD)
                if i % 3 == 0:
                    pe.wait_ge(w_out_loaded[i // 3], 16)
                if i >= 4:
                    pe.wait_ge(x2_ready, i - 3)
                for k in range(KD):
                    ins = pe.matmul(bank[3 + i % 4][:, 0:STRIP], merged[:, k, (i % 3) * P:(i % 3 + 1) * P], piece[i // 3][:, k, :],
                                    start=(k == 0), stop=(k == KD - 1))
                ins.then_inc(out_ready, 1)

            def turn_input(i):
                pe.wait_ge(h_ready, i // 2 + 1)
                if i < 2:
                    pe.wait_ge(x2_ready, 12)
                else:
                    pe.wait_ge(turned_taken, i - 1)
                for k in range(4):
                    dk = 4 * (i % 2) + k
                    ins = pe.transpose(bank[3 + i % 2][:, k * P:(k + 1) * P], h_tok[:, 1 + i // 2, dk * P:(dk + 1) * P],
                                       core.ident)
                ins.then_inc(turned, 1)

            def queries(h):
                if h == 0:
                    pe.wait_ge(turned_taken, 6)
                if h >= 2:
                    pe.wait_ge(q_taken, h - 1)
                if h % 2 == 0:
                    pe.wait_ge(wq_loaded[h // 2], 16)
                for k in range(KD):
                    ins = pe.matmul(bank[5 + h % 2][:, 0:SEQ - P], piece[h // 2][:, k, (h % 2) * P:(h % 2 + 1) * P],
                                    h_t[:, k, others], start=(k == 0), stop=(k == KD - 1))
                ins.then_inc(q_ready, 1)

            def rest_of_finish(q):
                if q < 2:
                    for t in range(4 * q, 4 * q + 4):
                        branches(t)
                for i in out_parts(q):
                    output(i)
                if q == 5:
                    for i in range(6):
                        turn_input(i)
                for h in query_heads(q):
                    queries(h)

            def end_inputs(b):
                pe.wait_ge(end_staged, b + 1)
                pe.wait_ge(end_free, b + 1)
                for k in range(2):
                    ins = pe.transpose(bank[7][:, k * P:(k + 1) * P], p_now[:, k * P:(k + 1) * P], core.ident)
                ins.then_inc(end_turned, 1)
                for half in range(2):
                    for k in range(4):
                        dk = 4 * half + k
                        ins = pe.transpose(bank[3 + half][:, k * P:(k + 1) * P], x_now[:, dk * P:(dk + 1) * P], core.ident)
                    ins.then_inc(end_turned, 1)
                pe.wait_ge(ple_loaded, 64)
                for half in range(2):
                    for k in range(KD):
                        if half == 0 and k % 4 == 0:
                            pe.wait_ge(end_turned_taken, 3 * b + 2 + k // 4)
                        ins = pe.matmul(bank[5 + half][:], x_t[:, k, :], ple_gate_sb[:, k, half * 512:(half + 1) * 512],
                                        start=(k == 0), stop=(k == KD - 1))
                    ins.then_inc(end_gate, 1)

            def end_projection(b):
                pe.wait_ge(end_turned_taken, 3 * b + 3)
                for half in range(2):
                    for k in range(2):
                        ins = pe.matmul(bank[(7, 3)[half]][:], p_t[:, k, :], ple_proj_sb[:, k, half * 512:(half + 1) * 512],
                                        start=(k == 0), stop=(k == 1))
                    ins.then_inc(end_proj, 1)

            def turn(n, more, ends=None):
                if more:
                    key_scores(n + 1)
                first_block = isinstance(n, int) and n < per_block
                for k in range(picks):
                    if first_block and k % TOPK == 0:
                        rest_of_finish(2 * n + k // TOPK)
                    if ends is not None and k == 0:
                        end_inputs(ends)
                    if ends is not None and k == TOPK:
                        end_projection(ends)
                    if k == 0 and not (isinstance(n, int) and n == 0):
                        pe.wait_ge(acc_taken, n)
                    pe.wait_ge(v_loaded[k % depth], 16 * (uses * n + k // depth + 1))
                    pe.wait_ge(diag_ready, picks * n + k + 1)
                    for half in range(2):
                        ins = pe.matmul(bank[half][:], diag[:, k % diags, :], v_ring[:, k % depth, half * 512:(half + 1) * 512],
                                        start=(k == 0), stop=(k == picks - 1))
                    ins.then_inc(v_used, 1)

            key_scores(0)
            for n in range(per_block):
                turn(n, True)

            def block_turns(g, last):
                for i in range(per_block):
                    turn(per_block * g + i, not (last and i == per_block - 1), g - 1 if i == 1 else None)

            with pe.Fori(1, NB - 1) as g:
                block_turns(g, False)
            block_turns(NB - 1, True)
            end_inputs(NB - 1)
            end_projection(NB - 1)

        @block.scalar
        def _(act):
            def stage_query(n):
                act.wait_ge(sc_ready, n)
                block_, pair = n // per_block, n % per_block
                act.activation(q_now, q_t[:, bass.ds(2 * pair, 2), bass.ds(block_ * P, P)], ACT.Copy).then_inc(q_staged, 1)

            def head(n, half):
                act.wait_ge(u_used, depth + picks * n + TOPK * (half + 1))
                act.activation(gelu[:, half, :], dots[:, half, :], ACT.Gelu).then_inc(gelu_ready, 1)
                act.wait_ge(coef_ready, 2 * n + half + 1)
                for k in range(TOPK * half, TOPK * (half + 1)):
                    act.wait_ge(v_used, depth + picks * n + k - diags + 1)
                    act.activation(diag[:, k % diags, :], core.ident, ACT.Copy,
                                   scale=coef[:, half, k % TOPK:k % TOPK + 1]).then_inc(diag_ready, 1)

            def softmax_exp(n):
                act.wait_ge(shift_ready, n + 1)
                act.activation(weight, shifted, ACT.Exp).then_inc(exp_ready, 1)

            def root_rest():
                act.wait_ge(ms_ready, 1)
                act.activation(root, mean, ACT.Sqrt).then_inc(rooted, 1)

            def rest_of_finish(q):
                if q == 5:
                    for i in range(6):
                        act.wait_ge(turned, i + 1)
                        b = 1 + i // 2
                        act.activation(h_t[:, 4 * (i % 2):4 * (i % 2) + 4, b * P:(b + 1) * P],
                                       bank[3 + i % 2][:].rearrange("p (k t) -> p k t", t=P), ACT.Copy).then_inc(turned_taken, 1)
                for h in query_heads(q):
                    act.wait_ge(q_ready, h + 1)
                    act.activation(q_t[:, h, others], bank[5 + h % 2][:, 0:SEQ - P], ACT.Copy).then_inc(q_taken, 1)

            stage_query(0)
            softmax_exp(0)
            for n in range(per_block):
                if n == per_block - 1:
                    act.wait_ge(q_taken, 2)
                stage_query(n + 1)
                rest_of_finish(2 * n)
                head(n, 0)
                if 2 * n == 4:
                    root_rest()
                softmax_exp(n + 1)
                rest_of_finish(2 * n + 1)
                head(n, 1)
            act.wait_ge(q_taken, PK_HEADS)

            def end_inputs(b):
                act.wait_ge(ple_loaded, 64)
                act.wait_ge(acc_taken, per_block * (b + 1))
                act.wait_ge(end_free, b + 1)
                act.sem_inc(carrier_a, 1)
                x_b = x2[:, bass.ds((b + X2_AT[0]) % NB, 1), :]
                act.activation(p_now, p_sb[:, bass.ds(b, 1), :], ACT.Copy)
                act.activation(x_now, x_b, ACT.Copy).then_inc(end_staged, 1)
                act.activation(y_all[:, bass.ds(b, 1), :], x_b, ACT.Square, accum_out=end_ssq).then_inc(end_squared, 1)
                act.wait_ge(end_turned, 3 * b + 1)
                act.activation(p_t, bank[7][:, 0:2 * P].rearrange("p (k t) -> p k t", t=P), ACT.Copy).then_inc(end_turned_taken, 1)
                for half in range(2):
                    act.wait_ge(end_turned, 3 * b + 2 + half)
                    for k in range(4):
                        dk = 4 * half + k
                        ins = act.activation(x_t[:, dk, :], bank[3 + half][:, k * P:(k + 1) * P], ACT.Copy,
                                             scale=core.col("norm_ple", dk))
                    ins.then_inc(end_turned_taken, 1)
                act.wait_ge(end_ms, 2 * b + 1)
                act.activation(end_root, end_mean, ACT.Sqrt).then_inc(end_rooted, 1)

            def end_gates(b):
                act.wait_ge(end_rstd_ready, 2 * b + 1)
                for half in range(2):
                    act.wait_ge(end_gate, 2 * b + half + 1)
                    act.activation(x_now[:, half * 512:(half + 1) * 512], bank[5 + half][:], ACT.Sigmoid,
                                   scale=end_rstd).then_inc(end_gated, 1)

            def end_norm(b):
                act.wait_ge(end_x, 2 * b + 2)
                act.wait_ge(end_squared, 2 * b + 1)
                act.sem_inc(carrier_a, 1)
                act.activation(y_all[:, bass.ds(b, 1), :], x2[:, bass.ds((b + X2_AT[0]) % NB, 1), :], ACT.Square,
                               accum_out=ssq_3).then_inc(end_squared, 1)
                act.wait_ge(end_ms, 2 * b + 2)
                act.activation(root_3, mean_3, ACT.Sqrt).then_inc(end_rooted, 1)

            def block_turns(g, last):
                for i in range(per_block):
                    n = per_block * g + i
                    more = not (last and i == per_block - 1)
                    if more:
                        stage_query(n + 1)
                    if i == 1:
                        end_inputs(g - 1)
                    if i == 2:
                        end_norm(g - 1)
                    head(n, 0)
                    if more:
                        softmax_exp(n + 1)
                    if i == 1:
                        end_gates(g - 1)
                    head(n, 1)

            with act.Fori(1, NB - 1) as g:
                block_turns(g, False)
            block_turns(NB - 1, True)
            end_inputs(NB - 1)
            end_gates(NB - 1)
            end_norm(NB - 1)

        @block.vector
        def _(v):
            link = Link(v, v_link)
            v.nop().then_inc(u_used, depth)
            v.nop().then_inc(end_free, 1)

            def select(n):
                v.wait_ge(sc_ready, n + 1)
                v.tensor_copy(sc, bank[2][:].rearrange("p (a b) -> p a b", b=N_KEYS)).then_inc(sc_taken, 1)
                v.wait_ge(sc_taken, n + 1)
                v.sem_inc(carrier_v, 1)
                for a in range(4):
                    ins = v.max(top[:, a, 0:8], sc[:, a, :])
                link(ins)
                for a in range(4):
                    v.max_index(top_i[:, a, 0:8], top[:, a, 0:8], sc[:, a, :])
                    ins = v.match_replace(rest[:, a, :], top[:, a, 0:8], sc[:, a, :], LOWEST)
                link(ins)
                for a in range(4):
                    ins = v.max(top[:, a, 8:16], rest[:, a, :])
                link(ins)
                for a in range(4):
                    ins = v.max_index(top_i[:, a, 8:16], top[:, a, 8:16], rest[:, a, :])
                link(ins)
                link(v.tensor_copy(top_f, top_i))
                scores_ = top.rearrange("p (h c) k -> p h c k", c=2)
                index_ = top_f.rearrange("p (h c) k -> p h c k", c=2)
                to = 0
                for i in range(8):
                    w = CAND[i]
                    v.tensor_tensor(cand[:, :, to:to + w], scores_[:, :, 0, i:i + 1].to_broadcast([P, 2, w]),
                                    scores_[:, :, 1, 0:w], ALU.add)
                    v.scalar_tensor_tensor(out=cand_id[:, :, to:to + w], in0=index_[:, :, 0, i:i + 1].to_broadcast([P, 2, w]),
                                           scalar=float(N_KEYS), in1=index_[:, :, 1, 0:w], op0=ALU.mult, op1=ALU.add)
                    to += w
                v.tensor_tensor(cand[:, :, to:], scores_[:, :, 0, 8:16], scores_[:, :, 1, 0:1].to_broadcast([P, 2, 8]), ALU.add)
                link(v.scalar_tensor_tensor(out=cand_id[:, :, to:], in0=index_[:, :, 0, 8:16], scalar=float(N_KEYS),
                                            in1=index_[:, :, 1, 0:1].to_broadcast([P, 2, 8]), op0=ALU.mult, op1=ALU.add))
                for h in range(2):
                    ins = v.max(best[:, h, 0:8], cand[:, h, :])
                link(ins)
                for h in range(2):
                    v.max_index(best_i[:, h, 0:8], best[:, h, 0:8], cand[:, h, :])
                    ins = v.match_replace(cand_rest[:, h, :], best[:, h, 0:8], cand[:, h, :], LOWEST)
                link(ins)
                for h in range(2):
                    ins = v.max(best[:, h, 8:16], cand_rest[:, h, :])
                link(ins)
                for h in range(2):
                    ins = v.max_index(best_i[:, h, 8:16], best[:, h, 8:16], cand_rest[:, h, :])
                link(ins)
                v.tensor_tensor(shifted, best, best[:, :, 0:1].to_broadcast([P, 2, TOPK]), ALU.subtract).then_inc(shift_ready, 1)
                link(v.tensor_copy(best_f, best_i))
                hot = onehot.rearrange("p (k c) -> p k c", c=N_CAND)
                link(v.tensor_tensor(hot, best_f.rearrange("p h k -> p (h k)").unsqueeze(2).to_broadcast([P, picks, N_CAND]),
                                     core.iota_cand.unsqueeze(1).to_broadcast([P, picks, N_CAND]), ALU.is_equal))
                hot4 = onehot.rearrange("p (h k c) -> p h k c", h=2, c=N_CAND)
                link(v.tensor_tensor(hot4, hot4, cand_id.unsqueeze(2).to_broadcast([P, 2, TOPK, N_CAND]), ALU.mult))
                link(v.tensor_reduce(ids_f, hot, AX.X, ALU.add))
                v.tensor_copy(ids[:, bass.ds(n % 2, 1), :], ids_f).then_inc(ids_ready, 1)

            def softmax_rest(n):
                v.wait_ge(exp_ready, n + 1)
                link(v.tensor_reduce(total, weight, AX.X, ALU.add))
                link(v.reciprocal(inverse, total))
                link(v.tensor_tensor(gate_next, weight, inverse.unsqueeze(2).to_broadcast([P, 2, TOPK]), ALU.mult))

            def merge(t):
                for which in range(2):
                    gate = gates[:, KD * which + t, :]
                    v.wait_ge(branch_ready, 2 * t + which + 1)
                    v.tensor_tensor(gate, bank[3 + 2 * (t % 2) + which][:, 0:SEQ - P], gate, ALU.mult).then_inc(branch_used, 1)
                v.wait_ge(branch_used, 2 * t + 2)
                v.tensor_tensor(merged[:, t, :], gates[:, t, :], gates[:, KD + t, :], ALU.add).then_inc(merged_ready, 1)

            def residual(i):
                if i == 0:
                    v.wait_ge(x_loaded, 16)
                v.wait_ge(out_ready, i + 1)
                part = x_others[:, i % 3, (i // 3) * STRIP:(i // 3 + 1) * STRIP]
                v.tensor_tensor(part, part, bank[3 + i % 4][:, 0:STRIP], ALU.add).then_inc(x2_ready, 1)

            def mean_squares():
                v.wait_ge(x2_ready, 12)
                for b in range(3):
                    v.scalar_tensor_tensor(out=junk, in0=x_others[:, b, :], scalar=1.0, in1=x_others[:, b, :], op0=ALU.mult,
                                           op1=ALU.mult, accum_out=mean[:, b:b + 1]).then_inc(squares, 1)
                    v.wait_ge(squares, b + 1)
                v.tensor_scalar(mean, mean, 1.0 / D, EPS, ALU.mult, ALU.add).then_inc(ms_ready, 1)

            def normed():
                v.wait_ge(rooted, 1)
                link(v.reciprocal(rstd, root))
                for b in range(3):
                    v.scalar_tensor_tensor(out=h_tok[:, 1 + b, :], in0=x_others[:, b, :], scalar=rstd[:, b:b + 1], in1=norm_row,
                                           op0=ALU.mult, op1=ALU.mult).then_inc(h_ready, 1)

            def rest_of_finish(q, k):
                if q < 2 and k % 4 == 3:
                    merge(4 * q + k // 4)
                parts = out_parts(q)
                if k % 3 == 2 and k // 3 < len(parts):
                    residual(parts[k // 3])

            def take_sum(n):
                for half in range(2):
                    v.wait_ge(v_used, depth + picks * (n + 1))
                    at = (n // per_block + X2_AT[0]) % NB
                    part = x2[:, bass.ds(at, 1), half * 512:(half + 1) * 512]
                    ins = v.tensor_tensor(part, part, bank[half][:], ALU.add)
                ins.then_inc(acc_taken, 1)
                v.wait_ge(acc_taken, n + 1)
                v.sem_inc(carrier_v, 1)

            def end_mean_square(b, i):
                v.wait_ge(end_squared, 2 * b + i + 1)
                v.tensor_scalar((end_mean, mean_3)[i], (end_ssq, ssq_3)[i], 1.0 / D, EPS, ALU.mult, ALU.add).then_inc(end_ms, 1)

            def end_reciprocal(b, i):
                v.wait_ge(end_rooted, 2 * b + i + 1)
                v.reciprocal((end_rstd, rstd_3)[i], (end_root, root_3)[i]).then_inc(end_rstd_ready, 1)

            def end_x_half(b, half):
                cols = slice(half * 512, (half + 1) * 512)
                v.wait_ge(end_gated, 2 * b + half + 1)
                v.wait_ge(end_proj, 2 * b + half + 1)
                link(v.tensor_tensor(x_now[:, cols], x_now[:, cols], bank[(7, 3)[half]][:], ALU.mult))
                x_b = x2[:, bass.ds((b + X2_AT[0]) % NB, 1), cols]
                v.tensor_tensor(x_b, x_b, x_now[:, cols], ALU.add).then_inc(end_x, 1)

            def end_output(b):
                v.wait_ge(end_rstd_ready, 2 * b + 2)
                v.scalar_tensor_tensor(out=y_all[:, bass.ds(b, 1), :], in0=x2[:, bass.ds((b + X2_AT[0]) % NB, 1), :],
                                       scalar=rstd_3, in1=final_row, op0=ALU.mult, op1=ALU.mult).then_inc(end_y, 1)

            def end_step(b, q, k):
                if (q, k) == (2, 5):
                    end_mean_square(b, 0)
                if (q, k) == (2, 11):
                    end_reciprocal(b, 0)
                if q == 3 and k in (11, 13):
                    end_x_half(b, (k - 11) // 2)
                if (q, k) == (3, 15):
                    v.wait_ge(end_x, 2 * b + 2)
                    v.sem_inc(end_free, 1)
                if (q, k) == (4, 5):
                    end_mean_square(b, 1)
                if (q, k) == (4, 11):
                    end_reciprocal(b, 1)
                if (q, k) == (4, 13):
                    end_output(b)

            def dot_products(n, half, i=None, b=None):
                h = h_tok[:, bass.ds(n // per_block, 1), :]
                for k in range(half * TOPK, (half + 1) * TOPK):
                    v.wait_ge(u_loaded[k % depth], 16 * (uses * n + k // depth + 1))
                    row = u_ring[:, k % depth, :]
                    v.scalar_tensor_tensor(out=row, in0=row, scalar=1.0, in1=h, op0=ALU.mult, op1=ALU.mult,
                                           accum_out=dots[:, half, k % TOPK:k % TOPK + 1]).then_inc(u_used, 1)
                    if isinstance(n, int) and n < per_block:
                        rest_of_finish(2 * n + half, k % TOPK)
                    if k == 9 and not (isinstance(n, int) and n == 0):
                        take_sum(n - 1)
                    if i in (1, 2):
                        end_step(b, 2 * i + half, k % TOPK)

            def coefficients(n, half):
                v.wait_ge(gelu_ready, 2 * n + half + 1)
                v.tensor_tensor(coef[:, half, :], gelu[:, half, :], gate_now[:, half, :], ALU.mult).then_inc(coef_ready, 1)

            def turn(n, more, i=None, b=None):
                if not (isinstance(n, int) and n == 0):
                    v.wait_ge(coef_ready, 2 * n)
                link(v.tensor_copy(gate_now, gate_next))
                dot_products(n, 0, i, b)
                coefficients(n, 0)
                norms = isinstance(n, int) and n == 2
                if norms:
                    mean_squares()
                if more:
                    select(n + 1)
                if norms:
                    normed()
                dot_products(n, 1, i, b)
                coefficients(n, 1)
                if more:
                    softmax_rest(n + 1)
                link.restart()

            select(0)
            softmax_rest(0)
            link.restart()
            for n in range(per_block):
                turn(n, True)

            def block_turns(g, last):
                for i in range(per_block):
                    turn(per_block * g + i, not (last and i == per_block - 1), i, g - 1)

            with v.Fori(1, NB - 1) as g:
                block_turns(g, False)
            block_turns(NB - 1, True)
            take_sum(turns - 1)
            b = NB - 1
            end_mean_square(b, 0)
            end_reciprocal(b, 0)
            end_x_half(b, 0)
            end_x_half(b, 1)
            end_mean_square(b, 1)
            end_reciprocal(b, 1)
            end_output(b)


def hybrid_block(nc, x, strips, params, w2, a2, g2, w_branch_hg, w_branch_rw, w_out, norm_ffn, wq, keys_t, u_emb, v_emb,
                 ple_gate, ple_proj, p_in, final_norm, out):
    with ExitStack() as ctx:
        core = Core(nc, ctx)
        project(core, x, strips, params, w2, a2, g2)
        core.end_phase()
        mix(core)
        finish(core, x, strips, g2, w_branch_hg, w_branch_rw, w_out, norm_ffn, wq)
        experts(core, x, w_out, wq, keys_t, u_emb, v_emb, ple_gate, ple_proj, p_in, final_norm, out)


def kernel(**inputs):
    import numpy as np
    import concourse.bacc as bacc
    from concourse.bass_utils import run_bass_kernel_spmd

    a = {name: np.asarray(value) for name, value in inputs.items()}
    vectors = [a["norm_mix_w"], a["rw_mu"], a["rw_w0"], a["rw_a0"], a["rw_k_k"], a["rw_k_a"], a["rw_r_k"], a["rw_ln_w"],
               a["rw_ln_b"], a["hg_lb"][0], a["hg_lb"][1], a["hg_norm_w"], a["norm_ple_w"]]
    arrays = {
        "x": a["x"][0],
        "w_in_strips": a["w_in"][0].reshape(KD, P, -1, STRIP).transpose(2, 1, 0, 3),
        "params": np.concatenate([vector.reshape(-1, P).T for vector in vectors], axis=1),
        "w2": a["rw_w2"][0], "a2": a["rw_a2"][0], "g2": a["rw_g2"][0],
        "w_branch_hg": a["w_branch_hg"][0], "w_branch_rw": a["w_branch_rw"][0], "w_out": a["w_out"][0],
        "norm_ffn": a["norm_ffn_w"][0], "wq": a["peer_wq"][0], "keys_t": a["peer_keys"][0].transpose(0, 2, 1),
        "u_emb": a["peer_u"][0], "v_emb": a["peer_v"][0], "ple_gate": a["ple_gate"][0], "ple_proj": a["ple_proj"][0],
        "p_in": a["p"][0, 0], "final_norm": a["final_norm_w"],
    }
    arrays = {name: np.ascontiguousarray(value) for name, value in arrays.items()}
    nc = bacc.Bacc("TRN2", target_bir_lowering=False, num_devices=1)
    args = [nc.dram_tensor(name, value.shape, mybir.dt.from_np(value.dtype), kind="ExternalInput").ap()
            for name, value in arrays.items()]
    out = nc.dram_tensor("out", (SEQ, D), F32, kind="ExternalOutput").ap()
    hybrid_block(nc, *args, out)
    result = run_bass_kernel_spmd(nc, [arrays], core_ids=[0])
    return result.results[0]["out"].reshape(1, SEQ, D)
```

```python
from contextlib import ExitStack

import concourse.bass as bass
from concourse import mybir

F32 = mybir.dt.float32
I32 = mybir.dt.int32
U32 = mybir.dt.uint32
ALU = mybir.AluOpType
ACT = mybir.ActivationFunctionType
AX = mybir.AxisListType

P = 128
SEQ = 512
D = 1024
KD = D // P
NB = SEQ // P
EPS = 1e-6
GN_EPS = 64e-5
HG_HEADS = 4
RW_HEADS = 8
PAIRS = RW_HEADS // 2
RH = 64
LEVELS = [64, 32, 16, 8, 4, 2, 1]
STRIP = 256
RING = 3
PK_HEADS = 8
N_KEYS = 128
TOPK = 16
PLE = 256
CAND = [TOPK // (i + 1) for i in range(TOPK)]
N_CAND = sum(CAND)
EXP_HALF = 0.6065306597126334
LOWEST = -3.0e38
N_CONSTANTS = 9 + 6 * len(LEVELS)
SLOT = 512
VECTOR_ROWS = [16, 18, 20, 22, 24, 26, 28, 30]
X2_AT = [3, 0, 1, 2]

COLS = {}
_at = 0
for _name, _n in [("norm_mix", 8), ("mu", 14), ("w0", 4), ("a0", 4), ("k_k", 4), ("k_a", 4), ("r_k", 4),
                  ("ln_w", 4), ("ln_b", 4), ("lb0", 4), ("lb1", 4), ("hg_norm", 4), ("norm_ple", 8)]:
    COLS[_name] = (_at, _n)
    _at += _n
N_COLS = _at

RW_STRIPS = [14, 10, 11, 8, 9, 12, 13]
FEATURE_STRIPS = RW_STRIPS + [0, 1, 2, 3, 6, 7]
TOKEN_STRIPS = [4, 5]
GATE_STRIPS = list(range(15, 23))


class Link:

    def __init__(self, eng, sem):
        self.eng, self.sem, self.n = eng, sem, 0

    def __call__(self, ins):
        ins.then_inc(self.sem, 1)
        self.n += 1
        self.eng.wait_ge(self.sem, self.n)

    def restart(self):
        self.eng.sem_clear(self.sem)
        self.n = 0


class Core:

    def __init__(self, nc, ctx):
        self.nc, self.phase_sems = nc, []
        self.const = ctx.enter_context(nc.sbuf_tensor("const", [P, 3072], F32))
        self.arena = ctx.enter_context(nc.sbuf_tensor("arena", [P, 97 * SLOT], F32))
        self.bank = [ctx.enter_context(nc.psum_tensor(f"bank{i}", [P, 512], F32)) for i in range(8)]
        at = 0

        def const(n):
            nonlocal at
            at += n
            return self.const[:, at - n:at]

        self.ident = const(P)
        self.ones_pair = const(P)
        self.ones_full = const(P)
        self.mask_t = const(len(LEVELS) * P).rearrange("p (l t) -> p l t", t=P)
        self.mask_n = const(len(LEVELS) * P).rearrange("p (l t) -> p l t", t=P)
        self.causal = const(2 * P).rearrange("p (a t) -> p a t", a=2)
        self.masks = self.const[:, 0:at]
        self.cols = const(N_COLS)
        self.lb = const(4)
        self.one_minus_lb = const(4)
        self.one_minus_ka = const(4)
        self.iota_cand = const(N_CAND)
        self.stats = const(64)
        self.exp_mid = const(4 * NB).rearrange("p (j c) -> p j c", c=NB)
        self.keys = const(2 * N_KEYS)
        self.exp_last = const(4 * NB).rearrange("p (j c) -> p j c", c=NB)

    def sem(self, name):
        self.phase_sems.append(self.nc.alloc_semaphore(name=name))
        return self.phase_sems[-1]

    def end_phase(self):
        self.nc.clear_and_free_semaphores(self.phase_sems)
        self.phase_sems = []
        self.nc.all_engine_barrier()

    def col(self, name, i):
        at, _ = COLS[name]
        return self.cols[:, at + i:at + i + 1]

    def slots(self, at, n, inner=SLOT):
        return self.arena[:, at * SLOT:(at + n) * SLOT].rearrange("p (a b) -> p a b", b=inner)


def mixer_inputs(core):
    return {
        "h_t": core.slots(0, 8), "r": core.slots(8, 4), "k": core.slots(12, 4), "v": core.slots(16, 4),
        "ld": core.slots(20, 4), "hq": core.slots(24, 4), "hgo": core.slots(28, 4), "sgd": core.slots(32, 1)[:, 0, :],
        "kk": core.slots(33, 4), "nb": core.slots(37, 4), "cum": core.slots(41, 4), "hk": core.slots(45, 4),
        "hcum": core.slots(49, 4), "vh": core.slots(53, 4),
    }


def make_constants(core, gp, made):
    n = 0

    def did(ins):
        nonlocal n
        n += 1
        ins.then_inc(made, 1)
        gp.wait_ge(made, n)

    did(gp.memset(core.masks, 0.0))
    did(gp.affine_select(out=core.ident, in_=core.ident, pattern=[[-1, P]], compare_op=ALU.not_equal, fill=1.0,
                         base=0, channel_multiplier=1))
    did(gp.memset(core.ones_pair[0:RH, 0:RH], 1.0))
    did(gp.memset(core.ones_pair[RH:P, RH:P], 1.0))
    did(gp.memset(core.ones_full, 1.0))
    did(gp.memset(core.causal, 1.0))
    did(gp.affine_select(out=core.causal[:, 0, :], in_=core.causal[:, 0, :], pattern=[[1, P]], compare_op=ALU.is_gt,
                         fill=0.0, base=0, channel_multiplier=-1))
    did(gp.affine_select(out=core.causal[:, 1, :], in_=core.causal[:, 1, :], pattern=[[1, P]], compare_op=ALU.is_ge,
                         fill=0.0, base=0, channel_multiplier=-1))
    for level, n_ in enumerate(LEVELS):
        blocks = P // (2 * n_)
        for mask, half, lo in ((core.mask_t, 1, 0), (core.mask_n, 0, n_)):
            view = mask[:, level, :].rearrange("p (b two n) -> p b two n", two=2, n=n_)[:, :, half, :]
            did(gp.memset(view, 1.0))
            did(gp.affine_select(out=view, in_=view, pattern=[[-2 * n_, blocks], [0, n_]], compare_op=ALU.is_ge,
                                 fill=0.0, base=-lo, channel_multiplier=1))
            did(gp.affine_select(out=view, in_=view, pattern=[[2 * n_, blocks], [0, n_]], compare_op=ALU.is_ge,
                                 fill=0.0, base=lo + n_ - 1, channel_multiplier=-1))
    did(gp.iota(core.iota_cand, pattern=[[1, N_CAND]], base=0, channel_multiplier=0,
                allow_small_or_imprecise_dtypes=True))
    assert n == N_CONSTANTS


def project(core, x, w_in_strips, params, w2, a2, keys_t):
    nc = core.nc
    m = mixer_inputs(core)
    bank = core.bank
    ring = [core.slots(57 + 4 * i, 4, STRIP) for i in range(RING)]
    xs = core.slots(8, 8, D)
    x_in = core.slots(16, 8, D)
    raw = [core.arena[:, (69 * SLOT + i * 520):(69 * SLOT + i * 520 + 513)] for i in range(2)]
    diff = core.slots(72, 2)
    low = core.slots(74, 1)[:, 0, :]
    gd = core.slots(75, 1)[:, 0, :]
    w2a2 = core.slots(76, 1)[:, 0, :]
    chunk_ones = core.slots(78, 1)[:, 0, :]
    sig = core.slots(79, 2)
    sq = core.slots(81, 4)
    ln_f = core.slots(85, 4)
    ka = core.slots(89, 2)
    junk = core.slots(91, 2, D)[:, 0, :]
    e_mid, e_prev, e_inv = (core.slots(91 + 2 * i, 2) for i in range(3))
    ssq, mean, root, rstd = (core.stats[:, 4 * i:4 * i + 4] for i in range(4))
    lb_t = core.stats[:, 16:32].rearrange("p (a b) -> p a b", b=4)

    loaded_x = [core.sem(f"x_loaded{b}") for b in range(NB)]
    loaded_p = core.sem("params_loaded")
    strip_loaded = [core.sem(f"strip_loaded{i}") for i in range(RING)]
    constants = core.sem("constants_made")
    squares = core.sem("scalar_squares_summed")
    squares_v = core.sem("vector_squares_summed")
    rstd_ready = core.sem("rstd_ready")
    rooted = core.sem("mean_squares_rooted")
    ms_ready = core.sem("mean_squares_ready")
    scaled = core.sem("x_scaled_by_vector")
    scaled_a = core.sem("x_scaled_by_scalar")
    turned = core.sem("x_turned")
    h_ready = core.sem("h_ready")
    cols_ready = core.sem("columns_ready")
    cols_taken = core.sem("columns_taken")
    mixed = core.sem("shifts_mixed")
    low_ready = core.sem("low_rank_ready")
    lora_done = core.sem("lora_done")
    lora_taken = core.sem("lora_taken")
    sig_used = core.sem("lora_sigmoid_used")
    kk_raw = core.sem("kk_raw_ready")
    kk_sq = core.sem("kk_squared")
    norm_done = core.sem("kk_norm_summed")
    norm_rooted = core.sem("kk_norm_rooted")
    hg_used = core.sem("hgrn_tiles_used")
    f_ready = core.sem("f_ready")
    ln_ready = core.sem("log_f_ready")
    keys_zero = core.sem("keys_zeroed")
    keys_loaded = core.sem("keys_loaded")
    lb_diff = core.sem("lb_differences")
    decay_diff = core.sem("decay_differences")
    decay_exp = core.sem("decay_exponentials")
    lb_exp = core.sem("lb_exponentials")
    v_link = core.sem("project_vector_link")

    def by_chunk(ap):
        return ap.rearrange("p (c t) -> p c t", t=P)

    n_rw = 2 * len(RW_STRIPS)
    n_feature = 2 * len(FEATURE_STRIPS)
    rw_tiles = [(low, 12), (gd, 13)]
    for name, first in (("k", 4), ("r", 0), ("v", 8)):
        rw_tiles += [(m[name][:, j, :], first + j) for j in range(4)]

    with nc.Block() as block:
        @block.sync
        def _(sp):
            for b in range(NB):
                sp.dma_start(x_in[:, b, :], x[b * P:(b + 1) * P, :]).then_inc(loaded_x[b], 16)
            for n, strip in enumerate(FEATURE_STRIPS + TOKEN_STRIPS):
                if n >= RING:
                    sp.wait_ge(cols_ready, 2 * (n - RING) + 2)
                sp.dma_start(ring[n % RING], w_in_strips[strip]).then_inc(strip_loaded[n % RING], 16)

        @block.gpsimd
        def _(gp):
            gp.dma_start(core.cols, params).then_inc(loaded_p, 16)
            gp.dma_start(w2a2[0:RH, :], w2).then_inc(loaded_p, 16)
            gp.dma_start(w2a2[RH:P, :], a2).then_inc(loaded_p, 16)
            gp.memset(core.keys, 0.0).then_inc(keys_zero, 1)
            make_constants(core, gp, constants)
            gp.wait_ge(keys_zero, 1)
            for c in range(2):
                gp.dma_start(core.keys[RH * c:RH * (c + 1), c * N_KEYS:(c + 1) * N_KEYS], keys_t[c]).then_inc(keys_loaded, 16)
            gp.wait_ge(keys_loaded, 32)

        @block.tensor
        def _(pe):
            pe.wait_ge(constants, 2)
            pe.wait_ge(scaled, 2)
            pe.wait_ge(scaled_a, 2)
            for dk in range(KD):
                for b in range(NB):
                    if dk >= 2 and b == 0:
                        pe.wait_ge(h_ready, dk - 1)
                    ins = pe.transpose(bank[6 + dk % 2][:, b * P:(b + 1) * P], xs[:, b, dk * P:(dk + 1) * P], core.ident)
                ins.then_inc(turned, 1)
            pe.wait_ge(h_ready, KD)

            def strips(i, count):
                for s in range(count):
                    pe.wait_ge(strip_loaded[s], 16 * (i + 1))
                    for half in range(2):
                        tile = 2 * s + half
                        if not (isinstance(i, int) and i == 0):
                            pe.wait_ge(cols_taken, 6 * i + tile - 5)
                        for k in range(KD):
                            ins = pe.matmul(bank[tile][:], ring[s][:, k, half * P:(half + 1) * P], m["h_t"][:, k, :],
                                            start=(k == 0), stop=(k == KD - 1))
                        ins.then_inc(cols_ready, 1)

            strips(0, RING)
            pe.wait_ge(low_ready, 1)
            pe.wait_ge(mixed, 1)
            for j in range(PAIRS):
                for half in range(2):
                    if j:
                        pe.wait_ge(lora_taken, 2 * (j - 1) + half + 1)
                    rows = slice(RH * half, RH * (half + 1))
                    pe.matmul(bank[6 + half][:], w2a2[rows, j * P:(j + 1) * P], low[rows, :], start=True,
                              stop=True).then_inc(lora_done, 1)
            strips(1, RING)
            pe.wait_ge(constants, N_CONSTANTS)
            pe.wait_ge(lora_taken, 2 * PAIRS)
            for j in range(PAIRS):
                pe.wait_ge(kk_sq, j + 1)
                if j >= 2:
                    pe.wait_ge(norm_rooted, j - 1)
                pe.matmul(bank[6 + j % 2][:], core.ones_pair, sq[:, j, :], start=True, stop=True).then_inc(norm_done, 1)
            with pe.Fori(2, len(FEATURE_STRIPS) // RING) as i:
                strips(i, RING)
            strips(len(FEATURE_STRIPS) // RING, 1)
            t = n_feature
            for n in range(len(FEATURE_STRIPS), len(FEATURE_STRIPS) + len(TOKEN_STRIPS)):
                pe.wait_ge(strip_loaded[n % RING], 16 * (n // RING + 1))
                for b in range(NB):
                    pe.wait_ge(cols_taken, t - 5)
                    for k in range(KD):
                        ins = pe.matmul(bank[t % 6][:, 0:STRIP], m["h_t"][:, k, b * P:(b + 1) * P], ring[n % RING][:, k, :],
                                        start=(k == 0), stop=(k == KD - 1))
                    ins.then_inc(cols_ready, 1)
                    t += 1

        @block.scalar
        def _(act):
            for i, b in enumerate((0, 2)):
                act.wait_ge(loaded_x[b], 16)
                act.activation(junk, x_in[:, b, :], ACT.Square, accum_out=ssq[:, b:b + 1]).then_inc(squares, 1)
                act.wait_ge(squares, i + 1)
            act.wait_ge(ms_ready, 1)
            act.activation(root, mean, ACT.Sqrt).then_inc(rooted, 1)
            act.wait_ge(rstd_ready, 1)
            for b in (0, 2):
                act.activation(xs[:, b, :], x_in[:, b, :], ACT.Copy, scale=rstd[:, b:b + 1]).then_inc(scaled_a, 1)
            act.wait_ge(loaded_p, 48)
            for dk in range(KD):
                act.wait_ge(turned, dk + 1)
                act.activation(m["h_t"][:, dk, :], bank[6 + dk % 2][:], ACT.Copy,
                               scale=core.col("norm_mix", dk)).then_inc(h_ready, 1)
            act.wait_ge(lb_diff, 1)
            act.activation(lb_t[:, 2, :], lb_t[:, 0, :], ACT.Exp)
            act.activation(lb_t[:, 3, :], lb_t[:, 1, :], ACT.Exp).then_inc(lb_exp, 1)

            def take_rw(t):
                act.wait_ge(cols_ready, t + 1)
                if t >= 2:
                    act.wait_ge(mixed, t - 1)
                act.activation(raw[t % 2][:, 1:SEQ + 1], bank[t % 6][:], ACT.Copy).then_inc(cols_taken, 1)

            def square_kk(j):
                act.wait_ge(kk_raw, j + 1)
                act.activation(sq[:, j, :], m["kk"][:, j, :], ACT.Square).then_inc(kk_sq, 1)

            def decay_exps(j):
                act.wait_ge(decay_diff, j + 1)
                act.activation(e_inv[:, j % 2, :], e_mid[:, j % 2, :], ACT.Exp, scale=-1.0)
                act.activation(e_prev[:, j % 2, :], e_prev[:, j % 2, :], ACT.Exp)
                act.activation(core.exp_mid[:, j, :], by_chunk(m["cum"][:, j, :])[:, :, P // 2 - 1], ACT.Exp)
                act.activation(e_mid[:, j % 2, :], e_mid[:, j % 2, :], ACT.Exp).then_inc(decay_exp, 1)

            take_rw(0)
            take_rw(1)
            act.wait_ge(mixed, 1)
            act.activation(low[0:RH, :], low[0:RH, :], ACT.Tanh).then_inc(low_ready, 1)
            act.wait_ge(mixed, 2)
            act.activation(m["sgd"], gd, ACT.Sigmoid)
            for t in range(2, 6):
                take_rw(t)
            for j in range(PAIRS):
                act.wait_ge(lora_done, 2 * j + 1)
                if j >= 2:
                    act.wait_ge(sig_used, j - 1)
                act.activation(sig[:, j % 2, :], bank[6][:], ACT.Sigmoid, bias=core.col("w0", j)).then_inc(lora_taken, 1)
                act.wait_ge(lora_done, 2 * j + 2)
                act.activation(m["nb"][:, j, :], bank[7][:], ACT.Sigmoid, bias=core.col("a0", j)).then_inc(lora_taken, 1)
            for t in range(6, n_rw):
                take_rw(t)
                if t < 6 + PAIRS:
                    square_kk(t - 6)
                if t == 11:
                    for i in range(PAIRS):
                        act.wait_ge(norm_done, i + 1)
                        act.activation(sq[:, i, :], bank[6 + i % 2][:], ACT.Sqrt).then_inc(norm_rooted, 1)
                if t == 13:
                    decay_exps(0)
            for j in range(12):
                t = n_rw + j
                act.wait_ge(cols_ready, t + 1)
                if j >= 2:
                    act.wait_ge(hg_used, j - 1)
                else:
                    act.wait_ge(sig_used, PAIRS)
                ins = act.activation(sig[:, j % 2, :], bank[t % 6][:], ACT.Sigmoid)
                if not 4 <= j < 8:
                    dest = m["hq"][:, j, :] if j < 4 else m["hgo"][:, j - 8, :]
                    ins = act.activation(dest, bank[t % 6][:], ACT.Copy)
                ins.then_inc(cols_taken, 1)
                if j in (0, 2, 4):
                    decay_exps(1 + j // 2)
            act.wait_ge(f_ready, 4)
            act.activation(ln_f, m["hcum"], ACT.Ln).then_inc(ln_ready, 1)
            for t in range(n_feature, n_feature + 2 * NB):
                act.wait_ge(cols_ready, t + 1)
                s, b = divmod(t - n_feature, NB)
                act.activation(m["vh"][:, b, s * STRIP:(s + 1) * STRIP], bank[t % 6][:, 0:STRIP],
                               ACT.Copy).then_inc(cols_taken, 1)

        @block.vector
        def _(v):
            link = Link(v, v_link)
            for i in range(2):
                v.memset(raw[i][:, 0:1], 0.0)
            link(v.memset(chunk_ones, 1.0))
            link(v.memset(chunk_ones.rearrange("p (c t) -> p c t", t=P)[:, :, 0:1], 0.0))
            for i, b in enumerate((1, 3)):
                v.wait_ge(loaded_x[b], 16)
                v.scalar_tensor_tensor(out=xs[:, b, :], in0=x_in[:, b, :], scalar=1.0, in1=x_in[:, b, :], op0=ALU.mult,
                                       op1=ALU.mult, accum_out=ssq[:, b:b + 1]).then_inc(squares_v, 1)
                v.wait_ge(squares_v, i + 1)
            v.wait_ge(squares, 2)
            v.tensor_scalar(mean, ssq, 1.0 / D, EPS, ALU.mult, ALU.add).then_inc(ms_ready, 1)
            v.wait_ge(rooted, 1)
            v.reciprocal(rstd, root).then_inc(rstd_ready, 1)
            v.wait_ge(rstd_ready, 1)
            for b in (1, 3):
                v.tensor_scalar(xs[:, b, :], x_in[:, b, :], rstd[:, b:b + 1], None, ALU.mult).then_inc(scaled, 1)
            v.wait_ge(constants, N_CONSTANTS)
            v.wait_ge(loaded_p, 48)
            lb0 = core.cols[:, COLS["lb0"][0]:COLS["lb0"][0] + 4]
            lb1 = core.cols[:, COLS["lb1"][0]:COLS["lb1"][0] + 4]
            top = core.stats[:, 32:36]
            link(v.tensor_tensor(top, lb0, lb1, ALU.max))
            v.tensor_tensor(lb_t[:, 0, :], lb0, top, ALU.subtract)
            v.tensor_tensor(lb_t[:, 1, :], lb1, top, ALU.subtract).then_inc(lb_diff, 1)
            v.wait_ge(lb_exp, 1)
            link(v.tensor_tensor(top, lb_t[:, 2, :], lb_t[:, 3, :], ALU.add))
            link(v.reciprocal(lb_t[:, 0, :], top))
            link(v.tensor_tensor(core.lb, lb_t[:, 2, :], lb_t[:, 0, :], ALU.mult))
            v.tensor_scalar(core.one_minus_lb, core.lb, -1.0, 1.0, ALU.mult, ALU.add)
            at, n = COLS["k_a"]
            link(v.tensor_scalar(core.one_minus_ka, core.cols[:, at:at + n], -1.0, 1.0, ALU.mult, ALU.add))

            def mix_shift(t):
                dest, c = rw_tiles[t]
                v.wait_ge(cols_taken, t + 1)
                link(v.tensor_tensor(diff[:, 0, :], raw[t % 2][:, 0:SEQ], raw[t % 2][:, 1:SEQ + 1], ALU.subtract))
                v.scalar_tensor_tensor(out=dest, in0=diff[:, 0, :], scalar=core.col("mu", c),
                                       in1=raw[t % 2][:, 1:SEQ + 1], op0=ALU.mult, op1=ALU.add).then_inc(mixed, 1)
                v.wait_ge(mixed, t + 1)

            def raw_kk(j):
                v.tensor_scalar(m["kk"][:, j, :], m["k"][:, j, :], core.col("k_k", j), None,
                                ALU.mult).then_inc(kk_raw, 1)

            for t in range(6):
                mix_shift(t)
                if t >= 2:
                    raw_kk(t - 2)
            for j in range(PAIRS):
                v.wait_ge(lora_taken, 2 * j + 1)
                v.tensor_scalar(m["ld"][:, j, :], sig[:, j % 2, :], -EXP_HALF, None, ALU.mult).then_inc(sig_used, 1)
                v.wait_ge(sig_used, j + 1)
                v.tensor_tensor_scan(m["cum"][:, j, :], chunk_ones, m["ld"][:, j, :], 0.0, ALU.mult, ALU.add)
            def finish_kk(j):
                a, k, kk = m["nb"][:, j, :], m["k"][:, j, :], m["kk"][:, j, :]
                v.wait_ge(lora_taken, 2 * j + 2)
                link(v.tensor_scalar(ka[:, 0, :], a, core.col("k_a", j), core.one_minus_ka[:, j:j + 1], ALU.mult, ALU.add))
                v.tensor_tensor(k, k, ka[:, 0, :], ALU.mult)
                v.wait_ge(norm_rooted, j + 1)
                link(v.tensor_scalar(sq[:, j, :], sq[:, j, :], 1e-12, None, ALU.max))
                link(v.reciprocal(ka[:, 1, :], sq[:, j, :]))
                link(v.tensor_tensor(kk, kk, ka[:, 1, :], ALU.mult))
                link(v.scalar_tensor_tensor(out=a, in0=kk, scalar=-1.0, in1=a, op0=ALU.mult, op1=ALU.mult))
                mid = by_chunk(m["cum"][:, j, :])[:, :, P // 2 - 1:P // 2].to_broadcast([P, NB, P])
                link(v.tensor_tensor(by_chunk(e_mid[:, j % 2, :]), by_chunk(m["cum"][:, j, :]), mid, ALU.subtract))
                v.tensor_tensor(e_prev[:, j % 2, :], e_mid[:, j % 2, :], m["ld"][:, j, :], ALU.subtract).then_inc(decay_diff, 1)

            def decayed(j):
                r, k, kk, a = (m[name][:, j, :] for name in ("r", "k", "kk", "nb"))
                v.wait_ge(decay_exp, j + 1)
                v.tensor_copy(core.exp_last[:, j, :], by_chunk(e_mid[:, j % 2, :])[:, :, P - 1])
                v.tensor_tensor(kk, kk, e_prev[:, j % 2, :], ALU.mult)
                v.tensor_tensor(a, a, e_inv[:, j % 2, :], ALU.mult)
                link(v.scalar_tensor_tensor(out=m["cum"][:, j, :], in0=r, scalar=core.col("r_k", j), in1=k, op0=ALU.mult,
                                            op1=ALU.mult))
                v.tensor_tensor(r, r, e_mid[:, j % 2, :], ALU.mult)
                link(v.tensor_tensor(k, k, e_inv[:, j % 2, :], ALU.mult))

            for t in range(6, n_rw):
                mix_shift(t)
                if t >= 12:
                    finish_kk(t - 12)
                if t == 13:
                    decayed(0)
            for j in range(12):
                v.wait_ge(cols_taken, n_rw + j + 1)
                if j < 4:
                    q = m["hq"][:, j, :]
                    v.scalar_tensor_tensor(out=q, in0=q, scalar=float(P) ** -0.5, in1=sig[:, j % 2, :], op0=ALU.mult,
                                           op1=ALU.mult).then_inc(hg_used, 1)
                    if j % 2:
                        finish_kk(2 + j // 2)
                        decayed(1 + j // 2)
                elif j < 8:
                    h = j - 4
                    v.tensor_scalar(m["hcum"][:, h, :], sig[:, j % 2, :], core.one_minus_lb[:, h:h + 1],
                                    core.lb[:, h:h + 1], ALU.mult, ALU.add).then_inc(hg_used, 1)
                    v.wait_ge(hg_used, j + 1)
                    v.tensor_scalar(m["hk"][:, h, :], m["hcum"][:, h, :], -1.0, 1.0, ALU.mult,
                                    ALU.add).then_inc(f_ready, 1)
                else:
                    g = m["hgo"][:, j - 8, :]
                    v.scalar_tensor_tensor(out=g, in0=g, scalar=core.col("hg_norm", j - 8), in1=sig[:, j % 2, :],
                                           op0=ALU.mult, op1=ALU.mult).then_inc(hg_used, 1)
            decayed(3)
            v.wait_ge(ln_ready, 1)
            for h in range(HG_HEADS):
                ins = v.tensor_tensor_scan(m["hcum"][:, h, :], chunk_ones, ln_f[:, h, :], 0.0, ALU.mult, ALU.add)
            link(ins)


def mix(core, w_in_strips):
    nc = core.nc
    m = mixer_inputs(core)
    bank = core.bank

    def tile(at, n=1, inner=P):
        return core.slots(at, n, inner)

    scores = core.slots(57, 8, P).rearrange("p (h a) t -> p h a t", a=4)
    x_t, x_n = tile(65, 2), tile(67, 2)
    y_sb = core.slots(69, 2).rearrange("p b (h t) -> p b h t", t=P)
    level_e = core.slots(71, 2).rearrange("p b (h t) -> p b h t", t=P)
    level_g = core.slots(73, 2).rearrange("p b (h t) -> p b h t", t=P)
    att_t, q_e, k_e, k_tok_h, state_h, v_h = (tile(s) for s in (75, 76, 77, 78, 79, 80))
    gate_w = [core.slots(at, 1, P) for at in (81, 82, 83, 93)]
    kr = core.slots(84, 2, P).rearrange("p (j a) t -> p j a t", a=2)
    k_s, b_s, k_tok, b_tok, v_tok, v_stage = (tile(s) for s in (86, 87, 88, 89, 90, 91))
    state = core.slots(92, 1, RH)[:, 0:PAIRS, :]
    state_0 = core.slots(92, 1, RH)[:, PAIRS:2 * PAIRS, :]
    rhs = core.slots(91, 1, RH)
    u = core.slots(94, 1, RH)
    e_inter, k_stage = tile(95), tile(96)

    per = dict(staged=4, kr_staged=1, tok_ready=4, tok_taken=4, scores_ready=PAIRS,
               scores_taken=PAIRS, xt_first=2, x_first=2, x_first_taken=2, hg_diff=len(LEVELS), hg_exp=len(LEVELS),
               hg_scaled=len(LEVELS), hg_scores=len(LEVELS) + 1, hg_att=len(LEVELS) + 1, inter_diff=1, inter_exp=1,
               inter_scaled=1, rhs_ready=1, rhs_taken=1, u_ready=1, u_taken=1, out_ready=1, hg_out=2, state_ready=1)
    s = {n: core.sem("mix_" + n) for n in per}
    gate_loaded = [core.sem(f"mix_gate_weights_loaded{t}") for t in range(2)]
    gate_summed = core.sem("mix_gate_summed")
    gate_kept = core.sem("mix_gate_kept")
    wait_carrier = core.sem("mix_wait_carrier")
    act_carrier = core.sem("mix_scalar_wait_carrier")
    vector_link = core.sem("mix_vector_link")

    def after(name, c, k):
        return c * per[name] + k

    inv_y = [core.sem(f"mix_inverse_y{i}") for i in range(2)]
    inv_y_taken = [core.sem(f"mix_inverse_y_taken{i}") for i in range(2)]
    inv_z = [core.sem(f"mix_inverse_z{i}") for i in range(2)]
    inv_done = [core.sem(f"mix_inverse_updated{i}") for i in range(2)]
    first_state = core.sem("mix_first_state")
    pe_end = core.sem("mix_tensor_chunk_end")
    act_end = core.sem("mix_scalar_chunk_end")
    dve_end = core.sem("mix_vector_chunk_end")

    n_inv = len(LEVELS) - 1
    inv_level = [len(LEVELS) - 2 - i for i in range(n_inv)]
    head_bank = {"y": (2, 5), "z": (3, 6), "zt": (4, 7)}

    def waited(v):
        v.sem_inc(wait_carrier, 1)

    def halves(ap, level):
        return ap.rearrange("p h (b two n) -> p h b two n", two=2, n=LEVELS[level])

    def side(ap, i, which):
        return ap.rearrange("p (b two n) -> p b two n", two=2, n=LEVELS[inv_level[i]])[:, :, which, :]

    def sides(ap, i, which):
        return halves(ap, inv_level[i])[:, :, :, which, :]

    def heads_of(bank_ap):
        return bank_ap[:].rearrange("p (h t) -> p h t", t=P)

    with nc.Block() as block:
        @block.sync
        def _(sp):
            for c in range(NB):
                for t in range(2):
                    if c:
                        sp.wait_ge(gate_summed, 2 * (c - 1) + t + 1)
                    for i in range(2):
                        sp.dma_start(gate_w[2 * t + i], w_in_strips[GATE_STRIPS[2 * c + 1]][:, 4 * i:4 * i + 4, t * P:(t + 1) * P],
                                     ).then_inc(gate_loaded[t], 16)

        @block.gpsimd
        def _(gp):
            gp.memset(core.slots(92, 1), 0.0)
            gp.memset(state_h, 0.0).then_inc(first_state, 1)

        @block.scalar
        def _(act):
            act.nop().then_inc(act_end, 1)

            def stage(which):
                at = bass.ds(which * P, P)
                act.activation(k_s, m["k"][:, :, at], ACT.Copy).then_inc(s["staged"], 1)
                act.activation(b_s, m["nb"][:, :, at], ACT.Copy).then_inc(s["staged"], 1)
                act.activation(k_stage, m["hk"][:, :, at], ACT.Copy).then_inc(s["staged"], 1)
                act.activation(v_h, m["vh"][:, bass.ds(which, 1), :], ACT.Copy)
                act.activation(v_stage, m["v"][:, :, at], ACT.Copy).then_inc(s["staged"], 1)

            stage(0)
            with act.Fori(0, NB) as c:
                act.wait_ge(pe_end, c + 1)
                act.wait_ge(dve_end, c + 1)
                act.wait_ge(act_end, c + 1)
                now = bass.ds(c * P, P)
                def level_exp(i):
                    act.wait_ge(s["hg_diff"], after("hg_diff", c, i))
                    act.activation(level_e[:, i % 2], level_e[:, i % 2], ACT.Exp).then_inc(s["hg_exp"], 1)

                level_exp(1)
                act.activation(e_inter, m["hcum"][:, :, now], ACT.Exp)
                act.wait_ge(s["inter_diff"], after("inter_diff", c, 1))
                act.activation(k_e, k_e, ACT.Exp).then_inc(s["inter_exp"], 1)
                level_exp(2)
                for i, (to, b) in enumerate(((k_tok, 7), (b_tok, 6), (v_tok, 6), (k_tok_h, 7))):
                    act.wait_ge(s["tok_ready"], after("tok_ready", c, i + 1))
                    act.activation(to, heads_of(bank[b]), ACT.Copy).then_inc(s["tok_taken"], 1)
                for b in range(2):
                    act.wait_ge(s["x_first"], after("x_first", c, b + 1))
                    act.activation(x_n[:, 4 * b:4 * b + 4, :], heads_of(bank[head_bank["z"][b]]),
                                   ACT.Copy).then_inc(s["x_first_taken"], 1)
                for i in range(n_inv):
                    for b in range(2):
                        if i == 4 and b == 0:
                            act.wait_ge(gate_summed, 2 * c + 1)
                            act.sem_inc(act_carrier, 1)
                            act.activation(m["k"][:, :, now], heads_of(bank[1]), ACT.Copy).then_inc(gate_kept, 1)
                        act.wait_ge(inv_y[b], c * n_inv + i + 1)
                        act.activation(sides(y_sb[:, b], i, 0), sides(heads_of(bank[head_bank["y"][b]]), i, 0),
                                       ACT.Copy).then_inc(inv_y_taken[b], 1)
                    if i + 3 <= len(LEVELS):
                        level_exp(i + 3)
                act.wait_ge(s["rhs_ready"], after("rhs_ready", c, 1))
                for e in range(2):
                    ins = act.activation(rhs[:, 4 * e:4 * e + 4, :],
                                         bank[(2, 5)[e]][:, 0:PAIRS * RH].rearrange("p (j v) -> p j v", v=RH), ACT.Copy)
                ins.then_inc(s["rhs_taken"], 1)
                act.wait_ge(s["u_ready"], after("u_ready", c, 1))
                act.activation(u, bank[3][:].rearrange("p (h v) -> p h v", v=RH), ACT.Copy).then_inc(s["u_taken"], 1)
                act.wait_ge(gate_summed, 2 * c + 2)
                act.sem_inc(act_carrier, 1)
                act.activation(m["r"][:, :, now], heads_of(bank[1]), ACT.Copy).then_inc(gate_kept, 1)
                stage((c + 1) % NB)
                act.wait_ge(s["hg_out"], after("hg_out", c, 1))
                act.activation(m["hq"][:, :, now], heads_of(bank[0]), ACT.Copy)
                act.wait_ge(s["out_ready"], after("out_ready", c, 1))
                act.activation(m["ld"][:, :, now], heads_of(bank[4]), ACT.Copy).then_inc(act_end, 1)

        @block.vector
        def _(v):
            link = Link(v, vector_link)
            v.memset(core.slots(57, 8), 0.0)
            v.memset(core.slots(69, 2), 0.0)
            v.wait_ge(first_state, 1)
            v.nop().then_inc(dve_end, 1)
            with v.Fori(0, NB) as c:
                v.wait_ge(pe_end, c + 1)
                v.wait_ge(act_end, c + 1)
                v.wait_ge(dve_end, c + 1)
                now = bass.ds(c * P, P)
                hcum = m["hcum"][:, :, now]
                full = [P, PAIRS, P]

                def level_diff(i):
                    b, out = halves(hcum, i - 1), halves(level_e[:, i % 2], i - 1)
                    n = LEVELS[i - 1]
                    edge = b[:, :, :, 0, n - 1:n].to_broadcast([P, HG_HEADS, P // (2 * n), n])
                    v.tensor_tensor(out[:, :, :, 0, :], edge, b[:, :, :, 0, :], ALU.subtract)
                    v.tensor_tensor(out[:, :, :, 1, :], b[:, :, :, 1, :], edge, ALU.subtract).then_inc(s["hg_diff"], 1)

                def level_scale(i):
                    v.wait_ge(s["hg_exp"], after("hg_exp", c, i))
                    e, g = halves(level_e[:, i % 2], i - 1), halves(level_g[:, i % 2], i - 1)
                    k, q = halves(m["hk"][:, :, now], i - 1), halves(m["hq"][:, :, now], i - 1)
                    v.tensor_tensor(g[:, :, :, 0, :], e[:, :, :, 0, :], k[:, :, :, 0, :], ALU.mult)
                    v.tensor_tensor(g[:, :, :, 1, :], e[:, :, :, 1, :], q[:, :, :, 1, :],
                                    ALU.mult).then_inc(s["hg_scaled"], 1)

                def level_keep(i):
                    v.wait_ge(s["hg_att"], after("hg_att", c, i))
                    v.wait_ge(s["hg_scores"], after("hg_scores", c, i + 1))
                    waited(v)
                    mask = core.mask_t[:, i - 1:i, :].bitcast(I32).to_broadcast([P, HG_HEADS, P])
                    v.copy_predicated(att_t, mask, heads_of(bank[0])).then_inc(s["hg_att"], 1)

                v.tensor_copy(kr[:, :, 0, :], m["kk"][:, :, now])
                v.tensor_copy(kr[:, :, 1, :], m["r"][:, :, now]).then_inc(s["kr_staged"], 1)
                level_diff(1)
                last = m["hcum"][:, :, bass.ds(c * P + P - 1, 1)].to_broadcast(full)
                v.tensor_tensor(k_e, last, hcum, ALU.subtract).then_inc(s["inter_diff"], 1)
                level_diff(2)
                v.tensor_tensor(state_0, state, core.exp_mid[:, :, bass.ds(c, 1)].to_broadcast([P, PAIRS, RH]), ALU.mult)
                level_scale(1)
                v.wait_ge(s["inter_exp"], after("inter_exp", c, 1))
                v.tensor_tensor(q_e, m["hq"][:, :, now], e_inter, ALU.mult)
                v.tensor_tensor(k_e, k_e, m["hk"][:, :, now], ALU.mult).then_inc(s["inter_scaled"], 1)
                for j in range(PAIRS):
                    v.wait_ge(s["scores_ready"], after("scores_ready", c, j + 1))
                    waited(v)
                    mask = core.causal.rearrange("p a t -> p (a t)").bitcast(I32).unsqueeze(1).to_broadcast([P, 2, 2 * P])
                    for e in range(2):
                        ins = v.copy_predicated(scores[:, 2 * j + e].rearrange("p (b a) t -> p b (a t)", b=2), mask,
                                                bank[2 + 2 * (j % 2) + e][:].rearrange("p (b a) -> p b a", b=2))
                    ins.then_inc(s["scores_taken"], 1)
                    if j == 0:
                        v.wait_ge(s["hg_scores"], after("hg_scores", c, 1))
                        v.tensor_tensor(att_t, heads_of(bank[0]), core.ident.unsqueeze(1).to_broadcast([P, HG_HEADS, P]),
                                        ALU.mult).then_inc(s["hg_att"], 1)
                    if j % 2 == 1:
                        heads = slice(2 * (j - 1), 2 * (j + 1))
                        v.wait_ge(s["scores_taken"], after("scores_taken", c, j + 1))
                        mask1 = core.mask_t[:, len(LEVELS) - 1:len(LEVELS), :].to_broadcast([P, 4, P])
                        link(v.tensor_tensor(x_t[:, heads, :], scores[:, heads, 0, :], mask1, ALU.mult))
                        v.tensor_tensor(x_t[:, heads, :], x_t[:, heads, :],
                                        core.ident.unsqueeze(1).to_broadcast([P, 4, P]), ALU.add).then_inc(s["xt_first"], 1)
                for i in range(n_inv):
                    if i + 2 <= len(LEVELS):
                        level_scale(i + 2)
                    if i + 3 <= len(LEVELS):
                        level_diff(i + 3)
                    level_keep(i + 1)
                    lv = inv_level[i]
                    half = [P, 4, P // (2 * LEVELS[lv]), LEVELS[lv]]
                    for b in range(2):
                        heads = slice(4 * b, 4 * b + 4)
                        v.wait_ge(inv_z[b], c * n_inv + i + 1)
                        waited(v)
                        if i < n_inv - 1:
                            v.copy_predicated(sides(x_n[:, heads, :], i, 0),
                                              sides(core.mask_n[:, lv:lv + 1, :].bitcast(I32), i, 0).to_broadcast(half),
                                              sides(heads_of(bank[head_bank["z"][b]]), i, 0))
                        v.copy_predicated(sides(x_t[:, heads, :], i, 1),
                                          sides(core.mask_t[:, lv:lv + 1, :].bitcast(I32), i, 1).to_broadcast(half),
                                          sides(heads_of(bank[head_bank["zt"][b]]), i, 1)).then_inc(inv_done[b], 1)
                level_keep(len(LEVELS))
                v.wait_ge(s["hg_out"], after("hg_out", c, 2))
                for h in range(HG_HEADS):
                    v.scalar_tensor_tensor(out=state_h[:, h, :], in0=state_h[:, h, :], scalar=e_inter[:, h, P - 1:P],
                                           in1=heads_of(bank[7])[:, h, :], op0=ALU.mult, op1=ALU.add)
                v.wait_ge(s["state_ready"], after("state_ready", c, 1))
                link(v.tensor_tensor(state, state_0, bank[6][:, 0:PAIRS * RH].rearrange("p (j v) -> p j v", v=RH), ALU.add))
                v.tensor_tensor(state, state, core.exp_last[:, :, bass.ds(c, 1)].to_broadcast([P, PAIRS, RH]),
                                ALU.mult).then_inc(dve_end, 1)
                link.restart()

        @block.tensor
        def _(pe):
            pe.wait_ge(first_state, 1)
            pe.nop().then_inc(pe_end, 1)
            with pe.Fori(0, NB) as c:
                pe.wait_ge(act_end, c + 1)
                pe.wait_ge(dve_end, c + 1)
                pe.wait_ge(pe_end, c + 1)
                now = bass.ds(c * P, P)

                def turn(src, to):
                    for j in range(4):
                        ins = pe.transpose(bank[to][:, j * P:(j + 1) * P], src[:, j, :], core.ident)
                    ins.then_inc(s["tok_ready"], 1)

                def gate_product(g):
                    t, k = g // KD, g % KD
                    if k == 0:
                        pe.wait_ge(gate_loaded[t], 32 * (c + 1))
                    if g == KD:
                        pe.wait_ge(gate_kept, 2 * c + 1)
                    ins = pe.matmul(bank[1][:], gate_w[g // 4][:, g % 4, :], m["h_t"][:, k, :], start=(k == 0), stop=(k == KD - 1))
                    if k == KD - 1:
                        ins.then_inc(gate_summed, 1)

                def level_scores(i):
                    pe.wait_ge(s["hg_scaled"], after("hg_scaled", c, i))
                    pe.wait_ge(s["hg_att"], after("hg_att", c, i))
                    for h in range(HG_HEADS):
                        g = level_g[:, i % 2, h, :]
                        ins = pe.matmul(bank[0][:, h * P:(h + 1) * P], g, g, start=True, stop=True)
                    ins.then_inc(s["hg_scores"], 1)

                def scores_of(j):
                    if j >= 2:
                        pe.wait_ge(s["scores_taken"], after("scores_taken", c, j - 1))
                    for e in range(2):
                        rows = slice(RH * e, RH * (e + 1))
                        to = bank[2 + 2 * (j % 2) + e]
                        both = kr[rows, j].rearrange("p a t -> p (a t)")
                        pe.matmul(to[:, 0:2 * P], b_s[rows, j, :], both, start=True, stop=True)
                        ins = pe.matmul(to[:, 2 * P:4 * P], k_s[rows, j, :], both, start=True, stop=True)
                    ins.then_inc(s["scores_ready"], 1)

                pe.wait_ge(s["staged"], after("staged", c, 1))
                turn(k_s, 7)
                pe.wait_ge(s["staged"], after("staged", c, 2))
                turn(b_s, 6)
                pe.wait_ge(s["staged"], after("staged", c, 3))
                for h in range(HG_HEADS):
                    ins = pe.matmul(bank[0][:, h * P:(h + 1) * P], k_stage[:, h, :], m["hq"][:, h, now], start=True, stop=True)
                ins.then_inc(s["hg_scores"], 1)
                pe.wait_ge(s["kr_staged"], after("kr_staged", c, 1))
                scores_of(0)
                scores_of(1)
                scores_of(2)
                scores_of(3)
                pe.wait_ge(s["staged"], after("staged", c, 4))
                pe.wait_ge(s["tok_taken"], after("tok_taken", c, 2))
                turn(v_stage, 6)
                pe.wait_ge(s["inter_scaled"], after("inter_scaled", c, 1))
                pe.wait_ge(s["tok_taken"], after("tok_taken", c, 1))
                turn(k_e, 7)
                for b in range(2):
                    pe.wait_ge(s["xt_first"], after("xt_first", c, b + 1))
                    pe.wait_ge(s["scores_taken"], after("scores_taken", c, 3 + b))
                    pe.wait_ge(s["tok_taken"], after("tok_taken", c, 3))
                    for j in range(4):
                        ins = pe.transpose(bank[head_bank["z"][b]][:, j * P:(j + 1) * P], x_t[:, 4 * b + j, :], core.ident)
                    ins.then_inc(s["x_first"], 1)
                pe.wait_ge(s["scores_taken"], after("scores_taken", c, PAIRS))
                pe.wait_ge(s["tok_taken"], after("tok_taken", c, 4))
                for i in range(n_inv):
                    for b in range(2):
                        if i == 0:
                            pe.wait_ge(s["x_first_taken"], after("x_first_taken", c, b + 1))
                        else:
                            pe.wait_ge(inv_done[b], c * n_inv + i)
                        for j in range(4):
                            h = 4 * b + j
                            ins = pe.matmul(side(bank[head_bank["y"][b]][:, j * P:(j + 1) * P], i, 0), scores[:, h, 0, :],
                                            side(x_n[:, h, :], i, 0), start=True, stop=True)
                        ins.then_inc(inv_y[b], 1)
                    level_scores(i + 1)
                    gate_product(2 * i)
                    for b in range(2):
                        pe.wait_ge(inv_y_taken[b], c * n_inv + i + 1)
                        for j in range(4):
                            h = 4 * b + j
                            if i < n_inv - 1:
                                pe.matmul(side(bank[head_bank["z"][b]][:, j * P:(j + 1) * P], i, 0), x_t[:, h, :],
                                          side(y_sb[:, b, j, :], i, 0), start=True, stop=True)
                            ins = pe.matmul(side(bank[head_bank["zt"][b]][:, j * P:(j + 1) * P], i, 1), y_sb[:, b, j, :],
                                            side(x_t[:, h, :], i, 1), start=True, stop=True)
                        ins.then_inc(inv_z[b], 1)
                    gate_product(2 * i + 1)
                level_scores(len(LEVELS))
                for e in range(2):
                    rows = slice(RH * e, RH * (e + 1))
                    for j in range(PAIRS):
                        h = 2 * j + e
                        to = bank[(2, 5)[e]][:, j * RH:(j + 1) * RH]
                        pe.matmul(to, kr[rows, j, 0, :], state_0[rows, j, :], start=True, stop=False)
                        ins = pe.matmul(to, scores[:, h, 2, :], v_tok.rearrange("p j v -> p (j v)")[:, h * RH:(h + 1) * RH],
                                        start=False, stop=True)
                ins.then_inc(s["rhs_ready"], 1)
                pe.wait_ge(s["hg_att"], after("hg_att", c, len(LEVELS) + 1))
                for h in range(HG_HEADS):
                    to = bank[0][:, h * P:(h + 1) * P]
                    pe.matmul(to, v_h[:, h, :], att_t[:, h, :], start=True, stop=False)
                    ins = pe.matmul(to, state_h[:, h, :], q_e[:, h, :], start=False, stop=True)
                ins.then_inc(s["hg_out"], 1)
                gate_product(12)
                gate_product(13)
                pe.wait_ge(inv_done[1], c * n_inv + n_inv)
                for h in range(HG_HEADS):
                    ins = pe.matmul(bank[7][:, h * P:(h + 1) * P], k_tok_h[:, h, :], v_h[:, h, :], start=True, stop=True)
                ins.then_inc(s["hg_out"], 1)
                pe.wait_ge(s["rhs_taken"], after("rhs_taken", c, 1))
                pe.wait_ge(inv_done[0], c * n_inv + n_inv)
                for h in range(RW_HEADS):
                    ins = pe.matmul(bank[3][:, h * RH:(h + 1) * RH], x_t[:, h, :], rhs[:, PAIRS * (h % 2) + h // 2, :],
                                    start=True, stop=True)
                ins.then_inc(s["u_ready"], 1)
                gate_product(14)
                gate_product(15)
                pe.wait_ge(s["u_taken"], after("u_taken", c, 1))
                v_heads = v_tok.rearrange("p j v -> p (j v)")
                for e in range(2):
                    rows = slice(RH * e, RH * (e + 1))
                    for j in range(PAIRS):
                        h = 2 * j + e
                        to = bank[6][rows, j * RH:(j + 1) * RH]
                        pe.matmul(to, k_tok[:, j, rows], v_heads[:, h * RH:(h + 1) * RH], start=True, stop=False)
                        ins = pe.matmul(to, b_tok[:, j, rows], u[:, h, :], start=False, stop=True)
                ins.then_inc(s["state_ready"], 1)
                for e in range(2):
                    rows = slice(RH * e, RH * (e + 1))
                    for j in range(PAIRS):
                        h = 2 * j + e
                        to = bank[4][rows, j * P:(j + 1) * P]
                        pe.matmul(to, v_heads[:, h * RH:(h + 1) * RH], scores[:, h, 3, :], start=True, stop=False)
                        pe.matmul(to, u[:, h, :], scores[:, h, 1, :], start=False, stop=False)
                        ins = pe.matmul(to, state_0[rows, j, :], kr[rows, j, 1, :], start=False, stop=True)
                ins.then_inc(s["out_ready"], 1)
                pe.nop().then_inc(pe_end, 1)


def finish(core, x, w_in_strips, g2, w_branch_hg, w_branch_rw, w_out, norm_ffn, wq):
    nc = core.nc
    m = mixer_inputs(core)
    bank = core.bank
    gates_0 = core.slots(51, 4, P)
    gates_rest = core.slots(35, 12, SEQ - P)
    gates_rest_by_block = core.slots(35, 12, P)
    ring = [core.slots(57 + 2 * i, 2, P) for i in range(2)]
    yc, y_sq, y_root, y_inv, rk, out, o_sq, o_root, g2_all, g2_now = (core.slots(s, 1)[:, 0, :] for s in range(65, 75))
    g2_now = g2_now[:, 0:P]
    w_branch = [core.slots(75 + 4 * i, 4, STRIP) for i in range(4)]
    norm_row = core.slots(95, 2, D)[:, 0, :]
    merged = core.slots(55, 2, P)
    w_out_sb = core.slots(0, 16, D)
    x2 = core.slots(41, 8, D)[:, X2_AT[0], :]
    wq_sb = core.slots(57, 16, D)
    h_tok, h_t, q_t = core.slots(33, 2, D)[:, 0, :], core.slots(73, 2, P), core.slots(49, 8)[:, :, 0:P]
    junk = core.slots(73, 2, D)[:, 0, :]
    ssq, mean, root, rstd = (core.stats[:, i:i + 1] for i in range(4))

    strip_loaded = [core.sem(f"gate_strip_loaded{i}") for i in range(2)]
    g2_loaded = core.sem("g2_loaded")
    weights = core.sem("branch_weights_loaded")
    w_out_loaded = core.sem("w_out_loaded")
    x_loaded = core.sem("x_reloaded")
    wq_loaded = core.sem("wq_loaded")
    y_mean = core.sem("y_mean_summed")
    centred = core.sem("y_centred")
    y_squared = core.sem("y_squared")
    y_var = core.sem("y_variance_summed")
    rooting = core.sem("variances_ready")
    rooted = core.sem("variances_rooted")
    o_squared = core.sem("o_squared")
    o_sum = core.sem("o_squares_summed")
    rk_sum = core.sem("rk_summed")
    g2_staged = core.sem("g2_staged")
    g_ready = core.sem("g_ready")
    y_done = core.sem("y_done")
    gates_ready = core.sem("gates_ready")
    gates_taken = core.sem("gates_taken")
    branch_ready = core.sem("branch_ready")
    branch_used = core.sem("branch_used")
    merged_ready = core.sem("merged_ready")
    out_ready = core.sem("w_out_summed")
    x2_ready = core.sem("x2_ready")
    squares = core.sem("x2_squares_summed")
    ms_ready = core.sem("x2_mean_squares_ready")
    x2_rooted = core.sem("x2_rooted")
    h_ready = core.sem("ffn_input_ready")
    turned = core.sem("ffn_input_turned")
    turned_taken = core.sem("ffn_input_turned_taken")
    q_ready = core.sem("queries_ready")
    v_link = core.sem("finish_vector_link")

    with nc.Block() as block:
        @block.sync
        def _(sp):
            sp.dma_start(g2_all, g2).then_inc(g2_loaded, 16)
            for n in range(2 * PAIRS):
                if n >= 2:
                    sp.wait_ge(gates_ready, n - 1)
                sp.dma_start(ring[n % 2], w_in_strips[GATE_STRIPS[n - n % 2]][:, :, (n % 2) * P:(n % 2 + 1) * P],
                             ).then_inc(strip_loaded[n % 2], 16)
                if n == 1:
                    for i in range(4):
                        for which, w in ((0, w_branch_hg), (1, w_branch_rw)):
                            sp.dma_start(w_branch[i][:, 4 * which:4 * which + 4, :],
                                         w.rearrange("(k p) n -> p k n", p=P)[:, :, i * STRIP:(i + 1) * STRIP],
                                         ).then_inc(weights, 16)
                    sp.dma_start(norm_row, norm_ffn.partition_broadcast(P)).then_inc(weights, 16)
            sp.wait_ge(y_done, PAIRS + 1)
            sp.wait_ge(gates_ready, 2 * PAIRS)
            sp.wait_ge(gates_taken, 4 * PAIRS + 4)
            sp.dma_start(x2, x[0:P, :]).then_inc(x_loaded, 16)
            sp.dma_start(w_out_sb, w_out.rearrange("(k p) n -> p k n", p=P)).then_inc(w_out_loaded, 16)
            sp.dma_start(wq_sb, wq.rearrange("(k p) n -> p k n", p=P)).then_inc(wq_loaded, 16)

        @block.tensor
        def _(pe):
            pe.wait_ge(g2_loaded, 16)
            with pe.Fori(0, PAIRS) as j:
                one = bass.ds(j, 1)

                def gate_tile(b):
                    pe.wait_ge(strip_loaded[b], 16 * (j + 1))
                    pe.wait_ge(gates_taken, 4 * j + b - 3 + 4)
                    for k in range(KD):
                        ins = pe.matmul(bank[b][:], ring[b][:, k, :], m["h_t"][:, k, :], start=(k == 0), stop=(k == KD - 1))
                    ins.then_inc(gates_ready, 1)

                pe.wait_ge(y_done, j + 1)
                pe.matmul(bank[4][:], core.ones_pair, m["ld"][:, one, :], start=True, stop=True).then_inc(y_mean, 1)
                pe.matmul(bank[5][:], core.ones_pair, m["cum"][:, one, :], start=True, stop=True).then_inc(rk_sum, 1)
                pe.wait_ge(g2_staged, j + 1)
                pe.matmul(bank[6][:], g2_now, m["sgd"], start=True, stop=True).then_inc(g_ready, 1)
                pe.wait_ge(o_squared, j + 1)
                pe.matmul(bank[7][:], core.ones_full, o_sq, start=True, stop=True).then_inc(o_sum, 1)
                pe.wait_ge(y_squared, j + 1)
                pe.matmul(bank[4][:], core.ones_pair, y_sq, start=True, stop=True).then_inc(y_var, 1)
                gate_tile(0)
                gate_tile(1)
            pe.wait_ge(weights, 144)
            pe.wait_ge(y_done, PAIRS + 1)
            pe.wait_ge(gates_taken, 4 * PAIRS + 4)
            for t in range(KD):
                if t >= 2:
                    pe.wait_ge(branch_used, 2 * (t - 1))
                for which, y in ((0, m["hq"]), (1, m["ld"])):
                    for k in range(4):
                        ins = pe.matmul(bank[2 * (t % 2) + which][:, 0:P],
                                        w_branch[t // 2][:, 4 * which + k, (t % 2) * P:(t % 2 + 1) * P], y[:, k, 0:P],
                                        start=(k == 0), stop=(k == 3))
                    ins.then_inc(branch_ready, 1)
            pe.wait_ge(w_out_loaded, 16)
            for half in range(2):
                for k in range(KD):
                    pe.wait_ge(merged_ready, k + 1)
                    ins = pe.matmul(bank[4 + half][:], merged[:, k, :], w_out_sb[:, k, half * 512:(half + 1) * 512],
                                    start=(k == 0), stop=(k == KD - 1))
                ins.then_inc(out_ready, 1)
            pe.wait_ge(h_ready, 1)
            for half in range(2):
                for k in range(4):
                    dk = 4 * half + k
                    ins = pe.transpose(bank[6 + half][:, k * P:(k + 1) * P], h_tok[:, dk * P:(dk + 1) * P], core.ident)
                ins.then_inc(turned, 1)
            pe.wait_ge(wq_loaded, 16)
            for h in range(2):
                if h == 0:
                    pe.wait_ge(branch_used, 16)
                for k in range(KD):
                    if h == 0 and k % 4 == 0:
                        pe.wait_ge(turned_taken, 1 + k // 4)
                    ins = pe.matmul(bank[h % 2][:, 0:P], wq_sb[:, k, h * P:(h + 1) * P], h_t[:, k, :], start=(k == 0),
                                    stop=(k == KD - 1))
                ins.then_inc(q_ready, 1)

        @block.scalar
        def _(act):
            act.wait_ge(g2_loaded, 16)
            act.nop().then_inc(gates_taken, 4)
            with act.Fori(0, PAIRS) as j:
                one = bass.ds(j, 1)
                act.wait_ge(y_done, j + 1)
                act.activation(g2_now, g2_all[:, bass.ds(j * P, P)], ACT.Copy).then_inc(g2_staged, 1)
                act.activation(o_sq, m["hq"][:, one, :], ACT.Square).then_inc(o_squared, 1)
                act.wait_ge(centred, j + 1)
                act.activation(y_sq, yc, ACT.Square).then_inc(y_squared, 1)

                def gate(b):
                    if b < 2:
                        act.wait_ge(gates_ready, 2 * j + b + 1)
                        act.activation(gates_0[:, bass.ds(4 * j + b, 1), :], bank[b][:, 0:P], ACT.Sigmoid)
                        act.activation(gates_rest[:, bass.ds(4 * j + b, 1), :], bank[b][:, P:], ACT.Sigmoid).then_inc(gates_taken, 1)
                    else:
                        left = m["kr"[b - 2]][:, :, bass.ds(j * P, P)]
                        act.activation(gates_0[:, bass.ds(4 * j + b, 1), :], left[:, 0:1, :], ACT.Sigmoid)
                        act.activation(gates_rest_by_block[:, bass.ds(3 * (4 * j + b), 3), :], left[:, 1:, :],
                                       ACT.Sigmoid).then_inc(gates_taken, 1)

                act.wait_ge(rooting, 2 * j + 1)
                act.activation(o_root, o_root, ACT.Sqrt).then_inc(rooted, 1)
                act.wait_ge(rooting, 2 * j + 2)
                act.activation(y_root, y_root, ACT.Sqrt).then_inc(rooted, 1)
                gate(0)
                gate(1)
                gate(2)
                gate(3)
            act.wait_ge(x2_ready, 2)
            act.activation(junk, x2, ACT.Square, accum_out=ssq).then_inc(squares, 1)
            act.wait_ge(ms_ready, 1)
            act.activation(root, mean, ACT.Sqrt).then_inc(x2_rooted, 1)
            for half in range(2):
                act.wait_ge(turned, half + 1)
                act.activation(h_t[:, 4 * half:4 * half + 4, :], bank[6 + half][:].rearrange("p (k t) -> p k t", t=P),
                               ACT.Copy).then_inc(turned_taken, 1)
            for h in range(2):
                act.wait_ge(q_ready, h + 1)
                act.activation(q_t[:, h, :], bank[h % 2][:, 0:P], ACT.Copy).then_inc(turned_taken, 1)

        @block.vector
        def _(v):
            link = Link(v, v_link)
            v.nop().then_inc(y_done, 1)
            with v.Fori(0, PAIRS) as j:
                one = bass.ds(j, 1)

                def col(name):
                    return core.cols[:, bass.ds(j + COLS[name][0], 1)]

                y, o = m["ld"][:, one, :], m["hq"][:, one, :]
                v.wait_ge(y_mean, j + 1)
                v.scalar_tensor_tensor(out=yc, in0=bank[4][:], scalar=-1.0 / RH, in1=y, op0=ALU.mult,
                                       op1=ALU.add).then_inc(centred, 1)
                v.wait_ge(o_sum, j + 1)
                v.tensor_scalar(o_root, bank[7][:], 1.0 / P, EPS, ALU.mult, ALU.add).then_inc(rooting, 1)
                v.wait_ge(rk_sum, j + 1)
                link(v.tensor_tensor(rk, bank[5][:], m["v"][:, one, :], ALU.mult))
                v.wait_ge(y_var, j + 1)
                v.tensor_scalar(y_root, bank[4][:], 1.0 / RH, GN_EPS, ALU.mult, ALU.add).then_inc(rooting, 1)
                v.wait_ge(rooted, 2 * j + 1)
                link(v.reciprocal(y_inv, o_root))
                link(v.tensor_tensor(o, o, y_inv, ALU.mult))
                link(v.tensor_tensor(o, o, m["hgo"][:, one, :], ALU.mult))
                v.wait_ge(rooted, 2 * j + 2)
                link(v.reciprocal(y_inv, y_root))
                link(v.tensor_tensor(yc, yc, y_inv, ALU.mult))
                link(v.tensor_scalar(out, yc, col("ln_w"), col("ln_b"), ALU.mult, ALU.add))
                link(v.tensor_tensor(out, out, rk, ALU.add))
                v.wait_ge(g_ready, j + 1)
                link(v.tensor_tensor(y, out, bank[6][:], ALU.mult))
                v.sem_inc(y_done, 1)
                link.restart()
            v.wait_ge(gates_taken, 4 * PAIRS + 4)
            for t in range(KD):
                for which in range(2):
                    gate = gates_0[:, KD * which + t, :]
                    v.wait_ge(branch_ready, 2 * t + which + 1)
                    v.tensor_tensor(gate, bank[2 * (t % 2) + which][:, 0:P], gate, ALU.mult).then_inc(branch_used, 1)
                v.wait_ge(branch_used, 2 * t + 2)
                v.tensor_tensor(merged[:, t, :], gates_0[:, t, :], gates_0[:, KD + t, :], ALU.add).then_inc(merged_ready, 1)
            v.wait_ge(x_loaded, 16)
            for half in range(2):
                v.wait_ge(out_ready, half + 1)
                part = x2[:, half * 512:(half + 1) * 512]
                v.tensor_tensor(part, part, bank[4 + half][:], ALU.add).then_inc(x2_ready, 1)
            v.wait_ge(squares, 1)
            v.tensor_scalar(mean, ssq, 1.0 / D, EPS, ALU.mult, ALU.add).then_inc(ms_ready, 1)
            v.wait_ge(x2_rooted, 1)
            link(v.reciprocal(rstd, root))
            v.wait_ge(weights, 144)
            v.scalar_tensor_tensor(out=h_tok, in0=x2, scalar=rstd, in1=norm_row, op0=ALU.mult,
                                   op1=ALU.mult).then_inc(h_ready, 1)


def experts(core, x, w_out, wq, u_emb, v_emb, ple_gate, ple_proj, p_in, final_norm, out):
    nc = core.nc
    bank = core.bank
    m = mixer_inputs(core)
    turns = NB * PK_HEADS // 2
    per_block = PK_HEADS // 2
    picks = 2 * TOPK
    depth = 8
    diags = 4
    uses = picks // depth
    x2, h_tok, q_t = core.slots(41, 8, D), core.slots(33, 8, D), core.slots(49, 8)
    u_ring, v_ring = core.slots(0, 16, D), core.slots(57, 16, D)
    sc = core.slots(17, 1, N_KEYS)
    rest = core.slots(18, 1, N_KEYS)
    q_now = core.slots(19, 1, P)[:, 0:2, :]
    diag = core.slots(31, 1, P)
    onehot = core.arena[:, 91 * SLOT:91 * SLOT + picks * N_CAND]
    wq_sb, h_t0 = core.slots(57, 16, D), core.slots(73, 2, P)
    others = slice(P, SEQ)
    piece = [core.slots(75 + 4 * i, 4, STRIP) for i in range(4)]
    gates = core.slots(35, 12, SEQ - P)
    merged = gates[:, 0:KD, :]
    x_others = core.slots(41, 6, D)
    h_t = core.slots(20, 8)
    norm_row = core.slots(95, 2, D)[:, 0, :]
    junk = onehot[:, 0:D]
    mean, root, rstd = (core.stats[:, 4 * i:4 * i + 3] for i in range(3))
    ple_gate_sb, ple_proj_sb, p_sb = core.slots(75, 16, D), core.slots(20, 4, D), core.slots(24, 2, PLE)
    final_row = core.slots(26, 2, D)[:, 0, :]
    p_now, p_t = core.slots(32, 1, PLE)[:, 0, :], core.slots(32, 1, PLE)[:, 1, :].rearrange("p (k t) -> p k t", t=P)
    x_now = core.slots(73, 2, D)[:, 0, :]
    x_t = core.slots(95, 2, P)
    y_all = h_tok
    end_ssq, end_mean, end_root, end_rstd = (core.stats[:, 32 + i:33 + i] for i in range(4))
    ssq_3, mean_3, root_3, rstd_3 = (core.stats[:, 36 + i:37 + i] for i in range(4))
    at = 28 * SLOT

    def small(*shape, dt=F32):
        nonlocal at
        n = 1
        for d in shape:
            n *= d
        ap = core.arena[:, at:at + n]
        at += n
        if dt != F32:
            ap = ap.bitcast(dt)
        return ap if len(shape) == 1 else ap.rearrange("p (a b) -> p a b", b=shape[1])

    top, top_i, top_f = small(4, TOPK), small(4, TOPK, dt=U32), small(4, TOPK)
    cand, cand_id, cand_rest = small(2, N_CAND), small(2, N_CAND), small(2, N_CAND)
    best, best_i, best_f = small(2, TOPK), small(2, TOPK, dt=U32), small(2, TOPK)
    ids_f, shifted, weight = small(picks), small(2, TOPK), small(2, TOPK)
    total, inverse = small(2), small(2)
    gate_next, gate_now = small(2, TOPK), small(2, TOPK)
    ids = small(2, picks, dt=U32)
    dots, gelu, coef = small(2, TOPK), small(2, TOPK), small(2, TOPK)
    assert at <= 31 * SLOT

    ple_loaded = core.sem("ple_weights_loaded")
    u_loaded = [core.sem(f"u_row_loaded{i}") for i in range(depth)]
    v_loaded = [core.sem(f"v_row_loaded{i}") for i in range(depth)]
    u_used = core.sem("u_row_used")
    v_used = core.sem("v_row_used")
    q_staged = core.sem("query_staged")
    sc_ready = core.sem("key_scores_ready")
    sc_taken = core.sem("key_scores_taken")
    ids_ready = core.sem("ids_ready")
    shift_ready = core.sem("best_scores_shifted")
    exp_ready = core.sem("best_scores_exp")
    gelu_ready = core.sem("gelu_ready")
    coef_ready = core.sem("coefficients_ready")
    diag_ready = core.sem("diagonal_ready")
    acc_taken = core.sem("sum_taken")
    v_link = core.sem("experts_vector_link")
    carrier = core.sem("experts_gpsimd_wait_carrier")
    carrier_v = core.sem("experts_vector_wait_carrier")
    carrier_a = core.sem("experts_scalar_wait_carrier")
    branch_ready = core.sem("others_branch_ready")
    branch_used = core.sem("others_branch_used")
    merged_ready = core.sem("others_merged_ready")
    w_out_loaded = [core.sem(f"others_w_out_loaded{i}") for i in range(4)]
    wq_loaded = [core.sem(f"others_wq_loaded{i}") for i in range(4)]
    x_loaded = core.sem("others_x_loaded")
    out_ready = core.sem("others_w_out_summed")
    x2_ready = core.sem("others_x2_ready")
    squares = core.sem("others_squares_summed")
    ms_ready = core.sem("others_mean_squares_ready")
    rooted = core.sem("others_rooted")
    h_ready = core.sem("others_input_ready")
    turned = core.sem("others_input_turned")
    turned_taken = core.sem("others_input_turned_taken")
    q_ready = core.sem("others_queries_ready")
    q_taken = core.sem("others_queries_taken")
    v_added = core.sem("v_row_added_by_vector")
    q0_ready = core.sem("first_queries_ready")
    q0_taken = core.sem("first_queries_taken")
    end_free = core.sem("end_buffers_free")
    end_p_staged = core.sem("end_p_staged")
    end_staged = core.sem("end_x_staged")
    end_squared = core.sem("end_squares_summed")
    end_ms = core.sem("end_mean_square_ready")
    end_rooted = core.sem("end_rooted")
    end_rstd_ready = core.sem("end_rstd_ready")
    end_turned = core.sem("end_inputs_turned")
    end_turned_taken = core.sem("end_inputs_turned_taken")
    end_gate = core.sem("end_gate_summed")
    end_proj = core.sem("end_proj_summed")
    end_gated = core.sem("end_gated")
    end_x = core.sem("end_x_ready")
    end_y = core.sem("end_output_ready")
    stored = core.sem("end_output_stored")

    def vector_sums(n, k):
        return isinstance(n, int) and n == turns - 1 and k in VECTOR_ROWS

    def vector_count(k):
        return sum(row <= k for row in VECTOR_ROWS)

    def tensor_rows(n):
        return [k for k in range(picks) if not vector_sums(n, k)]

    def diagonal(n, k):
        return tensor_rows(n).index(k)

    def out_parts(q):
        return {2: range(0, 5), 3: range(5, 10), 4: range(10, 12)}.get(q, ())

    def query_heads(q):
        return {5: (0, 1), 6: (2, 3, 4), 7: (5, 6, 7)}.get(q, ())

    with nc.Block() as block:
        @block.sync
        def _(sp):
            for i in range(4):
                sp.wait_ge(branch_ready, 4 * (i + 1))
                sp.dma_start(piece[i], w_out.rearrange("(k p) n -> p k n", p=P)[:, :, i * STRIP:(i + 1) * STRIP],
                             ).then_inc(w_out_loaded[i], 16)
            sp.wait_ge(merged_ready, KD)
            sp.dma_start(x_others, x[P:, :].rearrange("(b p) d -> p b d", p=P)).then_inc(x_loaded, 16)
            for i in range(4):
                sp.wait_ge(out_ready, 3 * (i + 1))
                sp.dma_start(piece[i], wq.rearrange("(k p) n -> p k n", p=P)[:, :, i * STRIP:(i + 1) * STRIP],
                             ).then_inc(wq_loaded[i], 16)
            sp.wait_ge(q_ready, PK_HEADS)
            sp.dma_start(ple_gate_sb, ple_gate.rearrange("(k p) n -> p k n", p=P)).then_inc(ple_loaded, 16)
            sp.dma_start(ple_proj_sb, ple_proj.rearrange("(k p) n -> p k n", p=P)).then_inc(ple_loaded, 16)
            sp.dma_start(p_sb, p_in.rearrange("(b p) d -> p b d", p=P)).then_inc(ple_loaded, 16)
            sp.dma_start(final_row, final_norm.partition_broadcast(P)).then_inc(ple_loaded, 16)
            for b in range(NB):
                sp.wait_ge(end_y, b + 1)
                sp.dma_start(out[b * P:(b + 1) * P, :], y_all[:, b, :]).then_inc(stored, 16)
            sp.wait_ge(stored, 16 * NB)

        @block.gpsimd
        def _(gp):
            def gather(n, parity, half):
                for table, ring, loaded, used in ((u_emb, u_ring, u_loaded, u_used), (v_emb, v_ring, v_loaded, v_used)):
                    for k in range(half * TOPK, (half + 1) * TOPK):
                        gp.wait_ge(used, picks * n + k + 1)
                        gp.sem_inc(carrier, 1)
                        gp.indirect_dma_start(ring[:, k % depth, :], None, table,
                                              bass.IndirectOffsetOnAxis(ap=ids[:, parity, k:k + 1], axis=0),
                                              ).then_inc(loaded[k % depth], 16)

            with gp.Fori(0, turns, 2) as n:
                for parity in range(2):
                    gp.wait_ge(ids_ready, n + parity + 1)
                    gp.sem_inc(carrier, 1)
                    gather(n + parity, parity, 0)
                    gather(n + parity, parity, 1)

        @block.tensor
        def _(pe):

            def key_scores(n):
                pe.wait_ge(q_staged, n + 1)
                pe.wait_ge(sc_taken, n)
                for h in range(2):
                    ins = pe.matmul(bank[2][:, h * 2 * N_KEYS:(h + 1) * 2 * N_KEYS], q_now[:, h, :], core.keys, start=True,
                                    stop=True)
                ins.then_inc(sc_ready, 1)

            def branches(t):
                if t >= 2:
                    pe.wait_ge(branch_used, 2 * (t - 1))
                for which, y in ((0, m["hq"]), (1, m["ld"])):
                    for k in range(4):
                        ins = pe.matmul(bank[3 + 2 * (t % 2) + which][:, 0:SEQ - P],
                                        piece[t // 2][:, 4 * which + k, (t % 2) * P:(t % 2 + 1) * P], y[:, k, others],
                                        start=(k == 0), stop=(k == 3))
                    ins.then_inc(branch_ready, 1)

            def output(i):
                if i == 0:
                    pe.wait_ge(merged_ready, KD)
                if i % 3 == 0:
                    pe.wait_ge(w_out_loaded[i // 3], 16)
                if i >= 4:
                    pe.wait_ge(x2_ready, i - 3)
                for k in range(KD):
                    ins = pe.matmul(bank[3 + i % 4][:, 0:STRIP], merged[:, k, (i % 3) * P:(i % 3 + 1) * P], piece[i // 3][:, k, :],
                                    start=(k == 0), stop=(k == KD - 1))
                ins.then_inc(out_ready, 1)

            def turn_input(i):
                pe.wait_ge(h_ready, i // 2 + 1)
                if i < 2:
                    pe.wait_ge(x2_ready, 12)
                else:
                    pe.wait_ge(turned_taken, i - 1)
                for k in range(4):
                    dk = 4 * (i % 2) + k
                    ins = pe.transpose(bank[3 + i % 2][:, k * P:(k + 1) * P], h_tok[:, 1 + i // 2, dk * P:(dk + 1) * P],
                                       core.ident)
                ins.then_inc(turned, 1)

            def queries(h):
                if h == 0:
                    pe.wait_ge(turned_taken, 6)
                if h >= 2:
                    pe.wait_ge(q_taken, h - 1)
                if h % 2 == 0:
                    pe.wait_ge(wq_loaded[h // 2], 16)
                for k in range(KD):
                    ins = pe.matmul(bank[5 + h % 2][:, 0:SEQ - P], piece[h // 2][:, k, (h % 2) * P:(h % 2 + 1) * P],
                                    h_t[:, k, others], start=(k == 0), stop=(k == KD - 1))
                ins.then_inc(q_ready, 1)

            def rest_of_finish(q):
                if q < 2:
                    for t in range(4 * q, 4 * q + 4):
                        branches(t)
                for i in out_parts(q):
                    output(i)
                if q == 5:
                    for i in range(6):
                        turn_input(i)
                for h in query_heads(q):
                    queries(h)

            def end_projection(b):
                pe.wait_ge(end_p_staged, b + 1)
                pe.wait_ge(end_free, b + 1)
                for k in range(2):
                    ins = pe.transpose(bank[4][:, k * P:(k + 1) * P], p_now[:, k * P:(k + 1) * P], core.ident)
                ins.then_inc(end_turned, 1)
                pe.wait_ge(ple_loaded, 64)
                pe.wait_ge(end_turned_taken, 3 * b + 1)
                for half in range(2):
                    for k in range(2):
                        ins = pe.matmul(bank[(7, 4)[half]][:], p_t[:, k, :], ple_proj_sb[:, k, half * 512:(half + 1) * 512],
                                        start=(k == 0), stop=(k == 1))
                    ins.then_inc(end_proj, 1)

            def end_inputs(b):
                pe.wait_ge(end_staged, b + 1)
                for half in range(2):
                    for k in range(4):
                        dk = 4 * half + k
                        ins = pe.transpose(bank[(3, 6)[half]][:, k * P:(k + 1) * P], x_now[:, dk * P:(dk + 1) * P], core.ident)
                    ins.then_inc(end_turned, 1)
                for half in range(2):
                    for k in range(KD):
                        if half == 0 and k % 4 == 0:
                            pe.wait_ge(end_turned_taken, 3 * b + 2 + k // 4)
                        ins = pe.matmul(bank[5 + half][:], x_t[:, k, :], ple_gate_sb[:, k, half * 512:(half + 1) * 512],
                                        start=(k == 0), stop=(k == KD - 1))
                    ins.then_inc(end_gate, 1)

            def turn(n, more, ends=None):
                if more:
                    key_scores(n + 1)
                first_block = isinstance(n, int) and n < per_block
                last_row = tensor_rows(n)[-1]
                for k in range(picks):
                    if first_block and k % TOPK == 0:
                        rest_of_finish(2 * n + k // TOPK)
                    if ends is not None and k == 0:
                        end_projection(ends)
                        end_inputs(ends)
                    if isinstance(n, int) and n == turns - 1 and k == TOPK:
                        end_projection(NB - 1)
                    if k == 0 and not (isinstance(n, int) and n == 0):
                        pe.wait_ge(acc_taken, n)
                    if vector_sums(n, k):
                        continue
                    pe.wait_ge(v_loaded[k % depth], 16 * (uses * n + k // depth + 1))
                    pe.wait_ge(diag_ready, picks * n + diagonal(n, k) + 1)
                    if vector_sums(n, k - 1):
                        pe.wait_ge(v_added, vector_count(k - 1))
                    for half in range(2):
                        ins = pe.matmul(bank[half][:], diag[:, diagonal(n, k) % diags, :], v_ring[:, k % depth, half * 512:(half + 1) * 512],
                                        start=(k == 0), stop=(k == last_row))
                    ins.then_inc(v_used, 2 if vector_sums(n, k - 1) else 1)

            key_scores(0)
            for h in range(2, PK_HEADS):
                if h >= 4:
                    pe.wait_ge(q0_taken, h - 3)
                for k in range(KD):
                    ins = pe.matmul(bank[5 + h % 2][:, 0:P], wq_sb[:, k, h * P:(h + 1) * P], h_t0[:, k, :], start=(k == 0),
                                    stop=(k == KD - 1))
                ins.then_inc(q0_ready, 1)
            pe.wait_ge(q0_taken, PK_HEADS - 2)
            pe.nop().then_inc(v_used, depth)
            for n in range(per_block):
                turn(n, True)

            def block_turns(g, last):
                for i in range(per_block):
                    turn(per_block * g + i, not (last and i == per_block - 1), g - 1 if i == 1 else None)

            with pe.Fori(1, NB - 1) as g:
                block_turns(g, False)
            block_turns(NB - 1, True)
            end_inputs(NB - 1)

        @block.scalar
        def _(act):
            def stage_query(n):
                act.wait_ge(sc_ready, n)
                block_, pair = n // per_block, n % per_block
                act.activation(q_now, q_t[:, bass.ds(2 * pair, 2), bass.ds(block_ * P, P)], ACT.Copy).then_inc(q_staged, 1)

            def head(n, half):
                act.wait_ge(u_used, depth + picks * n + TOPK * (half + 1))
                act.activation(gelu[:, half, :], dots[:, half, :], ACT.Gelu).then_inc(gelu_ready, 1)
                act.wait_ge(coef_ready, 2 * n + half + 1)
                for k in range(TOPK * half, TOPK * (half + 1)):
                    if vector_sums(n, k):
                        continue
                    d = diagonal(n, k)
                    if d >= diags:
                        act.wait_ge(v_used, depth + picks * n + tensor_rows(n)[d - diags] + 1)
                    elif not (isinstance(n, int) and n == 0):
                        act.wait_ge(v_used, depth + picks * (n - 1) + tensor_rows(0)[d - diags] + 1)
                    act.activation(diag[:, d % diags, :], core.ident, ACT.Copy,
                                   scale=coef[:, half, k % TOPK:k % TOPK + 1]).then_inc(diag_ready, 1)

            def softmax_exp(n):
                act.wait_ge(shift_ready, n + 1)
                act.activation(weight, shifted, ACT.Exp).then_inc(exp_ready, 1)

            def root_rest():
                act.wait_ge(ms_ready, 1)
                act.activation(root, mean, ACT.Sqrt).then_inc(rooted, 1)

            def rest_of_finish(q):
                if q == 5:
                    for i in range(6):
                        act.wait_ge(turned, i + 1)
                        b = 1 + i // 2
                        act.activation(h_t[:, 4 * (i % 2):4 * (i % 2) + 4, b * P:(b + 1) * P],
                                       bank[3 + i % 2][:].rearrange("p (k t) -> p k t", t=P), ACT.Copy).then_inc(turned_taken, 1)
                for h in query_heads(q):
                    act.wait_ge(q_ready, h + 1)
                    act.activation(q_t[:, h, others], bank[5 + h % 2][:, 0:SEQ - P], ACT.Copy).then_inc(q_taken, 1)

            stage_query(0)
            for h in range(2, PK_HEADS):
                act.wait_ge(q0_ready, h - 1)
                act.activation(q_t[:, h, 0:P], bank[5 + h % 2][:, 0:P], ACT.Copy).then_inc(q0_taken, 1)
            softmax_exp(0)
            act.wait_ge(q0_taken, PK_HEADS - 2)
            for n in range(per_block):
                if n == per_block - 1:
                    act.wait_ge(q_taken, 2)
                stage_query(n + 1)
                rest_of_finish(2 * n)
                head(n, 0)
                if 2 * n == 4:
                    root_rest()
                softmax_exp(n + 1)
                rest_of_finish(2 * n + 1)
                head(n, 1)
            act.wait_ge(q_taken, PK_HEADS)

            def end_p(b):
                act.wait_ge(ple_loaded, 64)
                act.wait_ge(end_free, b + 1)
                act.sem_inc(carrier_a, 1)
                act.activation(p_now, p_sb[:, bass.ds(b, 1), :], ACT.Copy).then_inc(end_p_staged, 1)
                act.wait_ge(end_turned, 3 * b + 1)
                act.activation(p_t, bank[4][:, 0:2 * P].rearrange("p (k t) -> p k t", t=P), ACT.Copy).then_inc(end_turned_taken, 1)

            def end_inputs(b):
                act.wait_ge(acc_taken, per_block * (b + 1))
                act.wait_ge(end_free, b + 1)
                act.sem_inc(carrier_a, 1)
                x_b = x2[:, bass.ds((b + X2_AT[0]) % NB, 1), :]
                act.activation(x_now, x_b, ACT.Copy).then_inc(end_staged, 1)
                act.activation(y_all[:, bass.ds(b, 1), :], x_b, ACT.Square, accum_out=end_ssq).then_inc(end_squared, 1)
                for half in range(2):
                    act.wait_ge(end_turned, 3 * b + 2 + half)
                    for k in range(4):
                        dk = 4 * half + k
                        ins = act.activation(x_t[:, dk, :], bank[(3, 6)[half]][:, k * P:(k + 1) * P], ACT.Copy,
                                             scale=core.col("norm_ple", dk))
                    ins.then_inc(end_turned_taken, 1)
                act.wait_ge(end_ms, 2 * b + 1)
                act.activation(end_root, end_mean, ACT.Sqrt).then_inc(end_rooted, 1)

            def end_gates(b):
                act.wait_ge(end_rstd_ready, 2 * b + 1)
                for half in range(2):
                    act.wait_ge(end_gate, 2 * b + half + 1)
                    act.activation(x_now[:, half * 512:(half + 1) * 512], bank[5 + half][:], ACT.Sigmoid,
                                   scale=end_rstd).then_inc(end_gated, 1)

            def end_norm(b):
                act.wait_ge(end_x, 2 * b + 2)
                act.wait_ge(end_squared, 2 * b + 1)
                act.sem_inc(carrier_a, 1)
                act.activation(y_all[:, bass.ds(b, 1), :], x2[:, bass.ds((b + X2_AT[0]) % NB, 1), :], ACT.Square,
                               accum_out=ssq_3).then_inc(end_squared, 1)
                act.wait_ge(end_ms, 2 * b + 2)
                act.activation(root_3, mean_3, ACT.Sqrt).then_inc(end_rooted, 1)

            def block_turns(g, last):
                for i in range(per_block):
                    n = per_block * g + i
                    more = not (last and i == per_block - 1)
                    if more:
                        stage_query(n + 1)
                    if i == 1:
                        end_p(g - 1)
                        end_inputs(g - 1)
                    if i == 2:
                        end_norm(g - 1)
                    head(n, 0)
                    if more:
                        softmax_exp(n + 1)
                    if i == 1:
                        end_gates(g - 1)
                    if not more:
                        end_p(NB - 1)
                    head(n, 1)

            with act.Fori(1, NB - 1) as g:
                block_turns(g, False)
            block_turns(NB - 1, True)
            end_inputs(NB - 1)
            end_gates(NB - 1)
            end_norm(NB - 1)

        @block.vector
        def _(v):
            link = Link(v, v_link)
            v.nop().then_inc(u_used, depth)
            v.nop().then_inc(end_free, 1)

            def select(n):
                v.wait_ge(sc_ready, n + 1)
                v.tensor_copy(sc, bank[2][:].rearrange("p (a b) -> p a b", b=N_KEYS)).then_inc(sc_taken, 1)
                v.wait_ge(sc_taken, n + 1)
                v.sem_inc(carrier_v, 1)
                for a in range(4):
                    ins = v.max(top[:, a, 0:8], sc[:, a, :])
                link(ins)
                for a in range(4):
                    v.max_index(top_i[:, a, 0:8], top[:, a, 0:8], sc[:, a, :])
                    ins = v.match_replace(rest[:, a, :], top[:, a, 0:8], sc[:, a, :], LOWEST)
                link(ins)
                for a in range(4):
                    ins = v.max(top[:, a, 8:16], rest[:, a, :])
                link(ins)
                for a in range(4):
                    ins = v.max_index(top_i[:, a, 8:16], top[:, a, 8:16], rest[:, a, :])
                link(ins)
                link(v.tensor_copy(top_f, top_i))
                scores_ = top.rearrange("p (h c) k -> p h c k", c=2)
                index_ = top_f.rearrange("p (h c) k -> p h c k", c=2)
                to = 0
                for i in range(8):
                    w = CAND[i]
                    v.tensor_tensor(cand[:, :, to:to + w], scores_[:, :, 0, i:i + 1].to_broadcast([P, 2, w]),
                                    scores_[:, :, 1, 0:w], ALU.add)
                    v.scalar_tensor_tensor(out=cand_id[:, :, to:to + w], in0=index_[:, :, 0, i:i + 1].to_broadcast([P, 2, w]),
                                           scalar=float(N_KEYS), in1=index_[:, :, 1, 0:w], op0=ALU.mult, op1=ALU.add)
                    to += w
                v.tensor_tensor(cand[:, :, to:], scores_[:, :, 0, 8:16], scores_[:, :, 1, 0:1].to_broadcast([P, 2, 8]), ALU.add)
                link(v.scalar_tensor_tensor(out=cand_id[:, :, to:], in0=index_[:, :, 0, 8:16], scalar=float(N_KEYS),
                                            in1=index_[:, :, 1, 0:1].to_broadcast([P, 2, 8]), op0=ALU.mult, op1=ALU.add))
                for h in range(2):
                    ins = v.max(best[:, h, 0:8], cand[:, h, :])
                link(ins)
                for h in range(2):
                    v.max_index(best_i[:, h, 0:8], best[:, h, 0:8], cand[:, h, :])
                    ins = v.match_replace(cand_rest[:, h, :], best[:, h, 0:8], cand[:, h, :], LOWEST)
                link(ins)
                for h in range(2):
                    ins = v.max(best[:, h, 8:16], cand_rest[:, h, :])
                link(ins)
                for h in range(2):
                    ins = v.max_index(best_i[:, h, 8:16], best[:, h, 8:16], cand_rest[:, h, :])
                link(ins)
                v.tensor_tensor(shifted, best, best[:, :, 0:1].to_broadcast([P, 2, TOPK]), ALU.subtract).then_inc(shift_ready, 1)
                link(v.tensor_copy(best_f, best_i))
                hot = onehot.rearrange("p (k c) -> p k c", c=N_CAND)
                link(v.tensor_tensor(hot, best_f.rearrange("p h k -> p (h k)").unsqueeze(2).to_broadcast([P, picks, N_CAND]),
                                     core.iota_cand.unsqueeze(1).to_broadcast([P, picks, N_CAND]), ALU.is_equal))
                hot4 = onehot.rearrange("p (h k c) -> p h k c", h=2, c=N_CAND)
                link(v.tensor_tensor(hot4, hot4, cand_id.unsqueeze(2).to_broadcast([P, 2, TOPK, N_CAND]), ALU.mult))
                link(v.tensor_reduce(ids_f, hot, AX.X, ALU.add))
                v.tensor_copy(ids[:, bass.ds(n % 2, 1), :], ids_f).then_inc(ids_ready, 1)

            def softmax_rest(n):
                v.wait_ge(exp_ready, n + 1)
                link(v.tensor_reduce(total, weight, AX.X, ALU.add))
                link(v.reciprocal(inverse, total))
                link(v.tensor_tensor(gate_next, weight, inverse.unsqueeze(2).to_broadcast([P, 2, TOPK]), ALU.mult))

            def merge(t):
                for which in range(2):
                    gate = gates[:, KD * which + t, :]
                    v.wait_ge(branch_ready, 2 * t + which + 1)
                    v.tensor_tensor(gate, bank[3 + 2 * (t % 2) + which][:, 0:SEQ - P], gate, ALU.mult).then_inc(branch_used, 1)
                v.wait_ge(branch_used, 2 * t + 2)
                v.tensor_tensor(merged[:, t, :], gates[:, t, :], gates[:, KD + t, :], ALU.add).then_inc(merged_ready, 1)

            def residual(i):
                if i == 0:
                    v.wait_ge(x_loaded, 16)
                v.wait_ge(out_ready, i + 1)
                part = x_others[:, i % 3, (i // 3) * STRIP:(i // 3 + 1) * STRIP]
                v.tensor_tensor(part, part, bank[3 + i % 4][:, 0:STRIP], ALU.add).then_inc(x2_ready, 1)

            def mean_squares():
                v.wait_ge(x2_ready, 12)
                for b in range(3):
                    v.scalar_tensor_tensor(out=junk, in0=x_others[:, b, :], scalar=1.0, in1=x_others[:, b, :], op0=ALU.mult,
                                           op1=ALU.mult, accum_out=mean[:, b:b + 1]).then_inc(squares, 1)
                    v.wait_ge(squares, b + 1)
                v.tensor_scalar(mean, mean, 1.0 / D, EPS, ALU.mult, ALU.add).then_inc(ms_ready, 1)

            def normed():
                v.wait_ge(rooted, 1)
                link(v.reciprocal(rstd, root))
                for b in range(3):
                    v.scalar_tensor_tensor(out=h_tok[:, 1 + b, :], in0=x_others[:, b, :], scalar=rstd[:, b:b + 1], in1=norm_row,
                                           op0=ALU.mult, op1=ALU.mult).then_inc(h_ready, 1)

            def rest_of_finish(q, k):
                if q < 2 and k % 4 == 3:
                    merge(4 * q + k // 4)
                parts = out_parts(q)
                if k % 3 == 2 and k // 3 < len(parts):
                    residual(parts[k // 3])

            def take_sum(n):
                for half in range(2):
                    v.wait_ge(v_used, depth + picks * (n + 1))
                    at = (n // per_block + X2_AT[0]) % NB
                    part = x2[:, bass.ds(at, 1), half * 512:(half + 1) * 512]
                    ins = v.tensor_tensor(part, part, bank[half][:], ALU.add)
                ins.then_inc(acc_taken, 1)
                v.wait_ge(acc_taken, n + 1)
                v.sem_inc(carrier_v, 1)

            def end_mean_square(b, i):
                v.wait_ge(end_squared, 2 * b + i + 1)
                v.tensor_scalar((end_mean, mean_3)[i], (end_ssq, ssq_3)[i], 1.0 / D, EPS, ALU.mult, ALU.add).then_inc(end_ms, 1)

            def end_reciprocal(b, i):
                v.wait_ge(end_rooted, 2 * b + i + 1)
                v.reciprocal((end_rstd, rstd_3)[i], (end_root, root_3)[i]).then_inc(end_rstd_ready, 1)

            def end_x_half(b, half):
                cols = slice(half * 512, (half + 1) * 512)
                v.wait_ge(end_gated, 2 * b + half + 1)
                v.wait_ge(end_proj, 2 * b + half + 1)
                link(v.tensor_tensor(x_now[:, cols], x_now[:, cols], bank[(7, 4)[half]][:], ALU.mult))
                x_b = x2[:, bass.ds((b + X2_AT[0]) % NB, 1), cols]
                v.tensor_tensor(x_b, x_b, x_now[:, cols], ALU.add).then_inc(end_x, 1)

            def end_output(b):
                v.wait_ge(end_rstd_ready, 2 * b + 2)
                v.scalar_tensor_tensor(out=y_all[:, bass.ds(b, 1), :], in0=x2[:, bass.ds((b + X2_AT[0]) % NB, 1), :],
                                       scalar=rstd_3, in1=final_row, op0=ALU.mult, op1=ALU.mult).then_inc(end_y, 1)

            def end_step(b, q, k):
                if (q, k) == (2, 5):
                    end_mean_square(b, 0)
                if (q, k) == (2, 11):
                    end_reciprocal(b, 0)
                if q == 3 and k in (11, 13):
                    end_x_half(b, (k - 11) // 2)
                if (q, k) == (3, 15):
                    v.wait_ge(end_x, 2 * b + 2)
                    v.sem_inc(end_free, 1)
                if (q, k) == (4, 5):
                    end_mean_square(b, 1)
                if (q, k) == (4, 11):
                    end_reciprocal(b, 1)
                if (q, k) == (4, 13):
                    end_output(b)

            def dot_products(n, half, i=None, b=None):
                h = h_tok[:, bass.ds(n // per_block, 1), :]
                for k in range(half * TOPK, (half + 1) * TOPK):
                    v.wait_ge(u_loaded[k % depth], 16 * (uses * n + k // depth + 1))
                    row = u_ring[:, k % depth, :]
                    v.scalar_tensor_tensor(out=row, in0=row, scalar=1.0, in1=h, op0=ALU.mult, op1=ALU.mult,
                                           accum_out=dots[:, half, k % TOPK:k % TOPK + 1]).then_inc(u_used, 1)
                    if isinstance(n, int) and n < per_block:
                        rest_of_finish(2 * n + half, k % TOPK)
                    if k == 9 and not (isinstance(n, int) and n == 0):
                        take_sum(n - 1)
                    if i in (1, 2):
                        end_step(b, 2 * i + half, k % TOPK)

            def coefficients(n, half):
                v.wait_ge(gelu_ready, 2 * n + half + 1)
                v.tensor_tensor(coef[:, half, :], gelu[:, half, :], gate_now[:, half, :], ALU.mult).then_inc(coef_ready, 1)

            def add_rows(n, half):
                rows = [k for k in range(TOPK * half, TOPK * (half + 1)) if vector_sums(n, k)]
                if rows:
                    v.wait_ge(coef_ready, 2 * n + half + 1)
                for k in rows:
                    v.wait_ge(v_loaded[k % depth], 16 * (uses * n + k // depth + 1))
                    x_b = x2[:, X2_AT[NB - 1], :]
                    v.scalar_tensor_tensor(out=x_b, in0=v_ring[:, k % depth, :], scalar=coef[:, half, k % TOPK:k % TOPK + 1],
                                           in1=x_b, op0=ALU.mult, op1=ALU.add).then_inc(v_added, 1)
                    v.wait_ge(v_added, vector_count(k))

            def turn(n, more, i=None, b=None):
                if not (isinstance(n, int) and n == 0):
                    v.wait_ge(coef_ready, 2 * n)
                link(v.tensor_copy(gate_now, gate_next))
                dot_products(n, 0, i, b)
                coefficients(n, 0)
                norms = isinstance(n, int) and n == 2
                if norms:
                    mean_squares()
                if more:
                    select(n + 1)
                if norms:
                    normed()
                dot_products(n, 1, i, b)
                coefficients(n, 1)
                if more:
                    softmax_rest(n + 1)
                add_rows(n, 1)
                link.restart()

            select(0)
            softmax_rest(0)
            link.restart()
            for n in range(per_block):
                turn(n, True)

            def block_turns(g, last):
                for i in range(per_block):
                    turn(per_block * g + i, not (last and i == per_block - 1), i, g - 1)

            with v.Fori(1, NB - 1) as g:
                block_turns(g, False)
            block_turns(NB - 1, True)
            take_sum(turns - 1)
            b = NB - 1
            end_mean_square(b, 0)
            end_reciprocal(b, 0)
            end_x_half(b, 0)
            end_x_half(b, 1)
            end_mean_square(b, 1)
            end_reciprocal(b, 1)
            end_output(b)


def hybrid_block(nc, x, strips, params, w2, a2, g2, w_branch_hg, w_branch_rw, w_out, norm_ffn, wq, keys_t, u_emb, v_emb,
                 ple_gate, ple_proj, p_in, final_norm, out):
    with ExitStack() as ctx:
        core = Core(nc, ctx)
        project(core, x, strips, params, w2, a2, keys_t)
        core.end_phase()
        mix(core, strips)
        finish(core, x, strips, g2, w_branch_hg, w_branch_rw, w_out, norm_ffn, wq)
        experts(core, x, w_out, wq, u_emb, v_emb, ple_gate, ple_proj, p_in, final_norm, out)


def kernel(**inputs):
    import numpy as np
    import concourse.bacc as bacc
    from concourse.bass_utils import run_bass_kernel_spmd

    a = {name: np.asarray(value) for name, value in inputs.items()}
    vectors = [a["norm_mix_w"], a["rw_mu"], a["rw_w0"], a["rw_a0"], a["rw_k_k"], a["rw_k_a"], a["rw_r_k"], a["rw_ln_w"],
               a["rw_ln_b"], a["hg_lb"][0], a["hg_lb"][1], a["hg_norm_w"], a["norm_ple_w"]]
    arrays = {
        "x": a["x"][0],
        "w_in_strips": a["w_in"][0].reshape(KD, P, -1, STRIP).transpose(2, 1, 0, 3),
        "params": np.concatenate([vector.reshape(-1, P).T for vector in vectors], axis=1),
        "w2": a["rw_w2"][0], "a2": a["rw_a2"][0], "g2": a["rw_g2"][0],
        "w_branch_hg": a["w_branch_hg"][0], "w_branch_rw": a["w_branch_rw"][0], "w_out": a["w_out"][0],
        "norm_ffn": a["norm_ffn_w"][0], "wq": a["peer_wq"][0], "keys_t": a["peer_keys"][0].transpose(0, 2, 1),
        "u_emb": a["peer_u"][0], "v_emb": a["peer_v"][0], "ple_gate": a["ple_gate"][0], "ple_proj": a["ple_proj"][0],
        "p_in": a["p"][0, 0], "final_norm": a["final_norm_w"],
    }
    arrays = {name: np.ascontiguousarray(value) for name, value in arrays.items()}
    nc = bacc.Bacc("TRN2", target_bir_lowering=False, num_devices=1)
    args = [nc.dram_tensor(name, value.shape, mybir.dt.from_np(value.dtype), kind="ExternalInput").ap()
            for name, value in arrays.items()]
    out = nc.dram_tensor("out", (SEQ, D), F32, kind="ExternalOutput").ap()
    hybrid_block(nc, *args, out)
    result = run_bass_kernel_spmd(nc, [arrays], core_ids=[0])
    return result.results[0]["out"].reshape(1, SEQ, D)
```
